# Optimizing a Trainium2 kernel written in Bass

```python
import math
import jax
import jax.numpy as jnp
from jax import lax
import numpy as np

D_MODEL = 1024
BATCH = 1
SEQ = 512
DEPTH = 2
DEC_BATCH = 8
DEC_SEQ = 4
PAST_LEN = 256
PAGE_SIZE = 128

PLE_DIM = 256
GLA_HEADS = 4
GLA_DK = 64
GLA_DV = 128
GLA_RANK = 16
GLA_GATE_NORM = 16.0
MLSTM_HEADS = 4
MLSTM_DQK = 64
MLSTM_DV = 128
MLSTM_FGATE_BIAS = 3.0
DIFF_HEADS = 4
DIFF_DQK = 64
DIFF_DV = 2 * DIFF_DQK
ROT_DIM = DIFF_DQK // 4
ROPE_THETA = 500000.0
Q_BLOCK = 128
CHUNK = 64
D_FF = -(-8 * D_MODEL // (3 * 256)) * 256
EPS = 1e-6
N_BRANCH = 3
GLA_VW = GLA_HEADS * GLA_DV
MLSTM_VW = MLSTM_HEADS * MLSTM_DV
DIFF_VW = DIFF_HEADS * DIFF_DV
MIX_V = GLA_VW + MLSTM_VW + DIFF_VW
IN_SPLITS = (GLA_HEADS * GLA_DK, GLA_HEADS * GLA_DK, GLA_VW, GLA_VW, GLA_RANK,
             MLSTM_HEADS * MLSTM_DQK, MLSTM_HEADS * MLSTM_DQK, MLSTM_VW, MLSTM_VW, 2 * MLSTM_HEADS,
             2 * DIFF_HEADS * DIFF_DQK, 2 * DIFF_HEADS * DIFF_DQK, DIFF_VW)
D_IN = sum(IN_SPLITS)

kernel_name = 'hybrid_gla_mlstm_diffattn_decode_step'

def _rmsnorm(x, g):
    x32 = x.astype(jnp.float32)
    y = x32 * lax.rsqrt(jnp.mean(x32 * x32, axis=-1, keepdims=True) + EPS)
    return (y * g.astype(jnp.float32)).astype(x.dtype)

def _chunk_len(L):
    return CHUNK if L % CHUNK == 0 else L

def _to_chunks(t, c):
    B, L, H, d = t.shape
    return t.reshape(B, L // c, c, H, d).transpose(1, 0, 3, 2, 4)

def _gate_chunks(t, c):
    B, L, H = t.shape
    return t.reshape(B, L // c, c, H).transpose(1, 0, 3, 2)

def _from_chunks(o):
    n, B, H, c, d = o.shape
    return o.transpose(1, 0, 3, 2, 4).reshape(B, n * c, H, d)

def _gla_chunked(q, k, v, log_a, s0):
    c = _chunk_len(q.shape[1])
    f32 = jnp.float32
    qc, kc, vc, gc = (_to_chunks(t.astype(f32), c) for t in (q, k, v, log_a))
    mask = jnp.tril(jnp.ones((c, c), dtype=bool))

    def step(S, inp):
        qi, ki, vi, gi = inp
        b = jnp.cumsum(gi, axis=-2)
        qg = qi * jnp.exp(b)
        kg = ki * jnp.exp(-b)
        A = jnp.where(mask, jnp.einsum('bhtd,bhsd->bhts', qg, kg), 0.0)
        o = jnp.einsum('bhtd,bhdv->bhtv', qg, S) + jnp.einsum('bhts,bhsv->bhtv', A, vi)
        b_last = b[..., -1:, :]
        kd = ki * jnp.exp(b_last - b)
        S = jnp.exp(b_last)[..., 0, :, None] * S + jnp.einsum('bhsd,bhsv->bhdv', kd, vi)
        return S, o

    S, o = lax.scan(step, s0.astype(f32), (qc, kc, vc, gc))
    return _from_chunks(o).astype(q.dtype), S

def _mlstm_chunked(q, k, v, i_pre, log_f, c0, n0, m0):
    c = _chunk_len(q.shape[1])
    f32 = jnp.float32
    qc, kc, vc = (_to_chunks(t.astype(f32), c) for t in (q, k, v))
    ic, fc = (_gate_chunks(t.astype(f32), c) for t in (i_pre, log_f))
    mask = jnp.tril(jnp.ones((c, c), dtype=bool))

    def step(carry, inp):
        C, nv, m = carry
        qi, ki, vi, ii, fi = inp
        F = jnp.cumsum(fi, axis=-1)
        logD = jnp.where(mask, F[..., :, None] - F[..., None, :] + ii[..., None, :], -jnp.inf)
        m_inter = m[..., None] + F
        m_row = jnp.maximum(m_inter, jnp.max(logD, axis=-1))
        D = jnp.exp(logD - m_row[..., None])
        w_inter = jnp.exp(m_inter - m_row)
        s = jnp.einsum('bhtd,bhsd->bhts', qi, ki) * D
        num = w_inter[..., None] * jnp.einsum('bhtd,bhdv->bhtv', qi, C) + jnp.einsum('bhts,bhsv->bhtv', s, vi)
        den = w_inter * jnp.einsum('bhtd,bhd->bht', qi, nv) + jnp.sum(s, axis=-1)
        h = num / jnp.maximum(jnp.abs(den), jnp.exp(-m_row))[..., None]
        F_last = F[..., -1]
        log_w = F_last[..., None] - F + ii
        m_new = jnp.maximum(m + F_last, jnp.max(log_w, axis=-1))
        wk = jnp.exp(log_w - m_new[..., None])
        decay = jnp.exp(m + F_last - m_new)
        C = decay[..., None, None] * C + jnp.einsum('bhs,bhsd,bhsv->bhdv', wk, ki, vi)
        nv = decay[..., None] * nv + jnp.einsum('bhs,bhsd->bhd', wk, ki)
        return (C, nv, m_new), h

    (C, nv, m), h = lax.scan(step, (c0.astype(f32), n0.astype(f32), m0.astype(f32)), (qc, kc, vc, ic, fc))
    return _from_chunks(h).astype(q.dtype), C, nv, m

def _rope_partial(x, pos):
    half = ROT_DIM // 2
    inv_freq = ROPE_THETA ** (-jnp.arange(half, dtype=jnp.float32) * 2.0 / ROT_DIM)
    ang = pos.astype(jnp.float32)[:, None] * inv_freq[None, :]
    cos = jnp.cos(ang)[None, :, None, :]
    sin = jnp.sin(ang)[None, :, None, :]
    x32 = x.astype(jnp.float32)
    x1 = x32[..., :half]
    x2 = x32[..., half:ROT_DIM]
    out = jnp.concatenate([x1 * cos - x2 * sin, x1 * sin + x2 * cos, x32[..., ROT_DIM:]], axis=-1)
    return out.astype(x.dtype)

def _diff_attention(q, k, v, q_pos, k_pos, lam):
    B, Lq, H2, d = q.shape
    H = H2 // 2
    Lk = k.shape[1]
    scale = d ** -0.5
    v32 = v.astype(jnp.float32)

    def block(qb, qp):
        s = jnp.einsum('bqhd,bkhd->bhqk', qb, k).astype(jnp.float32) * scale
        s = jnp.where(k_pos[None, :] <= qp[:, None], s, -jnp.inf)
        a = jax.nn.softmax(s, axis=-1).reshape(B, H, 2, qb.shape[1], Lk)
        w = a[:, :, 0] - lam * a[:, :, 1]
        return jnp.einsum('bhqk,bkhv->bqhv', w, v32)

    if Lq > Q_BLOCK and Lq % Q_BLOCK == 0:
        nb = Lq // Q_BLOCK
        qb = q.reshape(B, nb, Q_BLOCK, H2, d).transpose(1, 0, 2, 3, 4)
        qp = q_pos.reshape(nb, Q_BLOCK)
        out = lax.map(lambda a: block(a[0], a[1]), (qb, qp))
        out = out.transpose(1, 0, 2, 3, 4).reshape(B, Lq, H, v.shape[-1])
    else:
        out = block(q, q_pos)
    return out.astype(q.dtype)

def _layer(h, p_l, pos, layer_idx, lw, gla_s0, c0, n0, m0, past_k, past_v, past_pos):
    (g_mix, w_in, w_gla_gk, b_gla_gk, g_gla_norm, b_mlstm_if, g_mlstm_norm, diff_lambda, g_diff_norm,
     w_branch, w_gate, w_out, g_ffn, w_ffn_gate, w_ffn_up, w_ffn_down, g_ple, w_ple_gate, w_ple_proj) = lw
    B, L, D = h.shape
    xn = _rmsnorm(h, g_mix)
    proj = jnp.einsum('bld,de->ble', xn, w_in)
    offsets = np.cumsum(IN_SPLITS)[:-1].tolist()
    (gq, gk, gv, gr, glr, mq, mk, mv, mo, mif, dq, dk, dv) = jnp.split(proj, offsets, axis=-1)

    log_a = jax.nn.log_sigmoid((jnp.einsum('blr,re->ble', glr, w_gla_gk) + b_gla_gk).astype(jnp.float32)) / GLA_GATE_NORM
    o_a, gla_s = _gla_chunked(gq.reshape(B, L, GLA_HEADS, GLA_DK) * GLA_DK ** -0.5,
                              gk.reshape(B, L, GLA_HEADS, GLA_DK),
                              gv.reshape(B, L, GLA_HEADS, GLA_DV),
                              log_a.reshape(B, L, GLA_HEADS, GLA_DK), gla_s0)
    o_a = (_rmsnorm(o_a.astype(h.dtype), g_gla_norm) * jax.nn.silu(gr.reshape(B, L, GLA_HEADS, GLA_DV))).reshape(B, L, GLA_VW)

    g_if = mif.astype(jnp.float32) + b_mlstm_if.astype(jnp.float32)
    h_m, c_new, n_new, m_new = _mlstm_chunked(mq.reshape(B, L, MLSTM_HEADS, MLSTM_DQK),
                                              mk.reshape(B, L, MLSTM_HEADS, MLSTM_DQK) * MLSTM_DQK ** -0.5,
                                              mv.reshape(B, L, MLSTM_HEADS, MLSTM_DV),
                                              g_if[..., :MLSTM_HEADS], jax.nn.log_sigmoid(g_if[..., MLSTM_HEADS:]),
                                              c0, n0, m0)
    o_m = (jax.nn.sigmoid(mo.reshape(B, L, MLSTM_HEADS, MLSTM_DV)) * _rmsnorm(h_m.astype(h.dtype), g_mlstm_norm)).reshape(B, L, MLSTM_VW)

    q_d = _rope_partial(dq.reshape(B, L, 2 * DIFF_HEADS, DIFF_DQK), pos)
    k_d = _rope_partial(dk.reshape(B, L, 2 * DIFF_HEADS, DIFF_DQK), pos)
    v_d = dv.reshape(B, L, DIFF_HEADS, DIFF_DV)
    if past_k is None:
        k_all, v_all, k_pos = k_d, v_d, pos
    else:
        k_all = jnp.concatenate([past_k.astype(k_d.dtype), k_d], axis=1)
        v_all = jnp.concatenate([past_v.astype(v_d.dtype), v_d], axis=1)
        k_pos = jnp.concatenate([past_pos, pos], axis=0)
    lam32 = diff_lambda.astype(jnp.float32)
    lam_init = 0.8 - 0.6 * math.exp(-0.3 * layer_idx)
    lam = jnp.exp(jnp.sum(lam32[0] * lam32[1])) - jnp.exp(jnp.sum(lam32[2] * lam32[3])) + lam_init
    attn = _diff_attention(q_d, k_all, v_all, pos, k_pos, lam)
    o_d = (_rmsnorm(attn, g_diff_norm) * (1.0 - lam_init)).reshape(B, L, DIFF_VW)

    w_a = w_branch[:GLA_VW]
    w_m = w_branch[GLA_VW:GLA_VW + MLSTM_VW]
    w_d = w_branch[GLA_VW + MLSTM_VW:]
    gates = jax.nn.sigmoid(jnp.einsum('bld,de->ble', xn, w_gate).astype(jnp.float32)).astype(h.dtype).reshape(B, L, N_BRANCH, D)
    merged = (gates[:, :, 0] * jnp.einsum('blv,vd->bld', o_a, w_a)
              + gates[:, :, 1] * jnp.einsum('blv,vd->bld', o_m, w_m)
              + gates[:, :, 2] * jnp.einsum('blv,vd->bld', o_d, w_d))
    h = h + jnp.einsum('bld,de->ble', merged, w_out)

    xf = _rmsnorm(h, g_ffn)
    hid = jax.nn.silu(jnp.einsum('bld,df->blf', xf, w_ffn_gate)) * jnp.einsum('bld,df->blf', xf, w_ffn_up)
    h = h + jnp.einsum('blf,fd->bld', hid, w_ffn_down)

    ple_gate = jax.nn.sigmoid(jnp.einsum('bld,de->ble', _rmsnorm(h, g_ple), w_ple_gate))
    h = h + ple_gate * jnp.einsum('blp,pd->bld', p_l, w_ple_proj)
    return h, (k_d, v_d, gla_s, c_new, n_new, m_new)

def setup_inputs(seed: int = 0) -> dict:
    key = jax.random.key(seed)
    ks = iter(jax.random.split(key, 40))
    f32 = jnp.float32

    def nrm(shape, scale):
        return jax.random.normal(next(ks), shape, f32) * scale

    n_pages = PAST_LEN // PAGE_SIZE
    n_used = DEC_BATCH * n_pages
    n_pool = (n_used * 5 + 3) // 4
    page_table = jax.random.permutation(next(ks), n_pool)[:n_used].reshape(DEC_BATCH, n_pages).astype(jnp.int32)
    return {
        'x_prompt': nrm((BATCH, SEQ, D_MODEL), 1.0),
        'x_sample': nrm((DEC_BATCH, DEC_SEQ, D_MODEL), 1.0),
        'cache_k': nrm((DEPTH, n_pool, PAGE_SIZE, 2 * DIFF_HEADS, DIFF_DQK), 1.0),
        'cache_v': nrm((DEPTH, n_pool, PAGE_SIZE, DIFF_HEADS, DIFF_DV), 1.0),
        'state_gla': nrm((DEPTH, DEC_BATCH, GLA_HEADS, GLA_DK, GLA_DV), 1.0),
        'state_mlstm_c': nrm((DEPTH, DEC_BATCH, MLSTM_HEADS, MLSTM_DQK, MLSTM_DV), 1.0),
        'state_mlstm_n': nrm((DEPTH, DEC_BATCH, MLSTM_HEADS, MLSTM_DQK), 1.0),
        'state_mlstm_m': nrm((DEPTH, DEC_BATCH, MLSTM_HEADS), 1.0),
        'page_table': page_table,
        'p_prompt': nrm((DEPTH, BATCH, SEQ, PLE_DIM), 1.0),
        'p_sample': nrm((DEPTH, DEC_BATCH, DEC_SEQ, PLE_DIM), 1.0),
        'g_mix': 1.0 + nrm((DEPTH, D_MODEL), 0.05),
        'w_in': nrm((DEPTH, D_MODEL, D_IN), D_MODEL ** -0.5),
        'w_gla_gk': nrm((DEPTH, GLA_RANK, GLA_HEADS * GLA_DK), GLA_RANK ** -0.5),
        'b_gla_gk': nrm((DEPTH, GLA_HEADS * GLA_DK), 0.1),
        'g_gla_norm': 1.0 + nrm((DEPTH, GLA_DV), 0.05),
        'b_mlstm_if': jnp.concatenate([nrm((DEPTH, MLSTM_HEADS), 0.1),
                                       MLSTM_FGATE_BIAS + nrm((DEPTH, MLSTM_HEADS), 0.1)], axis=-1),
        'g_mlstm_norm': 1.0 + nrm((DEPTH, MLSTM_DV), 0.05),
        'diff_lambda': nrm((DEPTH, 4, DIFF_DQK), 0.1),
        'g_diff_norm': 1.0 + nrm((DEPTH, DIFF_DV), 0.05),
        'w_branch': nrm((DEPTH, MIX_V, D_MODEL), GLA_VW ** -0.5),
        'w_gate': nrm((DEPTH, D_MODEL, N_BRANCH * D_MODEL), D_MODEL ** -0.5),
        'w_out': nrm((DEPTH, D_MODEL, D_MODEL), D_MODEL ** -0.5),
        'g_ffn': 1.0 + nrm((DEPTH, D_MODEL), 0.05),
        'w_ffn_gate': nrm((DEPTH, D_MODEL, D_FF), D_MODEL ** -0.5),
        'w_ffn_up': nrm((DEPTH, D_MODEL, D_FF), D_MODEL ** -0.5),
        'w_ffn_down': nrm((DEPTH, D_FF, D_MODEL), D_FF ** -0.5),
        'g_ple': 1.0 + nrm((DEPTH, D_MODEL), 0.05),
        'w_ple_gate': nrm((DEPTH, D_MODEL, D_MODEL), D_MODEL ** -0.5),
        'w_ple_proj': nrm((DEPTH, PLE_DIM, D_MODEL), PLE_DIM ** -0.5),
        'g_final': 1.0 + nrm((D_MODEL,), 0.05),
    }

def reference(x_prompt, x_sample, cache_k, cache_v, state_gla, state_mlstm_c, state_mlstm_n, state_mlstm_m,
              page_table, p_prompt, p_sample, g_mix, w_in, w_gla_gk, b_gla_gk, g_gla_norm, b_mlstm_if,
              g_mlstm_norm, diff_lambda, g_diff_norm, w_branch, w_gate, w_out, g_ffn, w_ffn_gate, w_ffn_up,
              w_ffn_down, g_ple, w_ple_gate, w_ple_proj, g_final):
    f32 = jnp.float32
    bp, lp, _ = x_prompt.shape
    bs, ls, _ = x_sample.shape
    n_pages = page_table.shape[1]
    past_len = n_pages * cache_k.shape[2]
    pos_p = jnp.arange(lp, dtype=jnp.int32)
    pos_s = past_len + jnp.arange(ls, dtype=jnp.int32)
    past_pos = jnp.arange(past_len, dtype=jnp.int32)
    gla0 = jnp.zeros((bp, GLA_HEADS, GLA_DK, GLA_DV), f32)
    c0 = jnp.zeros((bp, MLSTM_HEADS, MLSTM_DQK, MLSTM_DV), f32)
    n0 = jnp.zeros((bp, MLSTM_HEADS, MLSTM_DQK), f32)
    m0 = jnp.zeros((bp, MLSTM_HEADS), f32)
    hp, hs = x_prompt, x_sample
    new_p, new_s = [], []
    for l in range(DEPTH):
        lw = (g_mix[l], w_in[l], w_gla_gk[l], b_gla_gk[l], g_gla_norm[l], b_mlstm_if[l], g_mlstm_norm[l],
              diff_lambda[l], g_diff_norm[l], w_branch[l], w_gate[l], w_out[l], g_ffn[l], w_ffn_gate[l],
              w_ffn_up[l], w_ffn_down[l], g_ple[l], w_ple_gate[l], w_ple_proj[l])
        hp, st_p = _layer(hp, p_prompt[l], pos_p, l, lw, gla0, c0, n0, m0, None, None, None)
        new_p.append(st_p)
        past_k = cache_k[l][page_table].reshape(bs, past_len, 2 * DIFF_HEADS, DIFF_DQK)
        past_v = cache_v[l][page_table].reshape(bs, past_len, DIFF_HEADS, DIFF_DV)
        hs, st_s = _layer(hs, p_sample[l], pos_s, l, lw, state_gla[l], state_mlstm_c[l], state_mlstm_n[l],
                          state_mlstm_m[l], past_k, past_v, past_pos)
        new_s.append(st_s)
    y_prompt = _rmsnorm(hp, g_final)
    y_sample = _rmsnorm(hs, g_final)
    k_prompt, v_prompt, gla_prompt, c_prompt, n_prompt, m_prompt = [jnp.stack(t) for t in zip(*new_p)]
    k_sample, v_sample, gla_sample, c_sample, n_sample, m_sample = [jnp.stack(t) for t in zip(*new_s)]
    return (y_prompt, y_sample, k_prompt, v_prompt, gla_prompt, c_prompt, n_prompt, m_prompt,
            k_sample, v_sample, gla_sample, c_sample, n_sample, m_sample)


_drawn_inputs = setup_inputs


def setup_inputs(seed=0):
    import zlib

    import numpy as np

    out = dict(_drawn_inputs(seed))
    spreads = {}
    factors = {'g_gla_norm': 2.995,
     'g_mlstm_norm': 3.126,
     'g_ple': 13.184,
     'diff_lambda': 2.873,
     'g_diff_norm': 2.737}
    for name, (base, spread) in spreads.items():
        noise = np.random.default_rng([zlib.crc32(name.encode()), seed]).standard_normal(out[name].shape)
        drawn = base * np.exp(spread * noise) if base else spread * noise
        out[name] = jnp.asarray(drawn.astype(out[name].dtype))
    for name, factor in factors.items():
        out[name] = (out[name] * factor).astype(out[name].dtype)
    return out
```

```python
from contextlib import ExitStack

import concourse.bass as bass
from concourse import mybir

F32 = mybir.dt.float32
F32R = mybir.dt.float32r
I32 = mybir.dt.int32
ALU = mybir.AluOpType
ACT = mybir.ActivationFunctionType
AX = mybir.AxisListType

P = 128
D = 1024
KD = D // P
SEQ, DEC_BATCH, DEC_SEQ = 512, 8, 4
NS = DEC_BATCH * DEC_SEQ
T = SEQ + NS
HALF = T // 2
PT = SEQ // P
TILES = [P] * PT + [NS]
DEPTH = 2
PAGE, PAGES = 128, 2
HEADS, DK, DV = 4, 64, 128
CH = 64
NCH = SEQ // CH
DFF = 2816
KF = DFF // P
PLE = 256
KP = PLE // P
RANK = 16
EPS = 1e-6
BIG = 1e30
COL_GLA, COL_LR, COL_ML, COL_IF, COL_DF = 0, 1536, 1552, 3088, 3096
RAW, SPLIT = 4, 2
KMAX = 8
DOWN_K = [(0, 6), (6, 6), (12, 5), (17, 5)]


class Steps:

    def __init__(self, eng, sem):
        self.eng, self.sem, self.n = eng, sem, 0

    def __call__(self, ins):
        ins.then_inc(self.sem, 1)
        self.n = self.n + 1
        self.eng.wait_ge(self.sem, self.n)


def halves(ap):
    return ap.rearrange("p (h n) -> p h n", h=2)


def program(nc, a, c, o):
    ctx = ExitStack()
    with ctx:
        ctx.enter_context(nc.allow_non_contiguous_dma(reason="gains and states' columns, a few kilobytes"))
        arena_size = (nc.sbuf_usable_end - nc.sbuf_base - 64) // 64 * 64
        arena = ctx.enter_context(nc.sbuf_tensor("arena", [P, arena_size // 4], F32, align_bytes=64))
        start = nc.sbuf_base - arena_size
        assert start >= 0

        class Area:

            def __init__(self, at, size):
                self.at, self.size, self.used = at, size, 0

            def put(self, name, shape, dt=F32):
                n = 4
                for s in shape[1:]:
                    n *= s
                n = (n + 31) // 32 * 32
                assert self.used + n <= self.size, (name, self.used + n, self.size)
                t = nc.alloc_sbuf_tensor_at(name, shape, dt, offset=self.at + self.used)
                self.used += n
                return t

            def again(self, skip=0):
                return Area(self.at + skip, self.size - skip)

        whole = Area(start, arena_size)

        def area(size):
            r = Area(whole.at + whole.used, size)
            whole.used += size
            assert whole.used <= whole.size, (whole.used, whole.size)
            return r

        BLK = T * 4
        fixed = area(10368)
        ident = fixed.put("ident", [P, P])
        ones = fixed.put("ones", [P, P])
        rot = fixed.put("rot", [P, P])
        big = fixed.put("big", [P, P])
        neg = fixed.put("neg", [P, P])
        gmask = fixed.put("gmask", [P, P])
        smask = fixed.put("smask", [NS, NS])
        sbig = fixed.put("sbig", [NS, NS])
        sneg = fixed.put("sneg", [P, 2, NS])
        sel = fixed.put("sel", [HEADS, HEADS, P])
        selp = fixed.put("selp", [HEADS, 2, P])
        seqm = fixed.put("seqm", [NS, DEC_BATCH])
        sign = fixed.put("sign", [P, 2])
        epsc = fixed.put("epsc", [P, 1])
        gains = fixed.put("gains", [P, 3, KD])
        gfin = fixed.put("gfin", [P, KD])
        ghead = fixed.put("ghead", [P, 3])
        bgk = fixed.put("bgk", [P, 2])
        bif = fixed.put("bif", [P, 1])
        wgk = fixed.put("wgk", [RANK, HEADS * DK])
        lamv = fixed.put("lamv", [P, 4, DK])
        lamp = fixed.put("lamp", [P, DK])
        lam = fixed.put("lam", [P, 8])
        lamc = fixed.put("lamc", [P, 2])
        m_in = fixed.put("m_in", [HEADS, DEC_BATCH])
        g_dec = fixed.put("g_dec", [P, 2, NCH + DEC_BATCH])
        pages = fixed.put("pages", [1, DEC_BATCH * PAGES], I32)

        rB = area(BLK).put("rB", [P, T])
        h = area(KD * BLK).put("h", [P, KD, T])
        xs = area(2 * KD * BLK)
        xH, xL = xs.put("xH", [P, KD, T], F32R), xs.put("xL", [P, KD, T], F32R)
        ws = area((RAW + 2 * SPLIT) * KMAX * P * 4)
        raw = [ws.put(f"raw{i}", [P, KMAX, P]) for i in range(RAW)]
        wH = [ws.put(f"wH{i}", [P, KMAX, P], F32R) for i in range(SPLIT)]
        wL = [ws.put(f"wL{i}", [P, KMAX, P], F32R) for i in range(SPLIT)]
        a_oA, a_oM, a_A, a_B, a_MG = (area(8 * BLK) for _ in range(5))
        a_VA = area(5 * 4 * DV * 4)
        a_VM = area(10336)
        a_T = area(whole.size - whole.used)
        hid_area = Area(a_oA.at, 5 * 8 * BLK + a_VA.size)
        tail = Area(a_VM.at, a_VM.size + a_T.size)

        oH, oL, oraw, rO = [], [], [], []
        for n, ar in zip(("g", "m", "d"), (a_oA, a_oM, a_B)):
            oH.append(ar.again().put(f"oH_{n}", [P, HEADS, T], F32R))
            oL.append(ar.again(4 * BLK).put(f"oL_{n}", [P, HEADS, T], F32R))
            rO.append(ar.again().put(f"rO_{n}", [P, HEADS, T]))
            oraw.append(ar.again(4 * BLK).put(f"oraw_{n}", [P, HEADS, T]))
        A = a_A.again().put("A", [P, 8, T])
        B = a_B.again().put("B", [P, 8, T])
        MG = a_MG.again().put("MG", [P, 8, T])
        gv = a_VA.again().put("gv", [P, 5, HEADS, DV])
        dv = a_VA.again().put("dv", [P, 5, HEADS, DV])
        mv = a_VM.again().put("mv", [P, 5, HEADS, DV + 1])
        small = a_T.put("small", [P, T])
        tmp_at = a_T.used
        sq0 = a_T.again(tmp_at).put("sq0", [P, 2, T])

        t = a_oM.again()
        g_b, g_E, g_kg = (t.put(n, [P, 2, T]) for n in ("g_b", "g_E", "g_kg"))
        g_az, g_reset = t.put("g_az", [P, T]), t.put("g_reset", [P, T])
        t = a_B.again()
        g_S, g_Sin = t.put("g_S", [P, NCH, 2, DV]), t.put("g_Sin", [P, DEC_BATCH, 2, DV])
        t = a_VM.again()
        g_kdT, g_A = t.put("g_kdT", [P, 5, HEADS * DK]), t.put("g_A", [P, 2, HEADS, P])
        g_As = t.put("g_As", [NS, HEADS, NS])
        g_qz = a_MG.again().put("g_qz", [P, HEADS, T])
        g_kdm = a_MG.again(4 * BLK).put("g_kdm", [NS, DEC_BATCH, HEADS * DK])
        t = a_A.again()
        r_a, r_m, r_en, r_F, r_d, r_g, r_wi, r_reset = (
            t.put(n, [HEADS, T]) for n in ("r_a", "r_m", "r_en", "r_F", "r_d", "r_g", "r_wi", "r_reset"))
        t = a_MG.again(4 * BLK)
        m_qwz = t.put("m_qwz", [P, HEADS, T])
        m_qz = a_oM.again().put("m_qz", [P, HEADS, T])
        t = a_B.again()
        m_qnz, m_qns = t.put("m_qnz", [P, HEADS, P]), t.put("m_qns", [P, HEADS, NS])
        m_Cin = a_MG.again().put("m_Cin", [P, DEC_BATCH, 2, DV + 1])
        t = a_VA.again()
        m_kT, m_kw = t.put("m_kT", [P, 5, HEADS, DK]), t.put("m_kw", [P, 5, HEADS, DK])
        m_kwm = a_oM.again().put("m_kwm", [NS, DEC_BATCH, HEADS * DK])
        t = a_T.again(tmp_at)
        m_D, m_C = t.put("m_D", [P, HEADS * P]), t.put("m_C", [P, 2, 2, DV + 1])
        t = a_MG.again(DEC_BATCH * 2 * (DV + 1) * 4)
        m_dec, m_cols = t.put("m_dec", [P, 2, 12]), t.put("m_cols", [P, 5, 8])
        m_prev = t.put("m_prev", [HEADS, 12])
        m_SD = a_A.again(3 * BLK).put("m_SD", [P, HEADS * P])
        m_ad = a_A.again(7 * BLK).put("m_ad", [P, HEADS * P])
        t = a_VM.again()
        d_e, d_w, d_wT = t.put("d_e", [P, 2, SEQ]), t.put("d_w", [P, SEQ]), t.put("d_wT", [P, SEQ])
        d_kout = t.put("d_kout", [P, 8 * DK])
        t = a_T.again()
        d_cos, d_sin = t.put("d_cos", [P, T]), t.put("d_sin", [P, T])
        d_t1 = t.put("d_t1", [P, T])
        t = a_T.again()
        d_qbd = t.put("d_qbd", [P, DEC_BATCH, HEADS, 2, DEC_SEQ * HEADS])
        d_es = t.put("d_es", [P, 2 * PAGE + NS])
        d_wTs, d_wTn = t.put("d_wTs", [P, PAGES, 4, HEADS, DEC_SEQ]), t.put("d_wTn", [NS, 4, HEADS, DEC_SEQ])
        d_nm, d_l, d_rc = t.put("d_nm", [P, 2]), t.put("d_l", [P, 2]), t.put("d_rc", [P, 2])
        d_V = a_MG.again().put("d_V", [P, 4, HEADS * DV])
        t = a_MG.again(4 * BLK)
        d_kr = t.put("d_kr", [P, 2, HEADS, P])
        d_KT = t.put("d_KT", [P, HEADS, PAGES * PAGE])
        t = a_T.again()
        u_g, u_p = t.put("u_g", [P, 2, T]), t.put("u_p", [P, T])
        mH = a_oA.again().put("mH", [P, KD, T], F32R)
        mL = a_oM.again().put("mL", [P, KD, T], F32R)
        sq1 = a_T.again().put("sq1", [P, 2, T])
        p_tok = a_A.again().put("p_tok", [P, 5, PLE])
        t = tail.again()
        pH, pL = t.put("pH", [P, KP, T], F32R), t.put("pL", [P, KP, T], F32R)
        p_raw = a_A.again(5120).put("p_raw", [P, KP, T])
        f_g, f_u = t.put("f_g", [P, 2, T]), t.put("f_u", [P, 2, T])
        t2 = hid_area.again()
        hidH, hidL = t2.put("hidH", [P, KF, T], F32R), t2.put("hidL", [P, KF, T], F32R)
        t = tail.again(4 * BLK)
        sq2 = t.put("sq2", [P, 2, T])
        e_g, e_p = t.put("e_g", [P, T]), t.put("e_p", [P, T])
        io_tok = hid_area.again().put("io_tok", [P, 5, D])
        y_f = hid_area.again(5 * D * 4).put("y_f", [P, KD, T])

        G = ctx.enter_context(nc.psum_tensor("G", [P, 2, 2, 512], F32))
        M = ctx.enter_context(nc.psum_tensor("M", [P, 4, 512], F32))

        def out2(slot):
            return G[:, slot, :, 0:HALF]

        M01 = M[:, 0:2, 0:HALF]
        M23 = M[:, 2:4, 0:HALF]

        class Semaphores:
            pass

        s, sems = Semaphores(), []

        def signals(names):
            new = [ctx.enter_context(nc.semaphore(n)) for n in names.split()]
            sems.extend(new)
            return new

        s.const_in, s.io_in, s.io_turned, s.io_copied, s.io_out = signals(
            "const_in io_in io_turned io_copied io_out")
        s.par_in, s.greset_in, s.rreset_in, s.trig_in, s.gst_in, s.mst_in = signals(
            "par_in greset_in rreset_in trig_in gst_in mst_in")
        s.mn_in, s.ptok_in = signals(
            "mn_in ptok_in")
        s.w_in0, s.w_in1, s.w_in2, s.w_in3, s.wh_split, s.wl_split = signals(
            "w_in0 w_in1 w_in2 w_in3 wh_split wl_split")
        s.chunk_done, s.out_taken = signals(
            "chunk_done out_taken")
        s.xh_ready, s.xl_ready, s.sq_ready, s.sq_used, s.stat_ps, s.r_ready = signals(
            "xh_ready xl_ready sq_ready sq_used stat_ps r_ready")
        s.h_mix, s.h_ffn, s.h_ple = signals(
            "h_mix h_ffn h_ple")
        s.tok_ps, s.tok_copied, s.vstore, s.kstore = signals(
            "tok_ps tok_copied vstore kstore")
        s.gz_ps, s.gz_abs, s.gz_ln, s.gz_min, s.g_b_ready, s.g_e = signals(
            "gz_ps gz_abs gz_ln gz_min g_b_ready g_e")
        s.g_qg, s.g_kg, s.g_kd, s.g_at_ps, s.g_at, s.g_ds_ps = signals(
            "g_qg g_kg g_kd g_at_ps g_at g_ds_ps")
        s.g_s, s.g_o_ps, s.g_o, s.g_kdm_ready = signals(
            "g_s g_o_ps g_o g_kdm_ready")
        s.gstore, s.mstore, s.nstore = signals(
            "gstore mstore nstore")
        s.bn_sq, s.bn_ps, s.bn_ln, s.bn_r, s.bn_gate, s.bn_o = signals(
            "bn_sq bn_ps bn_ln bn_r bn_gate bn_o")
        s.bn_h, s.bn_l = signals(
            "bn_h bn_l")
        s.ml_ab, s.ml_ln, s.ml_f, s.ml_rows, s.ml_ex, s.ml_col_ps = signals(
            "ml_ab ml_ln ml_f ml_rows ml_ex ml_col_ps")
        s.ml_col, s.ml_wi_ps, s.ml_wi, s.ml_kw, s.ml_d_ps, s.ml_d = signals(
            "ml_col ml_wi_ps ml_wi ml_kw ml_d_ps ml_d")
        s.ml_s_ps, s.ml_sd, s.ml_e_ps = signals(
            "ml_s_ps ml_sd ml_e_ps")
        s.ml_n_ps, s.ml_den_ps, s.ml_ad, s.ml_o, s.ml_c_ps, s.ml_c = signals(
            "ml_n_ps ml_den_ps ml_ad ml_o ml_c_ps ml_c")
        s.ml_qn, s.ml_kwm_ready = signals(
            "ml_qn ml_kwm_ready")
        s.rope_ps, s.rope_done, s.lam_sum, s.lam_exp, s.lam_ready = signals(
            "rope_ps rope_done lam_sum lam_exp lam_ready")
        s.sc_ps, s.nm_ready, s.e_ready, s.w_ready, s.wt_ps, s.wt_copied = signals(
            "sc_ps nm_ready e_ready w_ready wt_ps wt_copied")
        s.pv_ps, s.pv_copied = signals(
            "pv_ps pv_copied")
        s.page0, s.page1, s.vpage0, s.vpage1, s.vpage2, s.vpage3 = signals(
            "page0 page1 vpage0 vpage1 vpage2 vpage3")
        s.v_used, s.kt_copied, s.qbd_ready, s.ss_ps, s.ss_nm, s.ss_e = signals(
            "v_used kt_copied qbd_ready ss_ps ss_nm ss_e")
        s.ss_w, s.st_ps, s.st_red, s.sp_ps, s.sp_copied = signals(
            "ss_w st_ps st_red sp_ps sp_copied")
        s.u_lin, s.u_sig, s.u_mul, s.mg_ready, s.mh_ready, s.ml_split = signals(
            "u_lin u_sig u_mul mg_ready mh_ready ml_split")
        s.p_ps, s.p_copied, s.ph_ready, s.pl_ready = signals(
            "p_ps p_copied ph_ready pl_ready")
        s.f_lin, s.f_silu, s.f_hid, s.fh_ready, s.fl_ready, s.e_lin = signals(
            "f_lin f_silu f_hid fh_ready fl_ready e_lin")
        [s.e_sig] = signals("e_sig")
        s.act_step, s.dve_step, s.y_ps, s.y_ready = signals(
            "act_step dve_step y_ps y_ready")
        s.w_in = [s.w_in0, s.w_in1, s.w_in2, s.w_in3]
        s.page = [s.page0, s.page1]
        s.vpage = [s.vpage0, s.vpage1, s.vpage2, s.vpage3]

        def clear_all():
            nc.all_engine_barrier()
            numbers = [x.num for x in sems]
            assert max(numbers) - min(numbers) + 1 == len(numbers)
            nc.sync.sem_clear(range(min(numbers), max(numbers) + 1))
            nc.all_engine_barrier()

        with nc.Block() as block:

            @block.sync
            def _(sp):
                for dst, src in ((ident, "ident"), (ones, "ones"), (rot, "rot"), (big, "big"), (neg, "neg"),
                                 (gmask, "gmask"), (smask, "smask"), (sbig, "sbig"), (sneg, "sneg"), (sel, "sel"),
                                 (selp, "selp"), (seqm, "seqm"), (sign, "sign"), (epsc, "epsc")):
                    sp.dma_start(dst[:], c[src]).then_inc(s.const_in, 16)
                sp.dma_start(gfin[:, :], a["g_final"].rearrange("(k p) -> p k", p=P)).then_inc(s.const_in, 16)
                sp.dma_start(pages[:, :], a["page_table"].rearrange("(o b) n -> o (b n)", o=1)).then_inc(s.const_in, 16)
                sp.dma_start(io_tok[:, 0:PT, :],
                             a["x_prompt"].rearrange("a (i p) d -> p (a i) d", p=P)).then_inc(s.io_in, 16)
                sp.dma_start(io_tok[0:NS, PT, :], a["x_sample"].rearrange("b t d -> (b t) d")).then_inc(s.io_in, 16)

            @block.tensor
            def _(pe):
                pe.wait_ge(s.const_in, 16 * 16)
                pe.wait_ge(s.io_in, 32)
                for k in range(KD):
                    if k >= 2:
                        pe.wait_ge(s.io_copied, 2 * (k - 1))
                    for i, n in enumerate(TILES):
                        bank, col = (2 * (k % 2) + i // PT, (i % PT) * P)
                        pe.transpose(M[:, bank, col:col + n], io_tok[0:n, i, k * P:(k + 1) * P],
                                     ident[0:n, 0:n]).then_inc(s.io_turned, 1)

            @block.vector
            def _(dve):
                for k in range(KD):
                    dve.wait_ge(s.io_turned, 5 * (k + 1))
                    dve.tensor_copy(h[:, k, 0:SEQ], M[:, 2 * (k % 2), :]).then_inc(s.io_copied, 1)
                    dve.tensor_copy(h[:, k, SEQ:T], M[:, 2 * (k % 2) + 1, 0:NS]).then_inc(s.io_copied, 1)

        clear_all()

        CHUNK, OUT, cc, oo = {}, {}, 0, 0
        for name, chunks, outs in (("gla", 12, 12), ("small", 1, 1), ("ml", 12, 12), ("df", 12, 12),
                                   ("merge0", 16, 16), ("merge1", 16, 16), ("merge2", 16, 16), ("out", 8, 8),
                                   ("ffn", 2 * KF, 2 * KF), ("down", 4 * KD, KD), ("ple", 16, 16)):
            CHUNK[name], OUT[name] = cc, oo
            cc, oo = cc + chunks, oo + outs
        TOK = {"gv": 0, "kd": 5, "mv": 10, "mk": 15, "dv": 20, "dk": 25, "page": 30}

        def load(sp, chunk, slot, src, kb, turn):
            if not isinstance(chunk, int) or chunk >= RAW:
                sp.wait_ge(s.wl_split, chunk - (RAW - 1))
            sp.dma_start(raw[slot][:, 0:kb, :], src).then_inc(s.w_in[slot], 16)

        def split_high(act, chunk, slot, half, kb, extra=0):
            act.wait_ge(s.w_in[slot], used(slot, chunk))
            if not isinstance(chunk, int) or chunk >= SPLIT:
                act.wait_ge(s.chunk_done, chunk - (SPLIT - 1))
            act.activation(wH[half][:, 0:kb, :], raw[slot][:, 0:kb, :], ACT.Copy).then_inc(s.wh_split, 1)

        def split_low(pool, chunk, slot, half, kb):
            pool.wait_ge(s.wh_split, chunk + 1)
            pool.tensor_tensor(wL[half][:, 0:kb, :], raw[slot][:, 0:kb, :], wH[half][:, 0:kb, :].bitcast(F32),
                               ALU.subtract).then_inc(s.wl_split, 1)

        def used(slot, chunk):
            more = 48 if slot == CHUNK["small"] % RAW and (not isinstance(chunk, int) or chunk >= CHUNK["small"]) else 0
            if isinstance(chunk, int):
                return 16 * (chunk // RAW + 1) + more
            return None

        def chunks_loop(eng, name, count, body, per=4):
            base = CHUNK[name]
            assert count % per == 0
            with eng.Fori(0, count // per) as i:
                for j in range(per):
                    body(i, j, base + j)

        def w_count(slot_chunk, i, per):
            slot = slot_chunk % RAW
            more = 48 if slot == CHUNK["small"] % RAW and slot_chunk >= CHUNK["small"] else 0
            return 16 * (slot_chunk // RAW + 1) + more + 16 * (per // RAW) * i

        def load_loop(sp, name, count, kb, source, per=4, first=0):
            base = CHUNK[name]

            def turn(i, start):
                for j in range(per):
                    n = base + j + per * i
                    if start + j >= RAW:
                        sp.wait_ge(s.wl_split, n - (RAW - 1))
                    k = kb(j)
                    sp.dma_start(raw[(base + j) % RAW][:, 0:k, :], source(i, j)).then_inc(s.w_in[(base + j) % RAW], 16)

            lead = 1 if base < RAW else 0
            if lead:
                turn(0, base)
            if count // per > lead:
                with sp.Fori(lead, count // per) as i:
                    turn(i, RAW)

        def high_loop(act, name, count, kb, per=4):
            base = CHUNK[name]

            def turn(i, start):
                for j in range(per):
                    n = base + j
                    act.wait_ge(s.w_in[n % RAW], w_count(n, i, per))
                    if start + j >= SPLIT:
                        act.wait_ge(s.chunk_done, n + per * i - (SPLIT - 1))
                    act.activation(wH[n % SPLIT][:, 0:kb(j), :], raw[n % RAW][:, 0:kb(j), :],
                                   ACT.Copy).then_inc(s.wh_split, 1)

            lead = 1 if base < SPLIT else 0
            if lead:
                turn(0, base)
            if count // per > lead:
                with act.Fori(lead, count // per) as i:
                    turn(i, SPLIT)

        def low_loop(pool, name, count, kb, per=4):
            base = CHUNK[name]
            with pool.Fori(0, count // per) as i:
                for j in range(per):
                    n = base + j
                    pool.wait_ge(s.wh_split, n + 1 + per * i)
                    pool.tensor_tensor(wL[n % SPLIT][:, 0:kb(j), :], raw[n % RAW][:, 0:kb(j), :],
                                       wH[n % SPLIT][:, 0:kb(j), :].bitcast(F32), ALU.subtract).then_inc(s.wl_split, 1)

        def chunk_product(pe, n, k0, kb, slot, hi, lo, begin, end):
            for k in range(kb):
                for w, x in ((wH, hi), (wH, lo), (wL, hi)):
                    for half in range(2):
                        mm = pe.matmul(G[:, slot, half, 0:HALF], w[n % SPLIT][:, k, :],
                                       x[:, k0 + k, half * HALF:(half + 1) * HALF],
                                       start=(begin and k == 0 and w is wH and x is hi),
                                       stop=(end and k == kb - 1 and w is wL))
            mm.then_inc(s.chunk_done, 1)

        def product_loop(pe, name, turns, plan):
            base, out, per = CHUNK[name], OUT[name], len(plan)
            outs = sum(x[6] for x in plan)

            def turn(i, first):
                for j, (k0, kb, slot, hi, lo, begin, end, at) in enumerate(plan):
                    pe.wait_ge(s.wl_split, base + j + 1 + per * i)
                    if begin and not (first and out + at < 2):
                        pe.wait_ge(s.out_taken, out + at - 1 + outs * i)
                    chunk_product(pe, base + j, k0, kb, slot, hi, lo, begin, end)

            lead = 1 if out < 2 else 0
            if lead:
                turn(0, True)
            if turns > lead:
                with pe.Fori(lead, turns) as i:
                    turn(i, False)

        def panel_plan(name, k, hi, lo, n=4):
            out = OUT[name]
            return [(0, k, (out + j) % 2, hi, lo, True, True, j) for j in range(n)]

        def unit_plan(name, k1, hi1, lo1, k2, hi2, lo2, n=2):
            out, plan = OUT[name], []
            for u in range(n):
                plan.append((0, k1, (out + 2 * u) % 2, hi1, lo1, True, True, 2 * u))
                plan.append((0, k2, (out + 2 * u + 1) % 2, hi2, lo2, True, True, 2 * u + 1))
            return plan

        def norm_act(act, step, n, sq, gain, h_ready, free):
            if free:
                act.wait_ge(s.chunk_done, free)
            for k in range(KD):
                if h_ready is not None:
                    act.wait_ge(h_ready, k + 1)
                act.activation(xH[:, k, :], h[:, k, :], ACT.Copy, scale=gain[:, k:k + 1]).then_inc(s.xh_ready, 1)
                if k >= 2:
                    act.wait_ge(s.sq_used, KD * n + k - 1)
                act.activation(sq[:, k % 2, :], h[:, k, :], ACT.Square).then_inc(s.sq_ready, 1)
            norm_factor(act, step, n)

        def norm_factor(act, step, n):
            act.wait_ge(s.stat_ps, n + 1)
            step(act.activation(halves(rB[:, :]), M01, ACT.Ln, scale=1.0 / D, bias=epsc[:, 0:1]))
            act.activation(rB[:, :], rB[:, :], ACT.Exp, scale=-0.5).then_inc(s.r_ready, 1)

        def norm_dve(dve, n, gain):
            for k in range(KD):
                dve.wait_ge(s.xh_ready, KD * n + k + 1)
                dve.scalar_tensor_tensor(out=xL[:, k, :], in0=h[:, k, :], scalar=gain[:, k:k + 1],
                                         in1=xH[:, k, :].bitcast(F32), op0=ALU.mult,
                                         op1=ALU.subtract).then_inc(s.xl_ready, 1)

        def norm_pe(pe, n, sq, split=True):
            for k in range(KD):
                pe.wait_ge(s.sq_ready, KD * n + k + 1)
                for half in range(2):
                    mm = pe.matmul(M[:, half, 0:HALF], ones[:, :], sq[:, k % 2, half * HALF:(half + 1) * HALF],
                                   start=(k == 0), stop=(k == KD - 1))
                mm.then_inc(s.sq_used, 1)
            mm = pe.matmul(M[0:1, 2, 0:2], ones[:, 0:1], ones[:, 0:2], start=True, stop=True)
            mm.then_inc(s.stat_ps, 1)
            if split:
                pe.wait_ge(s.xl_ready, KD * (n + 1))

        def to_tokens_pe(pe, first, blocks, width=P):
            for i, n in enumerate(TILES):
                if first + i >= 2:
                    pe.wait_ge(s.tok_copied, first + i - 1)
                for m, src in enumerate(blocks):
                    mm = pe.transpose(M[0:n, 2 + (first + i) % 2, m * P:(m + 1) * P], src[:, i * P:i * P + n], ident[:, :])
                mm.then_inc(s.tok_ps, 1)

        def to_tokens_act(act, first, dst, cols, shape=None):
            for i, n in enumerate(TILES):
                act.wait_ge(s.tok_ps, first + i + 1)
                src = M[0:n, 2 + (first + i) % 2, 0:cols]
                if shape:
                    src = src.rearrange("p (h v) -> p h v", h=shape)
                act.activation(dst(i, n), src, ACT.Copy).then_inc(s.tok_copied, 1)

        def branch_pe(pe, b):
            for hd in range(HEADS):
                pe.wait_ge(s.bn_sq, b * HEADS + hd + 1)
                if hd or b:
                    pe.wait_ge(s.bn_ln, b * HEADS + hd)
                for half in range(2):
                    mm = pe.matmul(M[:, half, 0:HALF], ones[:, :], rO[b][:, hd, half * HALF:(half + 1) * HALF],
                                   start=True, stop=True)
                mm.then_inc(s.bn_ps, 1)

        def branch_act(act, step, b, gate):
            if gate is not None:
                func, src = gate
                act.activation(src, src, func).then_inc(s.bn_gate, 1)
            for hd in range(HEADS):
                act.activation(rO[b][:, hd, :], oraw[b][:, hd, :], ACT.Square).then_inc(s.bn_sq, 1)
            for hd in range(HEADS):
                act.wait_ge(s.bn_ps, b * HEADS + hd + 1)
                act.activation(halves(rO[b][:, hd, :]), M01, ACT.Ln, scale=1.0 / DV,
                               bias=epsc[:, 0:1]).then_inc(s.bn_ln, 1)
            act.wait_ge(s.bn_ln, (b + 1) * HEADS)
            act.activation(rO[b][:, :, :], rO[b][:, :, :], ACT.Exp, scale=-0.5).then_inc(s.bn_r, 1)
            act.wait_ge(s.bn_o, b + 1)
            act.activation(oH[b][:, :, :], oraw[b][:, :, :], ACT.Copy).then_inc(s.bn_h, 1)

        def branch_dve(dve, step, b, gate):
            dve.wait_ge(s.bn_r, b + 1)
            ins = dve.scalar_tensor_tensor(out=oraw[b][:, :, :], in0=oraw[b][:, :, :], scalar=ghead[:, b:b + 1],
                                           in1=rO[b][:, :, :], op0=ALU.mult, op1=ALU.mult)
            if gate is not None:
                step(ins)
                dve.wait_ge(s.bn_gate, b + 1)
                ins = dve.tensor_tensor(oraw[b][:, :, :], oraw[b][:, :, :], gate, ALU.mult)
            ins.then_inc(s.bn_o, 1)
            dve.wait_ge(s.bn_h, b + 1)
            dve.tensor_tensor(oL[b][:, :, :], oraw[b][:, :, :], oH[b][:, :, :].bitcast(F32),
                              ALU.subtract).then_inc(s.bn_l, 1)

        def take(dve, out, dst):
            dve.wait_ge(s.chunk_done, out + 1)
            dve.tensor_tensor(halves(dst), out2(out % 2), halves(rB[:, :]), ALU.mult).then_inc(s.out_taken, 1)

        lo64 = [slice(0, DK), slice(DK, P)]

        with nc.Fori(0, DEPTH) as layer:

            def at(x):
                return x[bass.ds(layer, 1)]

            with nc.Block() as block:

                @block.sync
                def _(sp):
                    for j, n in enumerate(("g_mix", "g_ffn", "g_ple")):
                        sp.dma_start(gains[:, j, :], at(a[n]).rearrange("o (k p) -> p (o k)", p=P)).then_inc(s.par_in, 16)
                    for j, n in enumerate(("g_gla_norm", "g_mlstm_norm", "g_diff_norm")):
                        sp.dma_start(ghead[:, j:j + 1], at(a[n]).rearrange("o p -> p o")).then_inc(s.par_in, 16)
                    sp.dma_start(bgk[:, :], at(a["b_gla_gk"]).rearrange("o (k p) -> p (o k)", p=P)).then_inc(s.par_in, 16)
                    for j in range(2):
                        sp.dma_start(bif[32 + 32 * j:32 + 32 * j + HEADS, :],
                                     at(a["b_mlstm_if"])[:, HEADS * j:HEADS * (j + 1)].rearrange("o p -> p o")).then_inc(s.par_in, 16)
                    sp.dma_start(wgk[:, :], at(a["w_gla_gk"]).rearrange("o r e -> (o r) e")).then_inc(s.par_in, 16)
                    sp.dma_start(lamv[:, :, :], at(a["diff_lambda"]).partition_broadcast(P).rearrange("p o r d -> p (o r) d")
                                 ).then_inc(s.par_in, 16)
                    sp.dma_start(lamc[:, :], at(c["lamc"]).rearrange("o p n -> (o p) n")).then_inc(s.par_in, 16)
                    sp.dma_start(m_in[:, :], at(a["state_mlstm_m"]).rearrange("o b h -> h (o b)")).then_inc(s.par_in, 16)
                    PARS = 16 * 13
                    win = at(a["w_in"]).rearrange("o (k p) e -> p (o k) e", p=P)
                    load_loop(sp, "gla", 12, lambda j: KD, lambda i, j: win[:, :, bass.ds(COL_GLA + 4 * P * i + P * j, P)])
                    n = CHUNK["small"]
                    sp.wait_ge(s.wl_split, n - (RAW - 1))
                    for at_col, col in ((0, COL_LR), (32, COL_IF), (64, COL_IF + HEADS), (96, COL_IF)):
                        sp.dma_start(raw[n % RAW][:, :, at_col:at_col + 32], win[:, :, col:col + 32]).then_inc(s.w_in[n % RAW], 16)
                    sp.dma_start(g_reset[:, :], c["greset"]).then_inc(s.greset_in, 16)
                    for q in range(2):
                        sp.dma_start(g_Sin[lo64[q], :, :, :], at(a["state_gla"])[:, :, q:HEADS:2].rearrange(
                            "o b p d v -> d (o b) p v")).then_inc(s.gst_in, 16)
                    sp.wait_ge(s.g_s, NCH + DEC_BATCH)
                    sp.dma_start(at(o["gla_prompt"]).rearrange("o b (p q) d v -> (q d) (o b p) v", q=2),
                                 g_S[:, NCH - 1, :, :]).then_inc(s.gstore, 16)
                    sp.dma_start(at(o["gla_sample"]).rearrange("o b (p q) d v -> (q d) (o b) p v", q=2),
                                 g_Sin[:, :, :, :]).then_inc(s.gstore, 16)
                    load_loop(sp, "ml", 12, lambda j: KD, lambda i, j: win[:, :, bass.ds(COL_ML + 4 * P * i + P * j, P)])
                    sp.wait_ge(s.bn_l, 1)
                    sp.dma_start(r_reset[:, :], c["rreset"]).then_inc(s.rreset_in, 16)
                    sp.wait_ge(s.tok_copied, TOK["mv"] + 5)
                    for q in range(2):
                        sp.dma_start(m_Cin[lo64[q], :, :, 0:DV], at(a["state_mlstm_c"])[:, :, q:HEADS:2].rearrange(
                            "o b p d v -> d (o b) p v")).then_inc(s.mst_in, 16)
                    sp.dma_start(m_Cin[:, :, :, DV:DV + 1], at(a["state_mlstm_n"]).rearrange(
                        "o b (p q) (d u) -> (q d) (o b) p u", q=2, u=1)).then_inc(s.mst_in, 16)
                    sp.wait_ge(s.ml_rows, 4)
                    sp.dma_start(at(o["m_prompt"]).rearrange("o b h -> h (o b)"), r_m[:, SEQ - 1:SEQ]).then_inc(s.mstore, 16)
                    sp.dma_start(at(o["m_sample"]).rearrange("o b h -> h (o b)"),
                                 r_m[:, SEQ + DEC_SEQ - 1:T:DEC_SEQ]).then_inc(s.mstore, 16)
                    sp.wait_ge(s.ml_c, PT + DEC_BATCH)
                    sp.dma_start(at(o["c_prompt"]).rearrange("o b (p q) d v -> (q d) (o b p) v", q=2),
                                 m_C[:, (PT - 1) % 2, :, 0:DV]).then_inc(s.mstore, 16)
                    sp.dma_start(at(o["n_prompt"]).rearrange("o b (p q) (d u) -> (q d) (o b p) u", q=2, u=1),
                                 m_C[:, (PT - 1) % 2, :, DV:DV + 1]).then_inc(s.mstore, 16)
                    sp.dma_start(at(o["c_sample"]).rearrange("o b (p q) d v -> (q d) (o b) p v", q=2),
                                 m_Cin[:, :, :, 0:DV]).then_inc(s.mstore, 16)
                    sp.dma_start(at(o["n_sample"]).rearrange("o b (p q) (d u) -> (q d) (o b) p u", q=2, u=1),
                                 m_Cin[:, :, :, DV:DV + 1]).then_inc(s.mstore, 16)
                    load_loop(sp, "df", 12, lambda j: KD, lambda i, j: win[:, :, bass.ds(COL_DF + 4 * P * i + P * j, P)])
                    sp.wait_ge(s.mstore, 16 * 6)
                    sp.wait_ge(s.bn_l, 2)
                    sp.dma_start(d_cos[:, :], c["cos"]).then_inc(s.trig_in, 16)
                    sp.dma_start(d_sin[:, :], c["sin"]).then_inc(s.trig_in, 16)
                    for i, n in enumerate(TILES):
                        sp.wait_ge(s.tok_copied, TOK["dv"] + i + 1)
                        dst = (at(o["v_prompt"])[:, :, i * P:(i + 1) * P].rearrange("o b t h v -> (o b t) h v") if n == P
                               else at(o["v_sample"]).rearrange("o b t h v -> (o b t) h v"))
                        sp.dma_start(dst, dv[0:n, i, :, :]).then_inc(s.vstore, 16)
                    for i, n in enumerate(TILES):
                        sp.wait_ge(s.tok_copied, TOK["dk"] + i + 1)
                        dst = (at(o["k_prompt"])[:, :, i * P:(i + 1) * P].rearrange("o b t h v -> (o b t) (h v)") if n == P
                               else at(o["k_sample"]).rearrange("o b t h v -> (o b t) (h v)"))
                        sp.dma_start(dst, d_kout[0:n, :]).then_inc(s.kstore, 16)
                    ck, cv = at(a["cache_k"]), at(a["cache_v"])
                    pool_n = a["cache_k"].shape[1]
                    sp.wait_ge(s.rope_done, 8)
                    for g in range(2):
                        for j in range(4 * PAGES):
                            n = 4 * PAGES * g + j
                            if n >= 2:
                                sp.wait_ge(s.tok_ps, TOK["page"] + n - 1)
                            page = sp.value_load(pages[0:1, n:n + 1], min_val=0, max_val=pool_n - 1)
                            sp.dma_start(d_kr[:, n % 2, :, :], ck[:, bass.ds(page, 1)].rearrange(
                                "o q p (m c) d -> (o q p) m (c d)", c=2)).then_inc(s.page[n % 2], 16)
                        for j in range(4 * PAGES):
                            n = 4 * PAGES * g + j
                            if n >= 4:
                                sp.wait_ge(s.v_used, n - 3)
                            page = sp.value_load(pages[0:1, n:n + 1], min_val=0, max_val=pool_n - 1)
                            sp.dma_start(d_V[:, n % 4, :], cv[:, bass.ds(page, 1)].rearrange(
                                "o q p h v -> (o q p) (h v)")).then_inc(s.vpage[n % 4], 16)
                    sp.wait_ge(s.sp_copied, 2)
                    sp.wait_ge(s.pv_copied, PT * HEADS)
                    sp.dma_start(p_tok[:, 0:PT, :], at(a["p_prompt"]).rearrange("o b (i p) e -> p (o b i) e", p=P)).then_inc(s.ptok_in, 16)
                    sp.dma_start(p_tok[0:NS, PT, :], at(a["p_sample"]).rearrange("o b t e -> (o b t) e")).then_inc(s.ptok_in, 16)
                    wg = at(a["w_gate"]).rearrange("o (k p) e -> p (o k) e", p=P)
                    wb = at(a["w_branch"]).rearrange("o (k p) e -> p (o k) e", p=P)
                    for b in range(3):
                        load_loop(sp, f"merge{b}", 16, lambda j: KD if j % 2 == 0 else HEADS,
                                  lambda i, j, b=b: (wg[:, :, bass.ds(D * b + 2 * P * i + P * (j // 2), P)] if j % 2 == 0 else
                                                     wb[:, HEADS * b:HEADS * (b + 1), bass.ds(2 * P * i + P * (j // 2), P)]))
                    wo = at(a["w_out"]).rearrange("o (k p) e -> p (o k) e", p=P)
                    load_loop(sp, "out", 8, lambda j: KD, lambda i, j: wo[:, :, bass.ds(4 * P * i + P * j, P)])
                    fg = at(a["w_ffn_gate"]).rearrange("o (k p) e -> p (o k) e", p=P)
                    fu = at(a["w_ffn_up"]).rearrange("o (k p) e -> p (o k) e", p=P)
                    load_loop(sp, "ffn", 2 * KF, lambda j: KD, lambda i, j: (fg, fu)[j % 2][:, :, bass.ds(2 * P * i + P * (j // 2), P)])
                    fd = at(a["w_ffn_down"]).rearrange("o (k p) e -> p (o k) e", p=P)
                    load_loop(sp, "down", 4 * KD, lambda j: DOWN_K[j % 4][1],
                              lambda i, j: fd[:, DOWN_K[j % 4][0]:DOWN_K[j % 4][0] + DOWN_K[j % 4][1], bass.ds(2 * P * i + P * (j // 4), P)], per=8)
                    pg = at(a["w_ple_gate"]).rearrange("o (k p) e -> p (o k) e", p=P)
                    pp = at(a["w_ple_proj"]).rearrange("o (k p) e -> p (o k) e", p=P)
                    load_loop(sp, "ple", 16, lambda j: KD if j % 2 == 0 else KP,
                              lambda i, j: (pg, pp)[j % 2][:, :, bass.ds(2 * P * i + P * (j // 2), P)])
                    sp.wait_ge(s.gstore, 32)
                    sp.wait_ge(s.mstore, 16 * 6)
                    sp.wait_ge(s.vstore, 16 * 5)
                    sp.wait_ge(s.kstore, 16 * 5)

                @block.gpsimd
                def _(pool):
                    low_loop(pool, "gla", 12, lambda j: KD)
                    low_loop(pool, "small", 1, lambda j: KD, per=1)
                    low_loop(pool, "ml", 12, lambda j: KD)
                    low_loop(pool, "df", 12, lambda j: KD)
                    for b in range(3):
                        low_loop(pool, f"merge{b}", 16, lambda j: KD if j % 2 == 0 else HEADS)
                    low_loop(pool, "out", 8, lambda j: KD)
                    low_loop(pool, "ffn", 2 * KF, lambda j: KD)
                    low_loop(pool, "down", 4 * KD, lambda j: DOWN_K[j % 4][1], per=8)
                    low_loop(pool, "ple", 16, lambda j: KD if j % 2 == 0 else KP)

                def gla_act(act, step):
                    to_tokens_act(act, TOK["gv"], lambda i, n: gv[0:n, i, :, :], HEADS * DV, HEADS)
                    for m in range(2):
                        act.wait_ge(s.gz_ps, m + 1)
                        if m:
                            act.wait_ge(s.gz_min, 2 * m)
                        step(act.activation(halves(g_az[:, :]), M01, ACT.Abs, bias=bgk[:, m:m + 1]))
                        act.sem_inc(s.gz_abs, 1)
                        step(act.activation(g_az[:, :], g_az[:, :], ACT.Exp, scale=-1.0))
                        act.activation(g_az[:, :], g_az[:, :], ACT.Ln, bias=1.0).then_inc(s.gz_ln, 1)
                    act.wait_ge(s.g_b_ready, 2)
                    act.activation(g_E[:, :, :], g_b[:, :, :], ACT.Exp, scale=1.0 / 16).then_inc(s.g_e, 1)
                    act.wait_ge(s.g_qg, 1)
                    act.activation(g_E[:, :, :], g_b[:, :, :], ACT.Exp, scale=-1.0 / 16).then_inc(s.g_e, 1)
                    act.wait_ge(s.g_kg, 2)
                    act.activation(g_E[:, :, :], g_b[:, :, :], ACT.Exp, scale=1.0 / 16).then_inc(s.g_e, 1)
                    to_tokens_act(act, TOK["kd"], lambda i, n: g_kdT[0:n, i, :], HEADS * DK)
                    for i in range(PT):
                        act.wait_ge(s.g_o_ps, i + 1)
                        act.activation(oraw[0][:, :, i * P:(i + 1) * P], M[:, 1, :].rearrange("p (h t) -> p h t", h=HEADS),
                                       ACT.Copy).then_inc(s.g_o, 1)
                    act.wait_ge(s.g_o_ps, PT + 1)
                    act.activation(oraw[0][:, :, SEQ:T], M[:, 1, 0:HEADS * NS].rearrange("p (h t) -> p h t", h=HEADS),
                                   ACT.Copy).then_inc(s.g_o, 1)
                    act.wait_ge(s.g_o, PT + 1)
                    branch_act(act, step, 0, (ACT.Silu, A[:, 4:8, :]))

                def gla_dve(dve, step):
                    for n in range(12):
                        take(dve, n, A[:, n, :] if n < 4 else MG[:, n - 4, :] if n < 8 else A[:, n - 4, :])
                    dve.wait_ge(s.chunk_done, 13)
                    ps = out2(0)
                    for at_row, rows in ((0, RANK), (32, HEADS), (64, HEADS)):
                        ins = dve.tensor_tensor(halves(small[at_row:at_row + rows, :]), ps[at_row:at_row + rows],
                                                halves(rB[at_row:at_row + rows, :]), ALU.mult)
                        if at_row < 64:
                            step(ins)
                    ins.then_inc(s.out_taken, 1)
                    for m in range(2):
                        dve.wait_ge(s.gz_abs, m + 1)
                        step(dve.tensor_scalar(halves(g_E[:, m, :]), M01, bgk[:, m:m + 1], 0.0, ALU.add, ALU.min))
                        dve.sem_inc(s.gz_min, 1)
                        dve.wait_ge(s.gz_ln, m + 1)
                        step(dve.tensor_tensor(g_E[:, m, :], g_E[:, m, :], g_az[:, :], ALU.subtract))
                        dve.sem_inc(s.gz_min, 1)
                        if m == 0:
                            dve.wait_ge(s.greset_in, 16)
                        dve.tensor_tensor_scan(g_b[:, m, :], g_reset[:, :], g_E[:, m, :], 0.0, ALU.mult,
                                               ALU.add).then_inc(s.g_b_ready, 1)
                    dve.wait_ge(s.g_b_ready, 2)
                    dve.wait_ge(s.g_e, 1)
                    step(dve.tensor_copy(g_dec[:, :, 0:NCH], g_E[:, :, CH - 1:SEQ:CH]))
                    step(dve.tensor_copy(g_dec[:, :, NCH:NCH + DEC_BATCH], g_E[:, :, SEQ + DEC_SEQ - 1:T:DEC_SEQ]))
                    dve.wait_ge(s.tok_copied, TOK["gv"] + 5)
                    for q in range(2):
                        step(dve.memset(g_qz[lo64[1 - q], q:HEADS:2, :], 0.0))
                        step(dve.scalar_tensor_tensor(out=g_qz[lo64[q], q:HEADS:2, :], in0=A[lo64[q], 0:2, :], scalar=DK ** -0.5,
                                                      in1=g_E[lo64[q], :, :], op0=ALU.mult, op1=ALU.mult))
                    dve.sem_inc(s.g_qg, 1)
                    dve.wait_ge(s.g_e, 2)
                    dve.tensor_tensor(g_kg[:, :, :], A[:, 2:4, :], g_E[:, :, :], ALU.mult).then_inc(s.g_kg, 1)
                    for m in range(2):
                        step(dve.tensor_copy(g_az[:, m * 16:m * 16 + NCH], g_b[:, m, CH - 1:SEQ:CH]))
                        step(dve.tensor_copy(g_az[:, m * 16 + 8:m * 16 + 16], g_b[:, m, SEQ + DEC_SEQ - 1:T:DEC_SEQ]))
                        for lo, hi, n, width in ((0, SEQ, NCH, CH), (SEQ, T, DEC_BATCH, DEC_SEQ)):
                            v = g_b[:, m, lo:hi].rearrange("p (n t) -> p n t", n=n)
                            last = g_az[:, m * 16 + (8 if lo else 0):m * 16 + (16 if lo else 8)].unsqueeze(2).to_broadcast([P, n, width])
                            step(dve.tensor_tensor(v, last, v, ALU.subtract))
                    dve.sem_inc(s.g_kg, 1)
                    dve.wait_ge(s.g_e, 3)
                    dve.tensor_tensor(A[:, 2:4, :], A[:, 2:4, :], g_E[:, :, :], ALU.mult).then_inc(s.g_kd, 1)
                    dve.wait_ge(s.tok_copied, TOK["kd"] + 5)
                    dve.tensor_tensor(g_kdm[:, :, :], g_kdT[0:NS, PT, :].unsqueeze(1).to_broadcast([NS, DEC_BATCH, HEADS * DK]),
                                      seqm[:, :].unsqueeze(2).to_broadcast([NS, DEC_BATCH, HEADS * DK]),
                                      ALU.mult).then_inc(s.g_kdm_ready, 1)

                    def masked(i):
                        dve.wait_ge(s.g_at_ps, i + 1)
                        if i >= 2:
                            dve.wait_ge(s.g_o_ps, i - 1)
                        dve.tensor_tensor(g_A[:, i % 2, :, :],
                                          M[:, 0, :].rearrange("p (h t) -> p h t", h=HEADS),
                                          gmask[:, :].unsqueeze(1).to_broadcast([P, HEADS, P]), ALU.mult).then_inc(s.g_at, 1)

                    masked(0)
                    for n in range(NCH):
                        if n % 2 == 0 and n // 2 + 1 < PT:
                            masked(n // 2 + 1)
                        dve.wait_ge(s.g_ds_ps, n + 1)
                        ps = M[:, 2 + n % 2, 0:2 * DV].rearrange("p (q v) -> p q v", q=2)
                        if n == 0:
                            dve.tensor_copy(g_S[:, 0, :, :], ps).then_inc(s.g_s, 1)
                            continue
                        dve.wait_ge(s.g_s, n)
                        step(dve.scalar_tensor_tensor(out=g_S[:, n, 0, :], in0=g_S[:, n - 1, 0, :], scalar=g_dec[:, 0, n:n + 1],
                                                      in1=ps[:, 0, :], op0=ALU.mult, op1=ALU.add))
                        dve.scalar_tensor_tensor(out=g_S[:, n, 1, :], in0=g_S[:, n - 1, 1, :], scalar=g_dec[:, 1, n:n + 1],
                                                 in1=ps[:, 1, :], op0=ALU.mult, op1=ALU.add).then_inc(s.g_s, 1)
                    dve.wait_ge(s.g_at_ps, PT + 1)
                    dve.tensor_tensor(g_As[:, :, :], M[0:NS, 0, 0:HEADS * NS].rearrange("p (h t) -> p h t", h=HEADS),
                                      smask[:, :].unsqueeze(1).to_broadcast([NS, HEADS, NS]), ALU.mult).then_inc(s.g_at, 1)
                    dve.wait_ge(s.g_o_ps, PT + 1)
                    dve.wait_ge(s.gst_in, 32)
                    for b in range(DEC_BATCH):
                        n = NCH + b
                        dve.wait_ge(s.g_ds_ps, n + 1)
                        ps = M[:, 2 + n % 2, 0:2 * DV].rearrange("p (q v) -> p q v", q=2)
                        step(dve.scalar_tensor_tensor(out=g_Sin[:, b, 0, :], in0=g_Sin[:, b, 0, :], scalar=g_dec[:, 0, n:n + 1],
                                                      in1=ps[:, 0, :], op0=ALU.mult, op1=ALU.add))
                        dve.scalar_tensor_tensor(out=g_Sin[:, b, 1, :], in0=g_Sin[:, b, 1, :], scalar=g_dec[:, 1, n:n + 1],
                                                 in1=ps[:, 1, :], op0=ALU.mult, op1=ALU.add).then_inc(s.g_s, 1)
                    branch_dve(dve, step, 0, A[:, 4:8, :])

                def gla_pe(pe):
                    pe.wait_ge(s.out_taken, 12)
                    to_tokens_pe(pe, TOK["gv"], [MG[:, m, :] for m in range(4)])
                    pe.wait_ge(s.out_taken, 13)
                    for m in range(2):
                        if m:
                            pe.wait_ge(s.gz_min, 2)
                            pe.wait_ge(s.gz_abs, 1)
                        for half in range(2):
                            mm = pe.matmul(M[:, half, 0:HALF], wgk[:, m * P:(m + 1) * P], small[0:RANK, half * HALF:(half + 1) * HALF],
                                           start=True, stop=True)
                        mm.then_inc(s.gz_ps, 1)
                    pe.wait_ge(s.g_kd, 1)
                    to_tokens_pe(pe, TOK["kd"], [A[:, 2 + m, :] for m in range(2)])
                    pe.wait_ge(s.tok_copied, TOK["kd"] + 5)

                    def scores(i):
                        if i:
                            pe.wait_ge(s.g_at, i)
                        for hd in range(HEADS):
                            mm = pe.matmul(M[:, 0, hd * P:(hd + 1) * P], g_kg[:, hd // 2, i * P:(i + 1) * P],
                                           g_qz[:, hd, i * P:(i + 1) * P], start=True, stop=True)
                        mm.then_inc(s.g_at_ps, 1)

                    scores(0)
                    for n in range(NCH):
                        i, q = n // 2, lo64[n % 2]
                        if n % 2 == 0 and i + 1 < PT:
                            scores(i + 1)
                        if n >= 2:
                            pe.wait_ge(s.g_s, n - 1)
                        for hd in range(HEADS):
                            c0 = (hd // 2) * DV
                            mm = pe.matmul(M[lo64[hd % 2], 2 + n % 2, c0:c0 + DV], g_kdT[q, i, hd * DK:(hd + 1) * DK], gv[q, i, hd, :],
                                           start=True, stop=True)
                        mm.then_inc(s.g_ds_ps, 1)
                        if n % 2 == 0:
                            continue
                        pe.wait_ge(s.g_at, i + 1)
                        pe.wait_ge(s.g_s, n)
                        if i:
                            pe.wait_ge(s.g_o, i)
                        for hd in range(HEADS):
                            pe.matmul(M[:, 1, hd * P:(hd + 1) * P], gv[:, i, hd, :], g_A[:, i % 2, hd, :], start=True, stop=False,
                                      skip_group_check=True)
                            for m in (n - 1, n):
                                if m:
                                    t0 = m * CH
                                    mm = pe.matmul(M[:, 1, hd * P + t0 % P:hd * P + t0 % P + CH], g_S[:, m - 1, hd // 2, :],
                                                   g_qz[:, hd, t0:t0 + CH], start=False, stop=(m == n), skip_group_check=True)
                        mm.then_inc(s.g_o_ps, 1)
                    pe.wait_ge(s.g_at, PT)
                    for hd in range(HEADS):
                        mm = pe.matmul(M[0:NS, 0, hd * NS:(hd + 1) * NS], g_kg[:, hd // 2, SEQ:T], g_qz[:, hd, SEQ:T],
                                       start=True, stop=True)
                    mm.then_inc(s.g_at_ps, 1)
                    pe.wait_ge(s.g_at, PT + 1)
                    pe.wait_ge(s.gst_in, 32)
                    pe.wait_ge(s.g_o, PT)
                    for hd in range(HEADS):
                        pe.matmul(M[:, 1, hd * NS:(hd + 1) * NS], gv[0:NS, PT, hd, :], g_As[:, hd, :], start=(hd == 0), stop=False,
                                  skip_group_check=True)
                    for b in range(DEC_BATCH):
                        for hd in range(HEADS):
                            t0 = b * DEC_SEQ
                            mm = pe.matmul(M[:, 1, hd * NS + t0:hd * NS + t0 + DEC_SEQ], g_Sin[:, b, hd // 2, :],
                                           g_qz[:, hd, SEQ + t0:SEQ + t0 + DEC_SEQ], start=False,
                                           stop=(b == DEC_BATCH - 1), skip_group_check=True)
                    mm.then_inc(s.g_o_ps, 1)
                    pe.wait_ge(s.g_kdm_ready, 1)
                    for b in range(DEC_BATCH):
                        n = NCH + b
                        pe.wait_ge(s.g_s, n - 1)
                        for hd in range(HEADS):
                            c0 = (hd // 2) * DV
                            mm = pe.matmul(M[lo64[hd % 2], 2 + n % 2, c0:c0 + DV], g_kdm[:, b, hd * DK:(hd + 1) * DK], gv[0:NS, PT, hd, :],
                                           start=True, stop=True)
                        mm.then_inc(s.g_ds_ps, 1)
                    branch_pe(pe, 0)

                def mlstm_act(act, step):
                    to_tokens_act(act, TOK["mv"], lambda i, n: mv[0:n, i, :, 0:DV], HEADS * DV, HEADS)
                    to_tokens_act(act, TOK["mk"], lambda i, n: m_kT[0:n, i, :, :], HEADS * DK, HEADS)
                    act.wait_ge(s.ml_rows, 1)
                    step(act.activation(r_en[:, :], r_m[:, :], ACT.Abs))
                    step(act.activation(r_en[:, :], r_en[:, :], ACT.Exp, scale=-1.0))
                    act.activation(r_en[:, :], r_en[:, :], ACT.Ln, bias=1.0).then_inc(s.ml_ln, 1)
                    act.wait_ge(s.ml_rows, 4)
                    step(act.activation(r_wi[:, :], r_wi[:, :], ACT.Exp))
                    step(act.activation(r_d[:, :], r_d[:, :], ACT.Exp))
                    act.activation(r_en[:, :], r_m[:, :], ACT.Exp, scale=-1.0).then_inc(s.ml_ex, 1)
                    for i, n in enumerate(TILES):
                        act.wait_ge(s.ml_d_ps, i + 1)
                        act.wait_ge(s.ml_col, 1)
                        if i:
                            act.wait_ge(s.ml_sd, i)
                        for hd in range(HEADS):
                            act.activation(m_D[0:n, hd * n:(hd + 1) * n], M[0:n, 0, hd * n:(hd + 1) * n], ACT.Exp, scale=-1.0,
                                           bias=m_cols[0:n, i, hd:hd + 1]).then_inc(s.ml_d, 1)
                        act.wait_ge(s.ml_den_ps, i + 1)
                        if i:
                            act.wait_ge(s.ml_o, i)
                        act.activation(m_ad[:, 0:HEADS * n], M[:, 3, 0:HEADS * n], ACT.Abs).then_inc(s.ml_ad, 1)
                    act.wait_ge(s.ml_o, 5)
                    act.wait_ge(s.ml_c, PT + DEC_BATCH)
                    branch_act(act, step, 1, (ACT.Sigmoid, B[:, 4:8, :]))

                def mlstm_dve(dve, step):
                    for n in range(12):
                        take(dve, OUT["ml"] + n, B[:, n, :] if n < 4 else MG[:, n - 4, :] if n < 8 else B[:, n - 4, :])
                    step(dve.memset(mv[:, :, :, DV:DV + 1], 1.0))
                    step(dve.tensor_scalar(r_a[:, :], small[32:32 + HEADS, :], bif[32:32 + HEADS, 0:1], None, ALU.add))
                    step(dve.tensor_scalar(r_m[:, :], small[64:64 + HEADS, :], bif[64:64 + HEADS, 0:1], None, ALU.add))
                    dve.sem_inc(s.ml_rows, 1)
                    step(dve.tensor_scalar(r_F[:, :], r_m[:, :], 0.0, None, ALU.min))
                    dve.wait_ge(s.ml_ln, 1)
                    step(dve.tensor_tensor(r_m[:, :], r_F[:, :], r_en[:, :], ALU.subtract))
                    dve.wait_ge(s.rreset_in, 16)
                    step(dve.tensor_tensor_scan(r_F[:, :], r_reset[:, :], r_m[:, :], 0.0, ALU.mult, ALU.add))
                    step(dve.tensor_tensor(r_a[:, :], r_a[:, :], r_F[:, :], ALU.subtract))
                    step(dve.memset(r_d[:, :], 0.0))
                    step(dve.tensor_copy(r_d[:, P:SEQ:P], r_F[:, P - 1:SEQ - P:P]))
                    step(dve.tensor_tensor_scan(r_g[:, 0:SEQ], r_d[:, 0:SEQ], r_a[:, 0:SEQ], 0.0, ALU.add, ALU.max))
                    for b in range(DEC_BATCH):
                        t0 = SEQ + b * DEC_SEQ
                        step(dve.tensor_tensor_scan(r_g[:, t0:t0 + DEC_SEQ], r_d[:, t0:t0 + DEC_SEQ], r_a[:, t0:t0 + DEC_SEQ],
                                                    m_in[:, b:b + 1], ALU.add, ALU.max))
                    step(dve.tensor_tensor(r_m[:, :], r_F[:, :], r_g[:, :], ALU.add))
                    step(dve.memset(m_prev[:, 0:1], 0.0))
                    step(dve.tensor_copy(m_prev[:, 1:PT], r_m[:, P - 1:SEQ - P:P]))
                    step(dve.tensor_copy(m_prev[:, PT:12], m_in[:, :]))
                    dve.sem_inc(s.ml_rows, 1)
                    for lo, hi, n, width, k in ((0, SEQ, PT, P, 0), (SEQ, T, DEC_BATCH, DEC_SEQ, PT)):
                        g3 = r_g[:, lo:hi].rearrange("p (n t) -> p n t", n=n)
                        step(dve.tensor_tensor(r_wi[:, lo:hi].rearrange("p (n t) -> p n t", n=n),
                                               m_prev[:, k:k + n].unsqueeze(2).to_broadcast([HEADS, n, width]), g3, ALU.subtract))
                        step(dve.tensor_tensor(r_d[:, lo:hi].rearrange("p (n t) -> p n t", n=n),
                                               r_a[:, lo:hi].rearrange("p (n t) -> p n t", n=n),
                                               g3[:, :, width - 1:width].to_broadcast([HEADS, n, width]), ALU.subtract))
                    dve.sem_inc(s.ml_rows, 2)
                    dve.wait_ge(s.ml_col_ps, 1)
                    step(dve.tensor_copy(m_cols[:, 0:PT, :], M[:, 0, 0:8 * PT].rearrange("p (i k) -> p i k", i=PT)))
                    dve.tensor_copy(m_cols[0:NS, PT, :], M[0:NS, 0, 8 * PT:8 * PT + 8]).then_inc(s.ml_col, 1)
                    dve.wait_ge(s.ml_col, 1)
                    for p in range(2):
                        ps = M01 if p == 0 else M23
                        dve.wait_ge(s.ml_wi_ps, p + 1)
                        for q in range(2):
                            r, hd = lo64[q], 2 * p + q
                            step(dve.memset(m_qwz[lo64[1 - q], hd, :], 0.0))
                            step(dve.tensor_tensor(halves(m_qwz[r, hd, :]), halves(B[r, p, :]), ps[r], ALU.mult))
                            step(dve.memset(m_qz[lo64[1 - q], hd, :], 0.0))
                            step(dve.tensor_copy(m_qz[r, hd, :], B[r, p, :]))
                        step(dve.tensor_copy(m_dec[:, p, 0:2], ps[:, 0, P - 1:2 * P:P]))
                        step(dve.tensor_copy(m_dec[:, p, 2:4], ps[:, 1, 3 * P - 1 - HALF:4 * P - HALF:P]))
                        dve.tensor_copy(m_dec[:, p, 4:12], ps[:, 1, SEQ + DEC_SEQ - 1 - HALF:HALF:DEC_SEQ]).then_inc(s.ml_wi, 1)
                    dve.wait_ge(s.ml_wi, 2)
                    dve.wait_ge(s.tok_copied, TOK["mk"] + 5)
                    for i, n in enumerate(TILES):
                        step(dve.scalar_tensor_tensor(out=m_kw[0:n, i, :, :], in0=m_kT[0:n, i, :, :], scalar=DK ** -0.5,
                                                      in1=m_cols[0:n, i, 4:8].unsqueeze(2).to_broadcast([n, HEADS, DK]),
                                                      op0=ALU.mult, op1=ALU.mult))
                    dve.sem_inc(s.ml_kw, 1)
                    dve.wait_ge(s.mst_in, 48)
                    for p in range(2):
                        for hd in (2 * p, 2 * p + 1):
                            step(dve.tensor_tensor(m_qns[:, hd, :].rearrange("p (b t) -> p b t", b=DEC_BATCH),
                                                   m_qwz[:, hd, SEQ:T].rearrange("p (b t) -> p b t", b=DEC_BATCH),
                                                   m_Cin[:, :, p, DV:DV + 1].to_broadcast([P, DEC_BATCH, DEC_SEQ]), ALU.mult))
                    dve.sem_inc(s.ml_qn, 1)
                    for i, n in enumerate(TILES):
                        w = HEADS * n
                        if i and n == P:
                            if i > 1:
                                dve.wait_ge(s.ml_den_ps, i)
                            for p in range(2):
                                ins = dve.tensor_scalar(m_qnz[:, 2 * p:2 * p + 2, :], m_qwz[:, 2 * p:2 * p + 2, i * P:(i + 1) * P],
                                                        m_C[:, (i - 1) % 2, p, DV:DV + 1], None, ALU.mult)
                                if p == 0:
                                    step(ins)
                            ins.then_inc(s.ml_qn, 1)
                        dve.wait_ge(s.ml_s_ps, i + 1)
                        dve.wait_ge(s.ml_d, HEADS * (i + 1))
                        if i:
                            dve.wait_ge(s.ml_den_ps, i)
                        dve.scalar_tensor_tensor(out=m_SD[0:n, 0:w], in0=M[0:n, 1, 0:w], scalar=DK ** -0.5, in1=m_D[0:n, 0:w],
                                                 op0=ALU.mult, op1=ALU.mult).then_inc(s.ml_sd, 1)
                        if n == P:
                            dve.wait_ge(s.ml_c_ps, i + 1)
                            ps = M[:, 1, 0:2 * (DV + 1)].rearrange("p (q v) -> p q v", q=2)
                            if i == 0:
                                dve.tensor_copy(m_C[:, 0, :, :], ps).then_inc(s.ml_c, 1)
                            else:
                                for p in range(2):
                                    ins = dve.scalar_tensor_tensor(out=m_C[:, i % 2, p, :], in0=m_C[:, (i - 1) % 2, p, :],
                                                                   scalar=m_dec[:, p, i:i + 1], in1=ps[:, p, :],
                                                                   op0=ALU.mult, op1=ALU.add)
                                    if p == 0:
                                        step(ins)
                                ins.then_inc(s.ml_c, 1)
                            dve.wait_ge(s.ml_c, i + 1)
                        dve.wait_ge(s.ml_ad, i + 1)
                        dve.wait_ge(s.ml_e_ps, i + 1)
                        step(dve.tensor_tensor(m_ad[:, 0:w], m_ad[:, 0:w], M[:, 0, 0:w], ALU.max))
                        step(dve.reciprocal(m_ad[:, 0:w], m_ad[:, 0:w]))
                        dve.wait_ge(s.ml_n_ps, i + 1)
                        dve.tensor_tensor(oraw[1][:, :, i * P:i * P + n], M[:, 2, 0:w].rearrange("p (h t) -> p h t", h=HEADS),
                                          m_ad[:, 0:w].rearrange("p (h t) -> p h t", h=HEADS), ALU.mult).then_inc(s.ml_o, 1)
                    dve.tensor_tensor(m_kwm[:, :, :], m_kw[0:NS, PT, :, :].rearrange("p h d -> p (h d)").unsqueeze(1).to_broadcast(
                        [NS, DEC_BATCH, HEADS * DK]), seqm[:, :].unsqueeze(2).to_broadcast([NS, DEC_BATCH, HEADS * DK]),
                        ALU.mult).then_inc(s.ml_kwm_ready, 1)
                    for b in range(DEC_BATCH):
                        n = PT + b
                        dve.wait_ge(s.ml_c_ps, n + 1)
                        ps = M[:, b % 2, 0:2 * (DV + 1)].rearrange("p (q v) -> p q v", q=2)
                        for p in range(2):
                            ins = dve.scalar_tensor_tensor(out=m_Cin[:, b, p, :], in0=m_Cin[:, b, p, :], scalar=m_dec[:, p, n:n + 1],
                                                           in1=ps[:, p, :], op0=ALU.mult, op1=ALU.add)
                            if p == 0:
                                step(ins)
                        ins.then_inc(s.ml_c, 1)
                    branch_dve(dve, step, 1, B[:, 4:8, :])

                def mlstm_pe(pe):
                    pe.wait_ge(s.out_taken, OUT["ml"] + 12)
                    to_tokens_pe(pe, TOK["mv"], [MG[:, m, :] for m in range(4)])
                    to_tokens_pe(pe, TOK["mk"], [B[:, 2 + m, :] for m in range(2)])
                    pe.wait_ge(s.ml_ex, 1)
                    pe.wait_ge(s.tok_copied, TOK["mk"] + 5)
                    for i, n in enumerate(TILES):
                        for j, row in enumerate((r_a, r_d)):
                            mm = pe.matmul(M[0:n, 0, 8 * i + 4 * j:8 * i + 4 * j + 4], row[:, i * P:i * P + n], ident[0:HEADS, 0:HEADS],
                                           start=True, stop=True)
                    mm.then_inc(s.ml_col_ps, 1)
                    pe.wait_ge(s.ml_col, 1)
                    for p in range(2):
                        for half in range(2):
                            mm = pe.matmul(M[:, 2 * p + half, 0:HALF], selp[:, p, :], r_wi[:, half * HALF:(half + 1) * HALF],
                                           start=True, stop=True)
                        mm.then_inc(s.ml_wi_ps, 1)
                    pe.wait_ge(s.ml_wi, 2)
                    for i, n in enumerate(TILES):
                        t0, w = i * P, HEADS * n
                        mask = big if n == P else sbig
                        if i:
                            pe.wait_ge(s.ml_o, i)
                        for hd in range(HEADS):
                            dst = M[0:n, 0, hd * n:(hd + 1) * n]
                            pe.matmul(dst, ident[0:n, 0:n], mask[:, :], start=True, stop=False)
                            mm = pe.matmul(dst, sel[:, hd, 0:n], r_g[:, t0:t0 + n], start=False, stop=True)
                        mm.then_inc(s.ml_d_ps, 1)
                        if i:
                            pe.wait_ge(s.ml_c, i)
                        for hd in range(HEADS):
                            mm = pe.matmul(M[0:n, 1, hd * n:(hd + 1) * n], B[:, 2 + hd // 2, t0:t0 + n], m_qz[:, hd, t0:t0 + n],
                                           start=True, stop=True)
                        mm.then_inc(s.ml_s_ps, 1)
                        pe.wait_ge(s.ml_d, HEADS * (i + 1))
                        for hd in range(HEADS):
                            mm = pe.matmul(M[:, 0, hd * n:(hd + 1) * n], sel[:, hd, :], r_en[:, t0:t0 + n], start=True, stop=True)
                        mm.then_inc(s.ml_e_ps, 1)
                        pe.wait_ge(s.ml_sd, i + 1)
                        if n == P:
                            pe.wait_ge(s.ml_kw, 1)
                            for hd in range(HEADS):
                                c0 = (hd // 2) * (DV + 1)
                                mm = pe.matmul(M[lo64[hd % 2], 1, c0:c0 + DV + 1], m_kw[:, i, hd, :], mv[:, i, hd, :],
                                               start=True, stop=True)
                            mm.then_inc(s.ml_c_ps, 1)
                            if i:
                                pe.wait_ge(s.ml_qn, i + 1)
                            for hd in range(HEADS):
                                dst = M[:, 2, hd * P:(hd + 1) * P]
                                mm = pe.matmul(dst, mv[:, i, hd, 0:DV], m_SD[:, hd * P:(hd + 1) * P], start=True, stop=(i == 0))
                                if i:
                                    mm = pe.matmul(dst, m_C[:, (i - 1) % 2, hd // 2, 0:DV], m_qwz[:, hd, t0:t0 + P],
                                                   start=False, stop=True)
                            mm.then_inc(s.ml_n_ps, 1)
                            for hd in range(HEADS):
                                dst = M[:, 3, hd * P:(hd + 1) * P]
                                mm = pe.matmul(dst, ones[:, :], m_SD[:, hd * P:(hd + 1) * P], start=True, stop=(i == 0))
                                if i:
                                    mm = pe.matmul(dst, ones[:, :], m_qnz[:, hd, :], start=False, stop=True)
                            mm.then_inc(s.ml_den_ps, 1)
                        else:
                            pe.wait_ge(s.ml_qn, 1)
                            for hd in range(HEADS):
                                pe.matmul(M[:, 2, hd * NS:(hd + 1) * NS], mv[0:NS, i, hd, 0:DV], m_SD[0:NS, hd * NS:(hd + 1) * NS],
                                          start=(hd == 0), stop=False, skip_group_check=True)
                            for b in range(DEC_BATCH):
                                for hd in range(HEADS):
                                    q0 = b * DEC_SEQ
                                    mm = pe.matmul(M[:, 2, hd * NS + q0:hd * NS + q0 + DEC_SEQ], m_Cin[:, b, hd // 2, 0:DV],
                                                   m_qwz[:, hd, SEQ + q0:SEQ + q0 + DEC_SEQ], start=False,
                                                   stop=(b == DEC_BATCH - 1), skip_group_check=True)
                            mm.then_inc(s.ml_n_ps, 1)
                            for hd in range(HEADS):
                                dst = M[:, 3, hd * NS:(hd + 1) * NS]
                                pe.matmul(dst, ones[0:NS, :], m_SD[0:NS, hd * NS:(hd + 1) * NS], start=True, stop=False)
                                mm = pe.matmul(dst, ones[:, :], m_qns[:, hd, :], start=False, stop=True)
                            mm.then_inc(s.ml_den_ps, 1)
                    pe.wait_ge(s.ml_kwm_ready, 1)
                    pe.wait_ge(s.ml_o, 5)
                    for b in range(DEC_BATCH):
                        if b >= 2:
                            pe.wait_ge(s.ml_c, PT + b - 1)
                        for hd in range(HEADS):
                            c0 = (hd // 2) * (DV + 1)
                            mm = pe.matmul(M[lo64[hd % 2], b % 2, c0:c0 + DV + 1], m_kwm[:, b, hd * DK:(hd + 1) * DK],
                                           mv[0:NS, PT, hd, :], start=True, stop=True)
                        mm.then_inc(s.ml_c_ps, 1)
                    branch_pe(pe, 1)

                def attention_act(act, step):
                    act.wait_ge(s.lam_sum, 1)
                    act.activation(lam[:, 2:4], lam[:, 0:2], ACT.Exp).then_inc(s.lam_exp, 1)
                    to_tokens_act(act, TOK["dv"], lambda i, n: dv[0:n, i, :, :], HEADS * DV, HEADS)
                    for i, n in enumerate(TILES):
                        act.wait_ge(s.tok_ps, TOK["dk"] + i + 1)
                        if i:
                            act.wait_ge(s.kstore, 16 * i)
                        act.activation(d_kout[0:n, :], M[0:n, 2 + (TOK["dk"] + i) % 2, :], ACT.Copy).then_inc(s.tok_copied, 1)

                    def exps(n):
                        width = P * (n // HEADS + 1)
                        act.wait_ge(s.nm_ready, n + 1)
                        if n:
                            act.wait_ge(s.w_ready, n)
                        for m in range(2):
                            act.activation(d_e[:, m, 0:width], M[:, m, 0:width], ACT.Exp, bias=d_nm[:, m:m + 1],
                                           accum_out=d_l[:, m:m + 1]).then_inc(s.e_ready, 1)

                    def turned(n):
                        width = P * (n // HEADS + 1)
                        act.wait_ge(s.wt_ps, n + 1)
                        if n:
                            act.wait_ge(s.pv_ps, n)
                        act.activation(d_wT[:, 0:width], M[:, 2, 0:width], ACT.Copy).then_inc(s.wt_copied, 1)

                    for n in range(PT * HEADS + 1):
                        if n < PT * HEADS:
                            exps(n)
                        if n:
                            turned(n - 1)
                    for g in range(2):
                        for j in range(4 * PAGES):
                            n = 4 * PAGES * g + j
                            act.wait_ge(s.tok_ps, TOK["page"] + n + 1)
                            if j % PAGES == 0 and n:
                                act.wait_ge(s.ss_ps, n // PAGES)
                            act.activation(d_KT[:, :, (j % PAGES) * PAGE:(j % PAGES + 1) * PAGE],
                                           M[:, 2 + n % 2, :].rearrange("p (h k) -> p h k", h=HEADS), ACT.Copy).then_inc(s.tok_copied, 1)
                        act.wait_ge(s.ss_nm, g + 1)
                        act.activation(d_es[:, :], M[:, 0, 0:2 * PAGE + NS], ACT.Exp, bias=d_nm[:, 0:1],
                                       accum_out=d_l[:, 0:1]).then_inc(s.ss_e, 1)
                    act.wait_ge(s.sp_copied, 2)
                    branch_act(act, step, 2, None)

                def attention_dve(dve, step):
                    for j in range(2):
                        step(dve.tensor_tensor(lamp[:, :], lamv[:, 2 * j, :], lamv[:, 2 * j + 1, :], ALU.mult))
                        step(dve.tensor_reduce(lam[:, j:j + 1], lamp[:, :], AX.X, ALU.add))
                    dve.sem_inc(s.lam_sum, 1)
                    for n in range(12):
                        take(dve, OUT["df"] + n, A[:, n, :] if n < 8 else MG[:, n - 8, :])
                    dve.wait_ge(s.lam_exp, 1)
                    step(dve.tensor_tensor(lam[:, 4:5], lam[:, 3:4], lam[:, 2:3], ALU.subtract))
                    step(dve.tensor_tensor(lam[:, 5:6], lam[:, 4:5], lamc[:, 0:1], ALU.subtract))
                    step(dve.tensor_tensor(ghead[:, 2:3], ghead[:, 2:3], lamc[:, 1:2], ALU.mult))
                    step(dve.scalar_tensor_tensor(out=lam[:, 6:7], in0=sign[:, 1:2], scalar=lam[:, 5:6], in1=sign[:, 0:1],
                                                  op0=ALU.mult, op1=ALU.add))
                    dve.wait_ge(s.trig_in, 32)
                    for n in range(8):
                        ps, f = (M01 if n % 2 == 0 else M23), (DK ** -0.5 if n < 4 else 1.0)
                        dve.wait_ge(s.rope_ps, n + 1)
                        step(dve.scalar_tensor_tensor(out=halves(d_t1[:, :]), in0=ps, scalar=f, in1=halves(d_sin[:, :]),
                                                      op0=ALU.mult, op1=ALU.mult))
                        step(dve.scalar_tensor_tensor(out=A[:, n, :], in0=A[:, n, :], scalar=f, in1=d_cos[:, :],
                                                      op0=ALU.mult, op1=ALU.mult))
                        step(dve.tensor_tensor(A[:, n, :], A[:, n, :], d_t1[:, :], ALU.add))
                        dve.sem_inc(s.rope_done, 1)
                    step(dve.memset(d_qbd[:, :, :, :, :], 0.0))
                    for m in range(2):
                        for hd in range(HEADS):
                            q0 = hd * 2 * DEC_SEQ + m * DEC_SEQ
                            flat = d_qbd[lo64[m], :, hd, :, :].rearrange("p b x y -> p b (x y)")
                            step(dve.tensor_copy(flat[:, :, q0:q0 + DEC_SEQ],
                                                 A[lo64[m], hd, SEQ:T].rearrange("p (b t) -> p b t", b=DEC_BATCH)))
                    dve.sem_inc(s.qbd_ready, 1)

                    def maxima(n):
                        width = P * (n // HEADS + 1)
                        dve.wait_ge(s.sc_ps, n + 1)
                        if n:
                            dve.wait_ge(s.e_ready, 2 * n)
                        dve.tensor_reduce(d_nm[:, 0:2], M[:, 0:2, 0:width], AX.X, ALU.max, negate=True).then_inc(s.nm_ready, 1)

                    def weights(n):
                        width = P * (n // HEADS + 1)
                        dve.wait_ge(s.e_ready, 2 * n + 2)
                        if n:
                            dve.wait_ge(s.wt_ps, n)
                        step(dve.reciprocal(d_rc[:, :], d_l[:, :]))
                        step(dve.tensor_tensor(d_rc[:, 1:2], d_rc[:, 1:2], lam[:, 5:6], ALU.mult))
                        step(dve.tensor_scalar(d_w[:, 0:width], d_e[:, 0, 0:width], d_rc[:, 0:1], None, ALU.mult))
                        dve.scalar_tensor_tensor(out=d_w[:, 0:width], in0=d_e[:, 1, 0:width], scalar=d_rc[:, 1:2],
                                                 in1=d_w[:, 0:width], op0=ALU.mult, op1=ALU.add).then_inc(s.w_ready, 1)

                    def values(n):
                        i, hd = n // HEADS, n % HEADS
                        dve.wait_ge(s.pv_ps, n + 1)
                        dve.tensor_copy(oraw[2][:, hd, i * P:(i + 1) * P], M[:, 3, 0:P]).then_inc(s.pv_copied, 1)

                    for n in range(PT * HEADS + 2):
                        if n < PT * HEADS:
                            maxima(n)
                            weights(n)
                        if n >= 2:
                            values(n - 2)
                    for g in range(2):
                        dve.wait_ge(s.ss_ps, 4 * (g + 1))
                        if g == 0:
                            dve.wait_ge(s.e_ready, 2 * PT * HEADS)
                            dve.wait_ge(s.w_ready, PT * HEADS)
                        dve.tensor_reduce(d_nm[:, 0:1], M[:, 0, 0:2 * PAGE + NS], AX.X, ALU.max, negate=True).then_inc(s.ss_nm, 1)
                        dve.wait_ge(s.ss_e, g + 1)
                        step(dve.reciprocal(d_rc[:, 0:1], d_l[:, 0:1]))
                        step(dve.tensor_tensor(d_rc[:, 0:1], d_rc[:, 0:1], lam[:, 6:7], ALU.mult))
                        dve.tensor_scalar(d_es[:, :], d_es[:, :], d_rc[:, 0:1], None, ALU.mult).then_inc(s.ss_w, 1)
                        dve.wait_ge(s.st_ps, g + 1)
                        for pg in range(PAGES):
                            v = M[:, 1, pg * P:(pg + 1) * P].rearrange("p (j h c t) -> p (j h) t c", j=4, h=HEADS, c=2)
                            step(dve.tensor_reduce(d_wTs[:, pg, :, :, :].rearrange("p j h t -> p (j h) t"), v, AX.X, ALU.add))
                        v = M[0:NS, 1, 2 * P:3 * P].rearrange("p (j h c t) -> p (j h) t c", j=4, h=HEADS, c=2)
                        dve.tensor_reduce(d_wTn[:, :, :, :].rearrange("p j h t -> p (j h) t"), v, AX.X, ALU.add).then_inc(s.st_red, 1)
                        dve.wait_ge(s.sp_ps, g + 1)
                        dve.tensor_copy(oraw[2][:, :, SEQ + 16 * g:SEQ + 16 * (g + 1)],
                                        M[:, 0, 2 * PAGE + NS:2 * PAGE + NS + 64].rearrange("p (h t) -> p h t", h=HEADS)
                                        ).then_inc(s.sp_copied, 1)
                    branch_dve(dve, step, 2, None)

                def attention_pe(pe):
                    pe.wait_ge(s.out_taken, OUT["df"] + 12)
                    to_tokens_pe(pe, TOK["dv"], [MG[:, m, :] for m in range(4)])
                    for n in range(8):
                        if n >= 2:
                            pe.wait_ge(s.rope_done, n - 1)
                        if n == 1:
                            pe.wait_ge(s.tok_copied, TOK["dv"] + 5)
                        for half in range(2):
                            mm = pe.matmul(M[:, 2 * (n % 2) + half, 0:HALF], rot[:, :], A[:, n, half * HALF:(half + 1) * HALF],
                                           start=True, stop=True)
                        mm.then_inc(s.rope_ps, 1)
                    pe.wait_ge(s.rope_done, 8)
                    to_tokens_pe(pe, TOK["dk"], [A[:, 4 + m, :] for m in range(4)])

                    def scores(n):
                        i, hd = n // HEADS, n % HEADS
                        if n:
                            pe.wait_ge(s.e_ready, 2 * n)
                        for m in range(2):
                            r = lo64[m]
                            pe.matmul(M[:, m, 0:(i + 1) * P], A[r, hd, i * P:(i + 1) * P], A[r, 4 + hd, 0:(i + 1) * P],
                                      start=True, stop=False)
                            mm = pe.matmul(M[:, m, i * P:(i + 1) * P], ident[:, :], neg[:, :], start=False, stop=True)
                        mm.then_inc(s.sc_ps, 1)

                    def turn(n):
                        i = n // HEADS
                        pe.wait_ge(s.w_ready, n + 1)
                        pe.wait_ge(s.tok_copied, TOK["dk"] + 5)
                        if n:
                            pe.wait_ge(s.wt_copied, n)
                        for j in range(i + 1):
                            mm = pe.transpose(M[:, 2, j * P:(j + 1) * P], d_w[:, j * P:(j + 1) * P], ident[:, :])
                        mm.then_inc(s.wt_ps, 1)

                    def value(n):
                        i, hd = n // HEADS, n % HEADS
                        pe.wait_ge(s.wt_copied, n + 1)
                        if n:
                            pe.wait_ge(s.pv_copied, n)
                        for j in range(i + 1):
                            mm = pe.matmul(M[:, 3, 0:P], dv[:, j, hd, :], d_wT[:, j * P:(j + 1) * P],
                                           start=(j == 0), stop=(j == i))
                        mm.then_inc(s.pv_ps, 1)

                    for n in range(PT * HEADS + 1):
                        if n < PT * HEADS:
                            scores(n)
                        if n:
                            turn(n - 1)
                            value(n - 1)
                    pe.wait_ge(s.qbd_ready, 1)
                    pe.wait_ge(s.e_ready, 2 * PT * HEADS)
                    pe.wait_ge(s.pv_copied, PT * HEADS)
                    for g in range(2):
                        if g:
                            pe.wait_ge(s.sp_copied, g)
                        for j in range(4):
                            b = 4 * g + j
                            for pg in range(PAGES):
                                n = PAGES * b + pg
                                pe.wait_ge(s.page[n % 2], 16 * (n // 2 + 1))
                                pe.wait_ge(s.tok_copied, TOK["page"] + n - 1)
                                for hd in range(HEADS):
                                    mm = pe.transpose(M[:, 2 + n % 2, hd * P:(hd + 1) * P], d_kr[:, n % 2, hd, :], ident[:, :])
                                mm.then_inc(s.tok_ps, 1)
                            pe.wait_ge(s.tok_copied, TOK["page"] + PAGES * (b + 1))
                            rows = slice(32 * j, 32 * (j + 1))
                            for hd in range(HEADS):
                                q = d_qbd[:, b, hd, :, :].rearrange("p x y -> p (x y)")
                                pe.matmul(M[rows, 0, 0:2 * PAGE], q, d_KT[:, hd, :], start=(hd == 0), stop=False,
                                          skip_group_check=True)
                                pe.matmul(M[rows, 0, 2 * PAGE:2 * PAGE + NS], q, A[:, 4 + hd, SEQ:T], start=False, stop=False,
                                          skip_group_check=True)
                            mm = pe.matmul(M[rows, 0, 2 * PAGE:2 * PAGE + NS], ident[:, 32 * j:32 * (j + 1)], sneg[:, g, :],
                                           start=False, stop=True, skip_group_check=True)
                            mm.then_inc(s.ss_ps, 1)
                        pe.wait_ge(s.ss_w, g + 1)
                        for pg in range(PAGES):
                            pe.transpose(M[:, 1, pg * P:(pg + 1) * P], d_es[:, pg * P:(pg + 1) * P], ident[:, :])
                        pe.transpose(M[0:NS, 1, 2 * P:3 * P], d_es[:, 2 * P:2 * P + NS], ident[:, :]).then_inc(s.st_ps, 1)
                        pe.wait_ge(s.st_red, g + 1)
                        base = 2 * PAGE + NS
                        for hd in range(HEADS):
                            pe.matmul(M[:, 0, base + 16 * hd:base + 16 * (hd + 1)], dv[0:NS, PT, hd, :], d_wTn[:, :, hd, :],
                                      start=(hd == 0), stop=False, skip_group_check=True)
                        for j in range(4):
                            for pg in range(PAGES):
                                n = PAGES * (4 * g + j) + pg
                                pe.wait_ge(s.vpage[n % 4], 16 * (n // 4 + 1))
                                for hd in range(HEADS):
                                    c0 = base + 16 * hd + DEC_SEQ * j
                                    mm = pe.matmul(M[:, 0, c0:c0 + DEC_SEQ], d_V[:, n % 4, hd * DV:(hd + 1) * DV],
                                                   d_wTs[:, pg, j, hd, :], start=False, stop=(j == 3 and pg == 1),
                                                   skip_group_check=True)
                                mm.then_inc(s.v_used, 1)
                        pe.matmul(M[0:1, 1, 500:502], ones[:, 0:1], ones[:, 0:2], start=True, stop=True).then_inc(s.sp_ps, 1)
                    branch_pe(pe, 2)

                def merge_act(act, b):
                    base = CHUNK[f"merge{b}"]
                    with act.Fori(0, 4) as i:
                        for j in range(4):
                            n = base + j
                            kb = KD if j % 2 == 0 else HEADS
                            act.wait_ge(s.w_in[n % RAW], w_count(n, i, 4))
                            act.wait_ge(s.chunk_done, n + 4 * i - (SPLIT - 1))
                            act.activation(wH[n % SPLIT][:, 0:kb, :], raw[n % RAW][:, 0:kb, :], ACT.Copy).then_inc(s.wh_split, 1)
                            if j % 2:
                                u = j // 2
                                act.wait_ge(s.u_lin, 8 * b + 2 * i + u + 1)
                                act.activation(u_g[:, u, :], u_g[:, u, :], ACT.Sigmoid).then_inc(s.u_sig, 1)

                def merge_dve(dve, b):
                    out = OUT[f"merge{b}"]
                    for m in range(KD):
                        u, n = m % 2, KD * b + m
                        dve.wait_ge(s.chunk_done, CHUNK[f"merge{b}"] + 2 * m + 1)
                        if n >= 2:
                            dve.wait_ge(s.u_mul, n - 1)
                        dve.tensor_tensor(halves(u_g[:, u, :]), out2((out + 2 * m) % 2), halves(rB[:, :]), ALU.mult
                                          ).then_inc(s.u_lin, 1)
                        dve.wait_ge(s.u_lin, n + 1)
                        dve.sem_inc(s.out_taken, 1)
                        dve.wait_ge(s.chunk_done, CHUNK[f"merge{b}"] + 2 * m + 2)
                        dve.wait_ge(s.u_sig, n + 1)
                        if b == 0:
                            dve.tensor_tensor(halves(MG[:, m, :]), out2((out + 2 * m + 1) % 2), halves(u_g[:, u, :]), ALU.mult
                                              ).then_inc(s.u_mul, 1)
                            dve.wait_ge(s.u_mul, n + 1)
                            dve.sem_inc(s.out_taken, 1)
                        else:
                            dve.tensor_tensor(halves(u_p[:, :]), out2((out + 2 * m + 1) % 2), halves(u_g[:, u, :]), ALU.mult
                                              ).then_inc(s.u_mul, 1)
                            dve.wait_ge(s.u_mul, n + 1)
                            dve.sem_inc(s.out_taken, 1)
                            if b == 2 and m:
                                dve.wait_ge(s.mg_ready, 8 + m)
                            elif m or b > 1:
                                dve.wait_ge(s.mg_ready, KD * (b - 1) + m)
                            dve.tensor_tensor(MG[:, m, :], MG[:, m, :], u_p[:, :], ALU.add).then_inc(s.mg_ready, 1)
                            dve.wait_ge(s.mg_ready, KD * (b - 1) + m + 1)

                def merged_act(act):
                    act.wait_ge(s.chunk_done, CHUNK["merge2"])
                    for m in range(KD):
                        act.wait_ge(s.mg_ready, KD + m + 1)
                        act.activation(mH[:, m, :], MG[:, m, :], ACT.Copy).then_inc(s.mh_ready, 1)

                def merged_dve(dve):
                    for m in range(KD):
                        dve.wait_ge(s.mh_ready, m + 1)
                        dve.tensor_tensor(mL[:, m, :], MG[:, m, :], mH[:, m, :].bitcast(F32), ALU.subtract).then_inc(s.ml_split, 1)

                def add_to_h(dve, name, sem, per=1):
                    for m in range(KD):
                        dve.wait_ge(s.chunk_done, CHUNK[name] + per * (m + 1))
                        dve.tensor_tensor(halves(h[:, m, :]), out2((OUT[name] + m) % 2), halves(h[:, m, :]), ALU.add).then_inc(sem, 1)
                        dve.wait_ge(sem, m + 1)
                        dve.sem_inc(s.out_taken, 1)

                def embed_pe(pe):
                    pe.wait_ge(s.ptok_in, 32)
                    pe.wait_ge(s.bn_ln, 12)
                    for m in range(KP):
                        for i, n in enumerate(TILES):
                            mm = pe.transpose(M[:, 2 * m + i // PT, (i % PT) * P:(i % PT) * P + n],
                                              p_tok[0:n, i, m * P:(m + 1) * P], ident[0:n, 0:n])
                    mm.then_inc(s.p_ps, 1)

                def embed_act(act):
                    act.wait_ge(s.p_copied, 1)
                    act.activation(pH[:, :, :], p_raw[:, :, :], ACT.Copy).then_inc(s.ph_ready, 1)

                def embed_dve(dve, step):
                    dve.wait_ge(s.p_ps, 1)
                    for m in range(KP):
                        step(dve.tensor_copy(p_raw[:, m, 0:SEQ], M[:, 2 * m, :]))
                        step(dve.tensor_copy(p_raw[:, m, SEQ:T], M[:, 2 * m + 1, 0:NS]))
                    dve.sem_inc(s.p_copied, 1)
                    dve.wait_ge(s.ph_ready, 1)
                    dve.tensor_tensor(pL[:, :, :], p_raw[:, :, :], pH[:, :, :].bitcast(F32), ALU.subtract).then_inc(s.pl_ready, 1)

                def ffn_act(act):
                    base = CHUNK["ffn"]

                    def turn(i):
                        for j in range(4):
                            n = base + j
                            act.wait_ge(s.w_in[n % RAW], w_count(n, i, 4))
                            act.wait_ge(s.chunk_done, n + 4 * i - (SPLIT - 1))
                            act.activation(wH[n % SPLIT][:, :, :], raw[n % RAW][:, :, :], ACT.Copy).then_inc(s.wh_split, 1)
                            if j % 2:
                                act.wait_ge(s.f_lin, 2 * i + j // 2 + 1)
                                act.activation(f_g[:, j // 2, :], f_g[:, j // 2, :], ACT.Silu).then_inc(s.f_silu, 1)

                    with act.Fori(0, KF // 2) as i:
                        turn(i)
                        for u in range(2):
                            act.wait_ge(s.f_hid, 2 * i + u + 1)
                            act.activation(hidH[:, bass.ds(2 * i + u, 1), :].rearrange("p o n -> p (o n)"), f_u[:, u, :],
                                           ACT.Copy).then_inc(s.fh_ready, 1)

                def ffn_dve(dve):
                    base, out = CHUNK["ffn"], OUT["ffn"]

                    def turn(i, first):
                        for u in range(2):
                            dve.wait_ge(s.chunk_done, base + 4 * i + 2 * u + 1)
                            dve.tensor_tensor(halves(f_g[:, u, :]), out2((out + 2 * u) % 2), halves(rB[:, :]), ALU.mult
                                              ).then_inc(s.f_lin, 1)
                            dve.wait_ge(s.f_lin, 2 * i + u + 1)
                            dve.sem_inc(s.out_taken, 1)
                            dve.wait_ge(s.chunk_done, base + 4 * i + 2 * u + 2)
                            dve.tensor_tensor(halves(f_u[:, u, :]), out2((out + 2 * u + 1) % 2), halves(rB[:, :]), ALU.mult
                                              ).then_inc(s.out_taken, 1)
                            dve.wait_ge(s.out_taken, out + 4 * i + 2 * u + 2)
                            dve.wait_ge(s.f_silu, 2 * i + u + 1)
                            dve.tensor_tensor(f_u[:, u, :], f_u[:, u, :], f_g[:, u, :], ALU.mult).then_inc(s.f_hid, 1)
                        for u in range(2):
                            dve.wait_ge(s.fh_ready, 2 * i + u + 1)
                            blk = bass.ds(2 * i + u, 1)
                            dve.tensor_tensor(hidL[:, blk, :].rearrange("p o n -> p (o n)"), f_u[:, u, :],
                                              hidH[:, blk, :].rearrange("p o n -> p (o n)").bitcast(F32),
                                              ALU.subtract).then_inc(s.fl_ready, 1)
                            dve.wait_ge(s.fl_ready, 2 * i + u + 1)

                    with dve.Fori(0, KF // 2) as i:
                        turn(i, False)

                def ple_act(act):
                    base = CHUNK["ple"]
                    with act.Fori(0, 4) as i:
                        for j in range(4):
                            n, kb = base + j, (KD if j % 2 == 0 else KP)
                            act.wait_ge(s.w_in[n % RAW], w_count(n, i, 4))
                            act.wait_ge(s.chunk_done, n + 4 * i - (SPLIT - 1))
                            act.activation(wH[n % SPLIT][:, 0:kb, :], raw[n % RAW][:, 0:kb, :], ACT.Copy).then_inc(s.wh_split, 1)
                            if j % 2:
                                act.wait_ge(s.e_lin, 2 * i + j // 2 + 1)
                                act.activation(e_g[:, :], e_g[:, :], ACT.Sigmoid).then_inc(s.e_sig, 1)

                def ple_dve(dve, step):
                    out = OUT["ple"]
                    for m in range(KD):
                        dve.wait_ge(s.chunk_done, CHUNK["ple"] + 2 * m + 1)
                        dve.tensor_tensor(halves(e_g[:, :]), out2(out % 2), halves(rB[:, :]), ALU.mult).then_inc(s.e_lin, 1)
                        dve.wait_ge(s.e_lin, m + 1)
                        dve.sem_inc(s.out_taken, 1)
                        dve.wait_ge(s.chunk_done, CHUNK["ple"] + 2 * m + 2)
                        dve.wait_ge(s.e_sig, m + 1)
                        step(dve.tensor_tensor(halves(e_p[:, :]), out2((out + 1) % 2), halves(e_g[:, :]), ALU.mult))
                        dve.sem_inc(s.out_taken, 1)
                        dve.tensor_tensor(h[:, m, :], h[:, m, :], e_p[:, :], ALU.add).then_inc(s.h_ple, 1)
                        dve.wait_ge(s.h_ple, m + 1)

                @block.scalar
                def _(act):
                    step = Steps(act, s.act_step)
                    act.wait_ge(s.par_in, 16 * 13)
                    norm_act(act, step, 0, sq0, gains[:, 0, :], None, 0)
                    high_loop(act, "gla", 12, lambda j: KD)
                    high_loop(act, "small", 1, lambda j: KD, per=1)
                    gla_act(act, step)
                    high_loop(act, "ml", 12, lambda j: KD)
                    mlstm_act(act, step)
                    high_loop(act, "df", 12, lambda j: KD)
                    attention_act(act, step)
                    embed_act(act)
                    for b in range(3):
                        merge_act(act, b)
                    merged_act(act)
                    high_loop(act, "out", 8, lambda j: KD)
                    norm_act(act, step, 1, sq1, gains[:, 1, :], s.h_mix, CHUNK["out"])
                    ffn_act(act)
                    high_loop(act, "down", 4 * KD, lambda j: DOWN_K[j % 4][1], per=8)
                    norm_act(act, step, 2, sq2, gains[:, 2, :], s.h_ffn, 0)
                    ple_act(act)

                @block.tensor
                def _(pe):
                    norm_pe(pe, 0, sq0)
                    product_loop(pe, "gla", 3, panel_plan("gla", KD, xH, xL))
                    product_loop(pe, "small", 1, panel_plan("small", KD, xH, xL, 1))
                    gla_pe(pe)
                    product_loop(pe, "ml", 3, panel_plan("ml", KD, xH, xL))
                    mlstm_pe(pe)
                    product_loop(pe, "df", 3, panel_plan("df", KD, xH, xL))
                    attention_pe(pe)
                    embed_pe(pe)
                    for b in range(3):
                        pe.wait_ge(s.bn_l, b + 1)
                        product_loop(pe, f"merge{b}", 4, unit_plan(f"merge{b}", KD, xH, xL, HEADS, oH[b], oL[b]))
                    pe.wait_ge(s.ml_split, KD)
                    product_loop(pe, "out", 2, panel_plan("out", KD, mH, mL))
                    norm_pe(pe, 1, sq1)
                    product_loop(pe, "ffn", KF // 2, unit_plan("ffn", KD, xH, xL, KD, xH, xL))
                    pe.wait_ge(s.fl_ready, KF)
                    product_loop(pe, "down", KD // 2,
                                 [(k0, kb, (OUT["down"] + j // 4) % 2, hidH, hidL, j % 4 == 0, j % 4 == 3, j // 4)
                                  for j, (k0, kb) in enumerate(DOWN_K * 2)])
                    norm_pe(pe, 2, sq2)
                    pe.wait_ge(s.pl_ready, 1)
                    product_loop(pe, "ple", 4, unit_plan("ple", KD, xH, xL, KP, pH, pL))

                @block.vector
                def _(dve):
                    step = Steps(dve, s.dve_step)
                    dve.wait_ge(s.par_in, 16 * 13)
                    norm_dve(dve, 0, gains[:, 0, :])
                    dve.wait_ge(s.r_ready, 1)
                    gla_dve(dve, step)
                    mlstm_dve(dve, step)
                    attention_dve(dve, step)
                    embed_dve(dve, step)
                    for b in range(3):
                        merge_dve(dve, b)
                    merged_dve(dve)
                    add_to_h(dve, "out", s.h_mix)
                    norm_dve(dve, 1, gains[:, 1, :])
                    dve.wait_ge(s.r_ready, 2)
                    ffn_dve(dve)
                    add_to_h(dve, "down", s.h_ffn, 4)
                    norm_dve(dve, 2, gains[:, 2, :])
                    dve.wait_ge(s.r_ready, 3)
                    ple_dve(dve, step)

            clear_all()

        with nc.Block() as block:

            @block.scalar
            def _(act):
                step = Steps(act, s.act_step)
                for k in range(KD):
                    if k >= 2:
                        act.wait_ge(s.sq_used, k - 1)
                    act.activation(sq0[:, k % 2, :], h[:, k, :], ACT.Square).then_inc(s.sq_ready, 1)
                norm_factor(act, step, 0)

            @block.vector
            def _(dve):
                dve.wait_ge(s.r_ready, 1)
                for k in range(KD):
                    dve.scalar_tensor_tensor(out=y_f[:, k, :], in0=h[:, k, :], scalar=gfin[:, k:k + 1], in1=rB[:, :],
                                             op0=ALU.mult, op1=ALU.mult).then_inc(s.y_ready, 1)
                for i, n in enumerate(TILES):
                    for half in range(2):
                        dve.wait_ge(s.y_ps, 2 * i + half + 1)
                        dve.tensor_copy(io_tok[0:n, i, half * 512:(half + 1) * 512], M[0:n, 2 * (i % 2) + half, :]).then_inc(s.io_copied, 1)

            @block.tensor
            def _(pe):
                norm_pe(pe, 0, sq0, split=False)
                pe.wait_ge(s.y_ready, KD)
                for i, n in enumerate(TILES):
                    for half in range(2):
                        if i >= 2:
                            pe.wait_ge(s.io_copied, 2 * (i - 2) + half + 1)
                        for k in range(4):
                            mm = pe.transpose(M[0:n, 2 * (i % 2) + half, k * P:(k + 1) * P], y_f[:, 4 * half + k, i * P:i * P + n],
                                              ident[:, :])
                        mm.then_inc(s.y_ps, 1)

            @block.sync
            def _(sp):
                for i, n in enumerate(TILES):
                    sp.wait_ge(s.io_copied, 2 * (i + 1))
                    dst = o["y_prompt"][0, i * P:(i + 1) * P, :] if n == P else o["y_sample"].rearrange("b t d -> (b t) d")
                    sp.dma_start(dst, io_tok[0:n, i, :]).then_inc(s.io_out, 16)
                sp.wait_ge(s.io_out, 16 * 5)


_INS = ["x_prompt", "x_sample", "cache_k", "cache_v", "state_gla", "state_mlstm_c", "state_mlstm_n", "state_mlstm_m",
        "page_table", "p_prompt", "p_sample", "g_mix", "w_in", "w_gla_gk", "b_gla_gk", "g_gla_norm", "b_mlstm_if",
        "g_mlstm_norm", "diff_lambda", "g_diff_norm", "w_branch", "w_gate", "w_out", "g_ffn", "w_ffn_gate", "w_ffn_up",
        "w_ffn_down", "g_ple", "w_ple_gate", "w_ple_proj", "g_final"]
_OUTS = [("y_prompt", (1, SEQ, D)), ("y_sample", (DEC_BATCH, DEC_SEQ, D)),
         ("k_prompt", (DEPTH, 1, SEQ, 2 * HEADS, DK)), ("v_prompt", (DEPTH, 1, SEQ, HEADS, DV)),
         ("gla_prompt", (DEPTH, 1, HEADS, DK, DV)), ("c_prompt", (DEPTH, 1, HEADS, DK, DV)),
         ("n_prompt", (DEPTH, 1, HEADS, DK)), ("m_prompt", (DEPTH, 1, HEADS)),
         ("k_sample", (DEPTH, DEC_BATCH, DEC_SEQ, 2 * HEADS, DK)), ("v_sample", (DEPTH, DEC_BATCH, DEC_SEQ, HEADS, DV)),
         ("gla_sample", (DEPTH, DEC_BATCH, HEADS, DK, DV)), ("c_sample", (DEPTH, DEC_BATCH, HEADS, DK, DV)),
         ("n_sample", (DEPTH, DEC_BATCH, HEADS, DK)), ("m_sample", (DEPTH, DEC_BATCH, HEADS))]


def constants():
    import math
    import numpy as np
    f = np.float32
    i = np.arange(P)
    k = {"ident": np.eye(P), "ones": np.ones((P, P)), "epsc": np.full((P, 1), EPS)}
    k["big"] = np.where(i[:, None] > i[None, :], BIG, 0.0)
    k["neg"] = np.where(i[None, :] > i[:, None], -BIG, 0.0)
    k["gmask"] = (i[:, None] // CH == i[None, :] // CH) & (i[:, None] <= i[None, :])
    n = np.arange(NS)
    seen = (n[:, None] // DEC_SEQ == n[None, :] // DEC_SEQ) & (n[:, None] <= n[None, :])
    k["smask"] = seen
    k["sbig"] = np.where(seen, 0.0, BIG)
    row_seq, row_t = i // NS, i % DEC_SEQ
    k["sneg"] = np.stack([np.where(seen[:, (4 * g + row_seq) * DEC_SEQ + row_t].T, 0.0, -BIG) for g in range(2)], 1)
    k["sel"] = np.repeat(np.eye(HEADS)[:, :, None], P, 2)
    k["selp"] = np.stack([(np.arange(HEADS)[:, None] == 2 * p + i[None, :] // DK) for p in range(2)], 1)
    k["seqm"] = (n[:, None] // DEC_SEQ == np.arange(DEC_BATCH)[None, :])
    k["sign"] = np.stack([(i // DEC_SEQ) % 2 == 0, (i // DEC_SEQ) % 2 == 1], 1)
    half = DK // 8
    rot = np.zeros((P, P))
    for h0 in (0, DK):
        for j in range(half):
            rot[h0 + half + j, h0 + j] = -1.0
            rot[h0 + j, h0 + half + j] = 1.0
    k["rot"] = rot
    pos = np.concatenate([np.arange(SEQ), PAGE * PAGES + n % DEC_SEQ]).astype(f)
    inv = f(500000.0) ** (-np.arange(half, dtype=f) * f(2.0) / f(2 * half))
    ang = (pos[:, None] * inv[None, :]).astype(f)
    cos, sin = np.ones((P, T), f), np.zeros((P, T), f)
    for h0 in (0, DK):
        for q in range(2):
            cos[h0 + half * q:h0 + half * (q + 1)] = np.cos(ang).T
            sin[h0 + half * q:h0 + half * (q + 1)] = np.sin(ang).T
    k["cos"], k["sin"] = cos, sin
    t = np.arange(SEQ)
    k["greset"] = np.repeat(np.concatenate([t % CH != 0, n % DEC_SEQ != 0])[None], P, 0)
    k["rreset"] = np.repeat(np.concatenate([t % P != 0, n % DEC_SEQ != 0])[None], HEADS, 0)
    init = [0.8 - 0.6 * math.exp(-0.3 * layer) for layer in range(DEPTH)]
    k["lamc"] = np.repeat(np.array([[x, 1.0 - x] for x in init])[:, None, :], P, 1)
    return {name: np.ascontiguousarray(v, dtype=f) for name, v in k.items()}


def kernel(**inputs):
    import numpy as _np
    import concourse.bacc as _bacc
    from concourse import mybir as _mybir
    from concourse.bass_utils import run_bass_kernel_spmd as _run

    nc = _bacc.Bacc("TRN2", target_bir_lowering=False, num_devices=1)
    arrays, args, consts, outs = {}, {}, {}, {}
    for name in _INS:
        x = _np.ascontiguousarray(inputs[name])
        arrays[f"in_{name}"] = x
        args[name] = nc.dram_tensor(f"in_{name}", x.shape, _mybir.dt.from_np(x.dtype), kind="ExternalInput").ap()
    for name, x in constants().items():
        arrays[f"const_{name}"] = x
        consts[name] = nc.dram_tensor(f"const_{name}", x.shape, _mybir.dt.from_np(x.dtype), kind="ExternalInput").ap()
    for name, shape in _OUTS:
        outs[name] = nc.dram_tensor(f"out_{name}", shape, F32, kind="ExternalOutput").ap()
    program(nc, args, consts, outs)
    r = _run(nc, [arrays], core_ids=[0])
    return tuple(r.results[0][f"out_{name}"] for name, _ in _OUTS)
```

```python
from contextlib import ExitStack

import concourse.bass as bass
from concourse import mybir

F32 = mybir.dt.float32
F32R = mybir.dt.float32r
I32 = mybir.dt.int32
ALU = mybir.AluOpType
ACT = mybir.ActivationFunctionType
AX = mybir.AxisListType

P = 128
D = 1024
KD = D // P
SEQ, DEC_BATCH, DEC_SEQ = 512, 8, 4
NS = DEC_BATCH * DEC_SEQ
T = SEQ + NS
HALF = T // 2
PT = SEQ // P
TILES = [P] * PT + [NS]
DEPTH = 2
PAGE, PAGES = 128, 2
HEADS, DK, DV = 4, 64, 128
CH = 64
NCH = SEQ // CH
DFF = 2816
KF = DFF // P
PLE = 256
KP = PLE // P
RANK = 16
EPS = 1e-6
BIG = 1e30
COL_GLA, COL_LR, COL_ML, COL_IF, COL_DF = 0, 1536, 1552, 3088, 3096
RAW, SPLIT = 4, 2
KMAX = 8
DOWN_K = [(0, 6), (6, 6), (12, 5), (17, 5)]


class Steps:

    def __init__(self, eng, sem):
        self.eng, self.sem, self.n = eng, sem, 0

    def __call__(self, ins):
        ins.then_inc(self.sem, 1)
        self.n = self.n + 1
        self.eng.wait_ge(self.sem, self.n)


class Between:

    def __init__(self, piece, total):
        self.piece, self.total, self.n = piece, total, 0

    def __call__(self, count=1):
        for _ in range(min(count, self.total - self.n)):
            self.piece(self.n)
            self.n = self.n + 1

    def rest(self):
        self(self.total - self.n)


def halves(ap):
    return ap.rearrange("p (h n) -> p h n", h=2)


def program(nc, a, c, o):
    ctx = ExitStack()
    with ctx:
        ctx.enter_context(nc.allow_non_contiguous_dma(reason="gains and states' columns, a few kilobytes"))
        arena_size = (nc.sbuf_usable_end - nc.sbuf_base - 64) // 64 * 64
        arena = ctx.enter_context(nc.sbuf_tensor("arena", [P, arena_size // 4], F32, align_bytes=64))
        start = nc.sbuf_base - arena_size
        assert start >= 0

        class Area:

            def __init__(self, at, size):
                self.at, self.size, self.used = at, size, 0

            def put(self, name, shape, dt=F32):
                n = 4
                for s in shape[1:]:
                    n *= s
                n = (n + 31) // 32 * 32
                assert self.used + n <= self.size, (name, self.used + n, self.size)
                t = nc.alloc_sbuf_tensor_at(name, shape, dt, offset=self.at + self.used)
                self.used += n
                return t

            def again(self, skip=0):
                return Area(self.at + skip, self.size - skip)

        whole = Area(start, arena_size)

        def area(size):
            r = Area(whole.at + whole.used, size)
            whole.used += size
            assert whole.used <= whole.size, (whole.used, whole.size)
            return r

        BLK = T * 4
        fixed = area(10368)
        ident = fixed.put("ident", [P, P])
        ones = fixed.put("ones", [P, P])
        rot = fixed.put("rot", [P, P])
        big = fixed.put("big", [P, P])
        neg = fixed.put("neg", [P, P])
        gmask = fixed.put("gmask", [P, P])
        smask = fixed.put("smask", [NS, NS])
        sbig = fixed.put("sbig", [NS, NS])
        sneg = fixed.put("sneg", [P, 2, NS])
        sel = fixed.put("sel", [HEADS, HEADS, P])
        selp = fixed.put("selp", [HEADS, 2, P])
        seqm = fixed.put("seqm", [NS, DEC_BATCH])
        sign = fixed.put("sign", [P, 2])
        epsc = fixed.put("epsc", [P, 1])
        gains = fixed.put("gains", [P, 3, KD])
        gfin = fixed.put("gfin", [P, KD])
        ghead = fixed.put("ghead", [P, 3])
        bgk = fixed.put("bgk", [P, 2])
        bif = fixed.put("bif", [P, 1])
        wgk = fixed.put("wgk", [RANK, HEADS * DK])
        lamv = fixed.put("lamv", [P, 4, DK])
        lamp = fixed.put("lamp", [P, DK])
        lam = fixed.put("lam", [P, 8])
        lamc = fixed.put("lamc", [P, 2])
        m_in = fixed.put("m_in", [HEADS, DEC_BATCH])
        g_dec = fixed.put("g_dec", [P, 2, NCH + DEC_BATCH])
        pages = fixed.put("pages", [1, DEC_BATCH * PAGES], I32)

        rB = area(BLK).put("rB", [P, T])
        a_H = area(KD * BLK)
        h = a_H.again().put("h", [P, KD, T])
        xs = area(2 * KD * BLK)
        xH, xL = xs.put("xH", [P, KD, T], F32R), xs.put("xL", [P, KD, T], F32R)
        ws = area((RAW + 2 * SPLIT) * KMAX * P * 4)
        raw = [ws.put(f"raw{i}", [P, KMAX, P]) for i in range(RAW)]
        wH = [ws.put(f"wH{i}", [P, KMAX, P], F32R) for i in range(SPLIT)]
        wL = [ws.put(f"wL{i}", [P, KMAX, P], F32R) for i in range(SPLIT)]
        a_oA, a_oM, a_A, a_B, a_MG = (area(8 * BLK) for _ in range(5))
        a_VA = area(5 * 4 * DV * 4)
        a_VM = area(10336)
        a_T = area(whole.size - whole.used)
        hid_area = Area(a_oA.at, 5 * 8 * BLK + a_VA.size)
        tail = Area(a_VM.at, a_VM.size + a_T.size)

        oH, oL, oraw, rO = [], [], [], []
        for n, ar in zip(("g", "m", "d"), (a_oA, a_oM, a_A)):
            oH.append(ar.again().put(f"oH_{n}", [P, HEADS, T], F32R))
            oL.append(ar.again(4 * BLK).put(f"oL_{n}", [P, HEADS, T], F32R))
            rO.append(ar.again().put(f"rO_{n}", [P, HEADS, T]))
            oraw.append(ar.again(4 * BLK).put(f"oraw_{n}", [P, HEADS, T]))
        A = a_A.again().put("A", [P, 8, T])
        B = a_H.again().put("B", [P, 8, T])
        C = a_B.again().put("C", [P, 8, T])
        MG = a_H.again().put("MG", [P, 8, T])
        gvf = a_MG.again().put("gvf", [P, 4, T])
        mvf = a_oA.again().put("mvf", [P, 4, T])
        dvf = a_MG.again(4 * BLK).put("dvf", [P, 4, T])
        gv = a_VA.again().put("gv", [P, 5, HEADS, DV])
        dv = a_VA.again().put("dv", [P, 5, HEADS, DV])
        mv = a_VM.again().put("mv", [P, 5, HEADS, DV + 1])
        small = a_T.put("small", [P, T])
        tmp_at = a_T.used
        sq0 = a_T.again(tmp_at).put("sq0", [P, 2, T])

        t = a_oM.again()
        g_b, g_E, g_kg = (t.put(n, [P, 2, T]) for n in ("g_b", "g_E", "g_kg"))
        g_az, g_reset = t.put("g_az", [P, T]), t.put("g_reset", [P, T])
        t = a_B.again()
        g_S, g_Sin = t.put("g_S", [P, NCH, 2, DV]), t.put("g_Sin", [P, DEC_BATCH, 2, DV])
        t = a_VM.again()
        g_kdT, g_A = t.put("g_kdT", [P, 5, HEADS * DK]), t.put("g_A", [P, 2, HEADS, P])
        g_As = t.put("g_As", [NS, HEADS, NS])
        g_qz = a_MG.again().put("g_qz", [P, HEADS, T])
        g_kdm = a_MG.again(4 * BLK).put("g_kdm", [NS, DEC_BATCH, HEADS * DK])
        t = a_A.again()
        r_a, r_m, r_en, r_F, r_d, r_g, r_wi, r_reset = (
            t.put(n, [HEADS, T]) for n in ("r_a", "r_m", "r_en", "r_F", "r_d", "r_g", "r_wi", "r_reset"))
        t = a_MG.again(4 * BLK)
        m_qwz = t.put("m_qwz", [P, HEADS, T])
        m_qz = a_oM.again().put("m_qz", [P, HEADS, T])
        t = a_H.again()
        m_qns, m_den = t.put("m_qns", [P, HEADS, NS]), t.put("m_den", [P, HEADS])
        m_Cin = a_MG.again().put("m_Cin", [P, DEC_BATCH, 2, DV + 1])
        t = a_VA.again()
        m_kT, m_kw = t.put("m_kT", [P, 5, HEADS, DK]), t.put("m_kw", [P, 5, HEADS, DK])
        m_kwm = a_oM.again().put("m_kwm", [NS, DEC_BATCH, HEADS * DK])
        t = a_T.again(tmp_at)
        m_D, m_C = t.put("m_D", [P, HEADS * P]), t.put("m_C", [P, 2, 2, DV + 1])
        t = a_MG.again(DEC_BATCH * 2 * (DV + 1) * 4)
        m_dec, m_cols = t.put("m_dec", [P, 2, 12]), t.put("m_cols", [P, 5, 12])
        m_prev = t.put("m_prev", [HEADS, 12])
        m_SD = a_A.again(3 * BLK).put("m_SD", [P, HEADS * P])
        m_ad = a_A.again(7 * BLK).put("m_ad", [P, HEADS * P])
        m_tok = a_A.again(7 * BLK).put("m_tok", [P, HEADS, DV])
        t = a_VM.again()
        d_e, d_w, d_wT = t.put("d_e", [P, 2, SEQ]), t.put("d_w", [P, SEQ]), t.put("d_wT", [P, SEQ])
        d_kout = t.put("d_kout", [P, 8 * DK])
        t = a_T.again()
        d_cos, d_sin = t.put("d_cos", [P, T]), t.put("d_sin", [P, T])
        d_t1 = t.put("d_t1", [P, T])
        t = a_T.again()
        d_qbd = t.put("d_qbd", [P, DEC_BATCH, HEADS, 2, DEC_SEQ * HEADS])
        d_es = t.put("d_es", [P, 2 * PAGE + NS])
        d_wTs, d_wTn = t.put("d_wTs", [P, PAGES, 4, HEADS, DEC_SEQ]), t.put("d_wTn", [NS, 4, HEADS, DEC_SEQ])
        d_nm, d_l, d_rc = t.put("d_nm", [P, 2]), t.put("d_l", [P, 2]), t.put("d_rc", [P, 2])
        t = a_MG.again()
        d_V = t.put("d_V", [P, 2, HEADS * DV])
        d_kr = t.put("d_kr", [P, 2, HEADS, P])
        d_KT = t.put("d_KT", [P, HEADS, PAGES * PAGE])
        u_g = t.put("u_g", [P, 2, T])
        mH = a_oA.again().put("mH", [P, KD, T], F32R)
        mL = a_oM.again().put("mL", [P, KD, T], F32R)
        sq1 = a_T.again().put("sq1", [P, 2, T])
        p_tok = a_B.again().put("p_tok", [P, 5, PLE])
        t = tail.again()
        pH, pL = t.put("pH", [P, KP, T], F32R), t.put("pL", [P, KP, T], F32R)
        p_raw = a_B.again(5120).put("p_raw", [P, KP, T])
        f_g, f_u = t.put("f_g", [P, 2, T]), t.put("f_u", [P, 2, T])
        t2 = hid_area.again()
        hidH, hidL = t2.put("hidH", [P, KF, T], F32R), t2.put("hidL", [P, KF, T], F32R)
        t = tail.again(4 * BLK)
        sq2 = t.put("sq2", [P, 2, T])
        e_g = t.put("e_g", [P, 2, T])
        e_p = hid_area.again().put("e_p", [P, KD, T])
        io_tok = hid_area.again().put("io_tok", [P, 5, D])
        y_f = hid_area.again(5 * D * 4).put("y_f", [P, KD, T])

        spill = o["spill"]
        G = ctx.enter_context(nc.psum_tensor("G", [P, 2, 2, 512], F32))
        M = ctx.enter_context(nc.psum_tensor("M", [P, 4, 512], F32))

        def out2(slot):
            return G[:, slot, :, 0:HALF]

        M01 = M[:, 0:2, 0:HALF]
        M23 = M[:, 2:4, 0:HALF]

        class Semaphores:
            pass

        s, sems = Semaphores(), []

        def signals(names):
            new = [ctx.enter_context(nc.semaphore(n)) for n in names.split()]
            sems.extend(new)
            return new

        s.const_in, s.io_in, s.io_turned, s.io_copied, s.io_out = signals(
            "const_in io_in io_turned io_copied io_out")
        s.par_in, s.greset_in, s.rreset_in, s.trig_in, s.gst_in, s.mst_in = signals(
            "par_in greset_in rreset_in trig_in gst_in mst_in")
        s.mn_in, s.ptok_in = signals(
            "mn_in ptok_in")
        s.w_in0, s.w_in1, s.w_in2, s.w_in3, s.wh_split, s.wl_split = signals(
            "w_in0 w_in1 w_in2 w_in3 wh_split wl_split")
        s.chunk_done, s.out_taken = signals(
            "chunk_done out_taken")
        s.xh_ready, s.xl_ready, s.sq_ready, s.sq_used, s.stat_ps, s.r_ready = signals(
            "xh_ready xl_ready sq_ready sq_used stat_ps r_ready")
        s.h_mix, s.h_ffn, s.h_ple = signals(
            "h_mix h_ffn h_ple")
        s.tok_ps, s.tok_copied, s.vstore, s.kstore = signals(
            "tok_ps tok_copied vstore kstore")
        s.gz_ps, s.gz_abs, s.gz_ln, s.gz_min, s.g_b_ready, s.g_e = signals(
            "gz_ps gz_abs gz_ln gz_min g_b_ready g_e")
        s.g_qg, s.g_kg, s.g_kd, s.g_at_ps, s.g_at, s.g_ds_ps = signals(
            "g_qg g_kg g_kd g_at_ps g_at g_ds_ps")
        s.g_s, s.g_o_ps, s.g_o, s.g_kdm_ready = signals(
            "g_s g_o_ps g_o g_kdm_ready")
        s.gstore, s.mstore, s.nstore = signals(
            "gstore mstore nstore")
        s.bn_sq, s.bn_ps, s.bn_ln, s.bn_r, s.bn_gate, s.bn_o = signals(
            "bn_sq bn_ps bn_ln bn_r bn_gate bn_o")
        s.bn_h, s.bn_l = signals(
            "bn_h bn_l")
        s.ml_ab, s.ml_ln, s.ml_f, s.ml_rows, s.ml_ex, s.ml_col_ps = signals(
            "ml_ab ml_ln ml_f ml_rows ml_ex ml_col_ps")
        s.ml_col, s.ml_wi_ps, s.ml_wi, s.ml_kw, s.ml_d_ps, s.ml_d = signals(
            "ml_col ml_wi_ps ml_wi ml_kw ml_d_ps ml_d")
        s.ml_s_ps, s.ml_sd, s.ml_e_ps = signals(
            "ml_s_ps ml_sd ml_e_ps")
        s.ml_n_ps, s.ml_den_ps, s.ml_ad, s.ml_o, s.ml_c_ps, s.ml_c = signals(
            "ml_n_ps ml_den_ps ml_ad ml_o ml_c_ps ml_c")
        s.ml_qn, s.ml_kwm_ready = signals(
            "ml_qn ml_kwm_ready")
        s.rope_ps, s.rope_done, s.lam_sum, s.lam_exp, s.lam_ready = signals(
            "rope_ps rope_done lam_sum lam_exp lam_ready")
        s.sc_ps, s.nm_ready, s.e_ready, s.w_ready, s.wt_ps, s.wt_copied = signals(
            "sc_ps nm_ready e_ready w_ready wt_ps wt_copied")
        s.pv_ps, s.pv_copied = signals(
            "pv_ps pv_copied")
        s.page0, s.page1, s.vpage0, s.vpage1, s.vpage2, s.vpage3 = signals(
            "page0 page1 vpage0 vpage1 vpage2 vpage3")
        s.v_used, s.kt_copied, s.qbd_ready, s.ss_ps, s.ss_nm, s.ss_e = signals(
            "v_used kt_copied qbd_ready ss_ps ss_nm ss_e")
        s.ss_w, s.st_ps, s.st_red, s.sp_ps, s.sp_copied = signals(
            "ss_w st_ps st_red sp_ps sp_copied")
        s.first_done, s.proj_done, s.proj_taken = signals("first_done proj_done proj_taken")
        s.ml_tok, s.ml_t_ps = signals("ml_tok ml_t_ps")
        s.e_mul, s.spilled, s.h_back, s.gain_in = signals("e_mul spilled h_back gain_in")
        s.u_lin, s.u_sig, s.u_mul, s.mg_ready, s.mh_ready, s.ml_split = signals(
            "u_lin u_sig u_mul mg_ready mh_ready ml_split")
        s.p_ps, s.p_copied, s.ph_ready, s.pl_ready = signals(
            "p_ps p_copied ph_ready pl_ready")
        s.f_lin, s.f_silu, s.f_hid, s.fh_ready, s.fl_ready, s.e_lin = signals(
            "f_lin f_silu f_hid fh_ready fl_ready e_lin")
        [s.e_sig] = signals("e_sig")
        s.act_step, s.dve_step, s.y_ps, s.y_ready = signals(
            "act_step dve_step y_ps y_ready")
        s.w_in = [s.w_in0, s.w_in1, s.w_in2, s.w_in3]
        s.page = [s.page0, s.page1]
        s.vpage = [s.vpage0, s.vpage1, s.vpage2, s.vpage3]

        def clear_all():
            nc.all_engine_barrier()
            numbers = [x.num for x in sems]
            assert max(numbers) - min(numbers) + 1 == len(numbers)
            nc.sync.sem_clear(range(min(numbers), max(numbers) + 1))
            nc.all_engine_barrier()

        with nc.Block() as block:

            @block.sync
            def _(sp):
                for dst, src in ((ident, "ident"), (ones, "ones"), (rot, "rot"), (big, "big"), (neg, "neg"),
                                 (gmask, "gmask"), (smask, "smask"), (sbig, "sbig"), (sneg, "sneg"), (sel, "sel"),
                                 (selp, "selp"), (seqm, "seqm"), (sign, "sign"), (epsc, "epsc")):
                    sp.dma_start(dst[:], c[src]).then_inc(s.const_in, 16)
                sp.dma_start(gfin[:, :], a["g_final"].rearrange("(k p) -> p k", p=P)).then_inc(s.const_in, 16)
                sp.dma_start(pages[:, :], a["page_table"].rearrange("(o b) n -> o (b n)", o=1)).then_inc(s.const_in, 16)
                sp.dma_start(io_tok[:, 0:PT, :],
                             a["x_prompt"].rearrange("a (i p) d -> p (a i) d", p=P)).then_inc(s.io_in, 16)
                sp.dma_start(io_tok[0:NS, PT, :], a["x_sample"].rearrange("b t d -> (b t) d")).then_inc(s.io_in, 16)

            @block.tensor
            def _(pe):
                pe.wait_ge(s.const_in, 16 * 16)
                pe.wait_ge(s.io_in, 32)
                for k in range(KD):
                    if k >= 2:
                        pe.wait_ge(s.io_copied, 2 * (k - 1))
                    for i, n in enumerate(TILES):
                        bank, col = (2 * (k % 2) + i // PT, (i % PT) * P)
                        pe.transpose(M[:, bank, col:col + n], io_tok[0:n, i, k * P:(k + 1) * P],
                                     ident[0:n, 0:n]).then_inc(s.io_turned, 1)

            @block.vector
            def _(dve):
                for k in range(KD):
                    dve.wait_ge(s.io_turned, 5 * (k + 1))
                    dve.tensor_copy(h[:, k, 0:SEQ], M[:, 2 * (k % 2), :]).then_inc(s.io_copied, 1)
                    dve.tensor_copy(h[:, k, SEQ:T], M[:, 2 * (k % 2) + 1, 0:NS]).then_inc(s.io_copied, 1)

        clear_all()

        CHUNK, OUT, cc, oo = {}, {}, 0, 0
        for name, chunks, outs in (("gla", 12, 12), ("small", 1, 1), ("ml", 12, 12), ("df", 12, 12),
                                   ("merge0", 12, 16), ("merge1", 12, 16), ("merge2", 12, 16), ("out", 8, 8),
                                   ("ffn", 2 * KF, 2 * KF), ("down", 4 * KD, KD), ("ple", 10, 16)):
            CHUNK[name], OUT[name] = cc, oo
            cc, oo = cc + chunks, oo + outs
        TOK = {"gv": 0, "kd": 5, "mv": 10, "mk": 15, "dv": 20, "dk": 25, "page": 30}

        def load_chunk(sp, n, view, src):
            if n >= RAW:
                sp.wait_ge(s.wl_split, n - (RAW - 1))
            sp.dma_start(view(raw[n % RAW]), src).then_inc(s.w_in[n % RAW], 16)

        def high_chunk(act, n, kb=KD):
            act.wait_ge(s.w_in[n % RAW], w_count(n, 0, 4))
            if n >= SPLIT:
                act.wait_ge(s.chunk_done, n - (SPLIT - 1))
            act.activation(wH[n % SPLIT][:, 0:kb, :], raw[n % RAW][:, 0:kb, :], ACT.Copy).then_inc(s.wh_split, 1)

        def low_chunk(pool, n, kb=KD):
            pool.wait_ge(s.wh_split, n + 1)
            pool.tensor_tensor(wL[n % SPLIT][:, 0:kb, :], raw[n % RAW][:, 0:kb, :], wH[n % SPLIT][:, 0:kb, :].bitcast(F32),
                               ALU.subtract).then_inc(s.wl_split, 1)

        def both_loop(pool, name, count=12, per=4):
            base = CHUNK[name]
            with pool.Fori(0, count // per) as i:
                for j in range(per):
                    n = base + j
                    pool.wait_ge(s.w_in[n % RAW], w_count(n, i, per))
                    pool.wait_ge(s.chunk_done, n + per * i - (SPLIT - 1))
                    pool.tensor_tensor(wH[n % SPLIT][:, :, :], raw[n % RAW][:, :, :],
                                       ones[:, 0:1].unsqueeze(1).to_broadcast([P, KD, P]), ALU.mult).then_inc(s.wh_split, 1)
                    pool.wait_ge(s.wh_split, n + 1 + per * i)
                    pool.tensor_tensor(wL[n % SPLIT][:, :, :], raw[n % RAW][:, :, :], wH[n % SPLIT][:, :, :].bitcast(F32),
                                       ALU.subtract).then_inc(s.wl_split, 1)

        def w_count(slot_chunk, i, per):
            slot = slot_chunk % RAW
            more = 48 if slot == CHUNK["small"] % RAW and slot_chunk >= CHUNK["small"] else 0
            return 16 * (slot_chunk // RAW + 1) + more + 16 * (per // RAW) * i

        def load_loop(sp, name, count, kb, source, per=4, first=0):
            base = CHUNK[name]

            def turn(i, start):
                for j in range(per):
                    n = base + j + per * i
                    if start + j >= RAW:
                        sp.wait_ge(s.wl_split, n - (RAW - 1))
                    k = kb(j)
                    sp.dma_start(raw[(base + j) % RAW][:, 0:k, :], source(i, j)).then_inc(s.w_in[(base + j) % RAW], 16)

            with sp.Fori(1 if base < RAW else 0, count // per) as i:
                turn(i, RAW)

        def high_loop(act, name, count, per=4):
            base = CHUNK[name]
            for n in range(base + SPLIT, base + per):
                high_chunk(act, n)
            with act.Fori(1, count // per) as i:
                for j in range(per):
                    n = base + j
                    act.wait_ge(s.w_in[n % RAW], w_count(n, i, per))
                    act.wait_ge(s.chunk_done, n + per * i - (SPLIT - 1))
                    act.activation(wH[n % SPLIT][:, :, :], raw[n % RAW][:, :, :], ACT.Copy).then_inc(s.wh_split, 1)

        def low_loop(pool, name, count, kb, per=4):
            base = CHUNK[name]
            with pool.Fori(0, count // per) as i:
                for j in range(per):
                    n = base + j
                    pool.wait_ge(s.wh_split, n + 1 + per * i)
                    pool.tensor_tensor(wL[n % SPLIT][:, 0:kb(j), :], raw[n % RAW][:, 0:kb(j), :],
                                       wH[n % SPLIT][:, 0:kb(j), :].bitcast(F32), ALU.subtract).then_inc(s.wl_split, 1)

        def blocks_product(pe, n, slot, hi, lo, blocks, start, stop):
            for at, (wk, xk) in enumerate(blocks):
                for w, x in ((wH, hi), (wH, lo), (wL, hi)):
                    for half in range(2):
                        mm = pe.matmul(G[:, slot, half, 0:HALF], w[n % SPLIT][:, wk, :],
                                       x[:, xk, half * HALF:(half + 1) * HALF],
                                       start=(start and at == 0 and w is wH and x is hi),
                                       stop=(stop and at == len(blocks) - 1 and w is wL))
            return mm

        def panel_chunk(pe, n, out, hi, lo, i=0, per=0, before=None):
            pe.wait_ge(s.wl_split, n + 1 + per * i)
            if out >= 2 or per:
                pe.wait_ge(s.out_taken, out - 1 + per * i)
            blocks = [(k, k) for k in range(KD)]
            if before is None:
                mm = blocks_product(pe, n, out % 2, hi, lo, blocks, True, True)
            else:
                for k in range(KD):
                    before(k)
                    mm = blocks_product(pe, n, out % 2, hi, lo, blocks[k:k + 1], k == 0, k == KD - 1)
            mm.then_inc(s.chunk_done, 1)

        def panel_piece(pe, name, at):
            j, part = at // 4, at % 4
            n, out = CHUNK[name] + j, OUT[name] + j
            if part == 0:
                pe.wait_ge(s.wl_split, n + 1)
                pe.wait_ge(s.out_taken, out - 1)
            mm = blocks_product(pe, n, out % 2, xH, xL, [(2 * part, 2 * part), (2 * part + 1, 2 * part + 1)],
                                part == 0, part == 3)
            if part == 3:
                mm.then_inc(s.chunk_done, 1)

        def panel_loop(pe, name, count, hi, lo, first=0, per=4):
            base, out = CHUNK[name], OUT[name]
            for j in range(first, per if first else 0):
                panel_chunk(pe, base + j, out + j, hi, lo)
            with pe.Fori(1 if first else 0, count // per) as i:
                for j in range(per):
                    panel_chunk(pe, base + j, out + j, hi, lo, i, per)

        def x_high(act, n, k, sq, gain, h_ready=None):
            if h_ready is not None:
                act.wait_ge(h_ready, k + 1)
            act.activation(xH[:, k, :], h[:, k, :], ACT.Copy, scale=gain[:, k:k + 1]).then_inc(s.xh_ready, 1)
            if KD * n + k >= 2:
                act.wait_ge(s.sq_used, KD * n + k - 1)
            act.activation(sq[:, k % 2, :], h[:, k, :], ACT.Square).then_inc(s.sq_ready, 1)

        def x_low(dve, n, k, gain):
            dve.wait_ge(s.xh_ready, KD * n + k + 1)
            dve.scalar_tensor_tensor(out=xL[:, k, :], in0=h[:, k, :], scalar=gain[:, k:k + 1],
                                     in1=xH[:, k, :].bitcast(F32), op0=ALU.mult,
                                     op1=ALU.subtract).then_inc(s.xl_ready, 1)

        def norm_factor(act, step, n):
            act.wait_ge(s.stat_ps, n + 1)
            step(act.activation(halves(rB[:, :]), M01, ACT.Ln, scale=1.0 / D, bias=epsc[:, 0:1]))
            act.activation(rB[:, :], rB[:, :], ACT.Exp, scale=-0.5).then_inc(s.r_ready, 1)

        def stat(pe, n, k, sq, ready=None, stop=None):
            pe.wait_ge(s.sq_ready, KD * n + k + 1 if ready is None else ready)
            for half in range(2):
                mm = pe.matmul(M[:, half, 0:HALF], ones[:, :], sq[:, k % 2, half * HALF:(half + 1) * HALF],
                               start=(k == 0), stop=(k == KD - 1), skip_group_check=True)
            mm.then_inc(s.sq_used, 1)

        def stats_done(pe, n):
            pe.wait_ge(s.sq_used, KD * (n + 1))
            pe.matmul(M[0:1, 2, 0:2], ones[:, 0:1], ones[:, 0:2], start=True, stop=True).then_inc(s.stat_ps, 1)

        def x_there(pe, n):
            return lambda k: pe.wait_ge(s.xl_ready, KD * n + k + 1)

        def to_tokens_pe(pe, first, blocks, width=P):
            for i, n in enumerate(TILES):
                if first + i >= 2:
                    pe.wait_ge(s.tok_copied, first + i - 1)
                for m, src in enumerate(blocks):
                    mm = pe.transpose(M[0:n, 2 + (first + i) % 2, m * P:(m + 1) * P], src[:, i * P:i * P + n], ident[:, :])
                mm.then_inc(s.tok_ps, 1)

        def to_tokens_act(act, first, dst, cols, shape=None):
            for i, n in enumerate(TILES):
                act.wait_ge(s.tok_ps, first + i + 1)
                src = M[0:n, 2 + (first + i) % 2, 0:cols]
                if shape:
                    src = src.rearrange("p (h v) -> p h v", h=shape)
                act.activation(dst(i, n), src, ACT.Copy).then_inc(s.tok_copied, 1)

        def branch_pe(pe, b, fill):
            for hd in range(HEADS):
                fill(1)
                pe.wait_ge(s.bn_sq, b * HEADS + hd + 1)
                if hd or b:
                    pe.wait_ge(s.bn_ln, b * HEADS + hd)
                for half in range(2):
                    mm = pe.matmul(M[:, half, 0:HALF], ones[:, :], rO[b][:, hd, half * HALF:(half + 1) * HALF],
                                   start=True, stop=True)
                mm.then_inc(s.bn_ps, 1)

        def branch_act(act, step, b, gate):
            if gate is not None:
                func, src = gate
                act.activation(src, src, func).then_inc(s.bn_gate, 1)
            for hd in range(HEADS):
                act.activation(rO[b][:, hd, :], oraw[b][:, hd, :], ACT.Square).then_inc(s.bn_sq, 1)
            for hd in range(HEADS):
                act.wait_ge(s.bn_ps, b * HEADS + hd + 1)
                act.activation(halves(rO[b][:, hd, :]), M01, ACT.Ln, scale=1.0 / DV,
                               bias=epsc[:, 0:1]).then_inc(s.bn_ln, 1)
            act.wait_ge(s.bn_ln, (b + 1) * HEADS)
            act.activation(rO[b][:, :, :], rO[b][:, :, :], ACT.Exp, scale=-0.5).then_inc(s.bn_r, 1)
            act.wait_ge(s.bn_o, b + 1)
            act.activation(oH[b][:, :, :], oraw[b][:, :, :], ACT.Copy).then_inc(s.bn_h, 1)

        def branch_dve(dve, step, b, gate, between):
            between()
            dve.wait_ge(s.bn_r, b + 1)
            ins = dve.scalar_tensor_tensor(out=oraw[b][:, :, :], in0=oraw[b][:, :, :], scalar=ghead[:, b:b + 1],
                                           in1=rO[b][:, :, :], op0=ALU.mult, op1=ALU.mult)
            if gate is not None:
                step(ins)
                dve.wait_ge(s.bn_gate, b + 1)
                ins = dve.tensor_tensor(oraw[b][:, :, :], oraw[b][:, :, :], gate, ALU.mult)
            ins.then_inc(s.bn_o, 1)
            between()
            dve.wait_ge(s.bn_h, b + 1)
            dve.tensor_tensor(oL[b][:, :, :], oraw[b][:, :, :], oH[b][:, :, :].bitcast(F32),
                              ALU.subtract).then_inc(s.bn_l, 1)

        def take(dve, out, dst):
            dve.wait_ge(s.chunk_done, out + 1)
            dve.tensor_tensor(halves(dst), out2(out % 2), halves(rB[:, :]), ALU.mult).then_inc(s.out_taken, 1)

        def merge_chunks(b):
            n = CHUNK[f"merge{b}"]
            for q in range(KD // 2):
                yield n + 3 * q, "gate", 2 * q
                yield n + 3 * q + 1, "gate", 2 * q + 1
                yield n + 3 * q + 2, "branch", 2 * q

        def two_outputs(r):
            return r[:, :, :].rearrange("p (k o) n -> p k (o n)", k=HEADS)

        LOAD_PROMPT = 11

        lo64 = [slice(0, DK), slice(DK, P)]

        with nc.Fori(0, DEPTH) as layer:

            def at(x):
                return x[bass.ds(layer, 1)]

            with nc.Block() as block:

                @block.sync
                def _(sp):
                    for j, n in enumerate(("g_mix", "g_ffn", "g_ple")):
                        sp.dma_start(gains[:, j, :], at(a[n]).rearrange("o (k p) -> p (o k)", p=P)).then_inc(s.gain_in, 16)
                    win = at(a["w_in"]).rearrange("o (k p) e -> p (o k) e", p=P)
                    for j in range(4):
                        load_chunk(sp, CHUNK["gla"] + j, lambda r: r[:, :, :], win[:, :, COL_GLA + P * j:COL_GLA + P * (j + 1)])
                    for j, n in enumerate(("g_gla_norm", "g_mlstm_norm", "g_diff_norm")):
                        sp.dma_start(ghead[:, j:j + 1], at(a[n]).rearrange("o p -> p o")).then_inc(s.par_in, 16)
                    sp.dma_start(bgk[:, :], at(a["b_gla_gk"]).rearrange("o (k p) -> p (o k)", p=P)).then_inc(s.par_in, 16)
                    for j in range(2):
                        sp.dma_start(bif[32 + 32 * j:32 + 32 * j + HEADS, :],
                                     at(a["b_mlstm_if"])[:, HEADS * j:HEADS * (j + 1)].rearrange("o p -> p o")).then_inc(s.par_in, 16)
                    sp.dma_start(wgk[:, :], at(a["w_gla_gk"]).rearrange("o r e -> (o r) e")).then_inc(s.par_in, 16)
                    sp.dma_start(lamv[:, :, :], at(a["diff_lambda"]).partition_broadcast(P).rearrange("p o r d -> p (o r) d")
                                 ).then_inc(s.par_in, 16)
                    sp.dma_start(lamc[:, :], at(c["lamc"]).rearrange("o p n -> (o p) n")).then_inc(s.par_in, 16)
                    sp.dma_start(m_in[:, :], at(a["state_mlstm_m"]).rearrange("o b h -> h (o b)")).then_inc(s.par_in, 16)
                    load_loop(sp, "gla", 12, lambda j: KD, lambda i, j: win[:, :, bass.ds(COL_GLA + 4 * P * i + P * j, P)])
                    n = CHUNK["small"]
                    sp.wait_ge(s.wl_split, n - (RAW - 1))
                    for at_col, col in ((0, COL_LR), (32, COL_IF), (64, COL_IF + HEADS), (96, COL_IF)):
                        sp.dma_start(raw[n % RAW][:, :, at_col:at_col + 32], win[:, :, col:col + 32]).then_inc(s.w_in[n % RAW], 16)
                    sp.dma_start(spill, h[:, :, :]).then_inc(s.spilled, 16)
                    sp.dma_start(g_reset[:, :], c["greset"]).then_inc(s.greset_in, 16)
                    for q in range(2):
                        sp.dma_start(g_Sin[lo64[q], :, :, :], at(a["state_gla"])[:, :, q:HEADS:2].rearrange(
                            "o b p d v -> d (o b) p v")).then_inc(s.gst_in, 16)
                    load_loop(sp, "ml", 12, lambda j: KD, lambda i, j: win[:, :, bass.ds(COL_ML + 4 * P * i + P * j, P)])
                    sp.wait_ge(s.g_s, NCH + DEC_BATCH)
                    sp.dma_start(at(o["gla_prompt"]).rearrange("o b (p q) d v -> (q d) (o b p) v", q=2),
                                 g_S[:, NCH - 1, :, :]).then_inc(s.gstore, 16)
                    sp.dma_start(at(o["gla_sample"]).rearrange("o b (p q) d v -> (q d) (o b) p v", q=2),
                                 g_Sin[:, :, :, :]).then_inc(s.gstore, 16)
                    load_df = Between(lambda j: load_chunk(sp, CHUNK["df"] + j, lambda r: r[:, :, :],
                                                           win[:, :, COL_DF + P * j:COL_DF + P * (j + 1)]), 12)
                    load_df(4)
                    sp.wait_ge(s.bn_l, 1)
                    sp.dma_start(r_reset[:, :], c["rreset"]).then_inc(s.rreset_in, 16)
                    sp.wait_ge(s.tok_copied, TOK["mv"] + 5)
                    for q in range(2):
                        sp.dma_start(m_Cin[lo64[q], :, :, 0:DV], at(a["state_mlstm_c"])[:, :, q:HEADS:2].rearrange(
                            "o b p d v -> d (o b) p v")).then_inc(s.mst_in, 16)
                    sp.dma_start(m_Cin[:, :, :, DV:DV + 1], at(a["state_mlstm_n"]).rearrange(
                        "o b (p q) (d u) -> (q d) (o b) p u", q=2, u=1)).then_inc(s.mst_in, 16)
                    load_df(12 - 4)
                    sp.wait_ge(s.ml_rows, 4)
                    sp.dma_start(at(o["m_prompt"]).rearrange("o b h -> h (o b)"), r_m[:, SEQ - 1:SEQ]).then_inc(s.mstore, 16)
                    sp.dma_start(at(o["m_sample"]).rearrange("o b h -> h (o b)"),
                                 r_m[:, SEQ + DEC_SEQ - 1:T:DEC_SEQ]).then_inc(s.mstore, 16)
                    sp.wait_ge(s.ml_c, PT + DEC_BATCH)
                    sp.dma_start(at(o["c_prompt"]).rearrange("o b (p q) d v -> (q d) (o b p) v", q=2),
                                 m_C[:, (PT - 1) % 2, :, 0:DV]).then_inc(s.mstore, 16)
                    sp.dma_start(at(o["n_prompt"]).rearrange("o b (p q) (d u) -> (q d) (o b p) u", q=2, u=1),
                                 m_C[:, (PT - 1) % 2, :, DV:DV + 1]).then_inc(s.mstore, 16)
                    sp.dma_start(at(o["c_sample"]).rearrange("o b (p q) d v -> (q d) (o b) p v", q=2),
                                 m_Cin[:, :, :, 0:DV]).then_inc(s.mstore, 16)
                    sp.dma_start(at(o["n_sample"]).rearrange("o b (p q) (d u) -> (q d) (o b) p u", q=2, u=1),
                                 m_Cin[:, :, :, DV:DV + 1]).then_inc(s.mstore, 16)
                    wg = at(a["w_gate"]).rearrange("o (k p) e -> p (o k) e", p=P)
                    wb = at(a["w_branch"]).rearrange("o (k p) e -> p (o k) e", p=P)

                    def merge_load(b, chunk):
                        n, what, m = chunk
                        if what == "gate":
                            load_chunk(sp, n, lambda r: r[:, :, :], wg[:, :, D * b + P * m:D * b + P * (m + 1)])
                        else:
                            load_chunk(sp, n, two_outputs, wb[:, HEADS * b:HEADS * (b + 1), P * m:P * (m + 2)])

                    chunks01 = [(b, chunk) for b in range(2) for chunk in merge_chunks(b)]
                    load_next = Between(lambda at_chunk: merge_load(*chunks01[at_chunk]), len(chunks01))
                    load_next(4)
                    sp.wait_ge(s.mstore, 16 * 6)
                    sp.wait_ge(s.bn_l, 2)
                    sp.dma_start(d_cos[:, :], c["cos"]).then_inc(s.trig_in, 16)
                    sp.dma_start(d_sin[:, :], c["sin"]).then_inc(s.trig_in, 16)
                    for i, n in enumerate(TILES):
                        sp.wait_ge(s.tok_copied, TOK["dv"] + i + 1)
                        dst = (at(o["v_prompt"])[:, :, i * P:(i + 1) * P].rearrange("o b t h v -> (o b t) h v") if n == P
                               else at(o["v_sample"]).rearrange("o b t h v -> (o b t) h v"))
                        sp.dma_start(dst, dv[0:n, i, :, :]).then_inc(s.vstore, 16)
                    load_next(2)
                    for i, n in enumerate(TILES):
                        sp.wait_ge(s.tok_copied, TOK["dk"] + i + 1)
                        dst = (at(o["k_prompt"])[:, :, i * P:(i + 1) * P].rearrange("o b t h v -> (o b t) (h v)") if n == P
                               else at(o["k_sample"]).rearrange("o b t h v -> (o b t) (h v)"))
                        sp.dma_start(dst, d_kout[0:n, :]).then_inc(s.kstore, 16)
                    load_next(LOAD_PROMPT)
                    ck, cv = at(a["cache_k"]), at(a["cache_v"])
                    pool_n = a["cache_k"].shape[1]
                    sp.wait_ge(s.tok_copied, TOK["dv"] + 5)
                    for g in range(2):
                        for j in range(4 * PAGES):
                            n = 4 * PAGES * g + j
                            if n >= 2:
                                sp.wait_ge(s.tok_ps, TOK["page"] + n - 1)
                            page = sp.value_load(pages[0:1, n:n + 1], min_val=0, max_val=pool_n - 1)
                            sp.dma_start(d_kr[:, n % 2, :, :], ck[:, bass.ds(page, 1)].rearrange(
                                "o q p (m c) d -> (o q p) m (c d)", c=2)).then_inc(s.page[n % 2], 16)
                            if j % 2:
                                load_next()
                        for j in range(4 * PAGES):
                            n = 4 * PAGES * g + j
                            if n >= 2:
                                sp.wait_ge(s.v_used, n - 1)
                            page = sp.value_load(pages[0:1, n:n + 1], min_val=0, max_val=pool_n - 1)
                            sp.dma_start(d_V[:, n % 2, :], cv[:, bass.ds(page, 1)].rearrange(
                                "o q p h v -> (o q p) (h v)")).then_inc(s.vpage[n % 2], 16)
                    load_next.rest()
                    sp.wait_ge(s.sp_copied, 2)
                    sp.wait_ge(s.pv_copied, PT * HEADS)
                    sp.dma_start(p_tok[:, 0:PT, :], at(a["p_prompt"]).rearrange("o b (i p) e -> p (o b i) e", p=P)).then_inc(s.ptok_in, 16)
                    sp.dma_start(p_tok[0:NS, PT, :], at(a["p_sample"]).rearrange("o b t e -> (o b t) e")).then_inc(s.ptok_in, 16)
                    for chunk in merge_chunks(2):
                        merge_load(2, chunk)
                    wo = at(a["w_out"]).rearrange("o (k p) e -> p (o k) e", p=P)
                    load_loop(sp, "out", 8, lambda j: KD, lambda i, j: wo[:, :, bass.ds(4 * P * i + P * j, P)])
                    fg = at(a["w_ffn_gate"]).rearrange("o (k p) e -> p (o k) e", p=P)
                    fu = at(a["w_ffn_up"]).rearrange("o (k p) e -> p (o k) e", p=P)
                    load_loop(sp, "ffn", 2 * KF, lambda j: KD, lambda i, j: (fg, fu)[j % 2][:, :, bass.ds(2 * P * i + P * (j // 2), P)])
                    fd = at(a["w_ffn_down"]).rearrange("o (k p) e -> p (o k) e", p=P)
                    load_loop(sp, "down", 4 * KD, lambda j: DOWN_K[j % 4][1],
                              lambda i, j: fd[:, DOWN_K[j % 4][0]:DOWN_K[j % 4][0] + DOWN_K[j % 4][1], bass.ds(2 * P * i + P * (j // 4), P)], per=8)
                    pg = at(a["w_ple_gate"]).rearrange("o (k p) e -> p (o k) e", p=P)
                    pp = at(a["w_ple_proj"]).rearrange("o (k p) e -> p (o k) e", p=P)
                    for q in range(2):
                        load_chunk(sp, CHUNK["ple"] + q, lambda r: r[:, :, :].rearrange("p (k o) n -> p k (o n)", k=KP),
                                   pp[:, :, 4 * P * q:4 * P * (q + 1)])
                    for m in range(KD):
                        load_chunk(sp, CHUNK["ple"] + 2 + m, lambda r: r[:, :, :], pg[:, :, P * m:P * (m + 1)])
                    sp.wait_ge(s.gstore, 32)
                    sp.wait_ge(s.mstore, 16 * 6)
                    sp.wait_ge(s.vstore, 16 * 5)
                    sp.wait_ge(s.kstore, 16 * 5)

                @block.gpsimd
                def _(pool):
                    low_loop(pool, "gla", 12, lambda j: KD)
                    low_loop(pool, "small", 1, lambda j: KD, per=1)
                    for name in ("ml", "df", "merge0", "merge1", "merge2"):
                        both_loop(pool, name)
                    low_loop(pool, "out", 8, lambda j: KD)
                    low_loop(pool, "ffn", 2 * KF, lambda j: KD)
                    low_loop(pool, "down", 4 * KD, lambda j: DOWN_K[j % 4][1], per=8)
                    for n in range(10):
                        low_chunk(pool, CHUNK["ple"] + n)

                def gla_act(act, step):
                    to_tokens_act(act, TOK["gv"], lambda i, n: gv[0:n, i, :, :], HEADS * DV, HEADS)
                    for m in range(2):
                        act.wait_ge(s.gz_ps, m + 1)
                        if m:
                            act.wait_ge(s.gz_min, 2 * m)
                        step(act.activation(halves(g_az[:, :]), M01, ACT.Abs, bias=bgk[:, m:m + 1]))
                        act.sem_inc(s.gz_abs, 1)
                        step(act.activation(g_az[:, :], g_az[:, :], ACT.Exp, scale=-1.0))
                        act.activation(g_az[:, :], g_az[:, :], ACT.Ln, bias=1.0).then_inc(s.gz_ln, 1)
                    act.wait_ge(s.g_b_ready, 2)
                    act.activation(g_E[:, :, :], g_b[:, :, :], ACT.Exp, scale=1.0 / 16).then_inc(s.g_e, 1)
                    act.wait_ge(s.g_qg, 1)
                    act.activation(g_E[:, :, :], g_b[:, :, :], ACT.Exp, scale=-1.0 / 16).then_inc(s.g_e, 1)
                    act.wait_ge(s.g_kg, 2)
                    act.activation(g_E[:, :, :], g_b[:, :, :], ACT.Exp, scale=1.0 / 16).then_inc(s.g_e, 1)
                    to_tokens_act(act, TOK["kd"], lambda i, n: g_kdT[0:n, i, :], HEADS * DK)
                    for i in range(PT):
                        act.wait_ge(s.g_o_ps, i + 1)
                        act.activation(oraw[0][:, :, i * P:(i + 1) * P], M[:, 1, :].rearrange("p (h t) -> p h t", h=HEADS),
                                       ACT.Copy).then_inc(s.g_o, 1)
                    act.wait_ge(s.g_o_ps, PT + 1)
                    act.activation(oraw[0][:, :, SEQ:T], M[:, 1, 0:HEADS * NS].rearrange("p (h t) -> p h t", h=HEADS),
                                   ACT.Copy).then_inc(s.g_o, 1)
                    act.wait_ge(s.g_o, PT + 1)
                    to_tokens_act(act, TOK["mv"], lambda i, n: mv[0:n, i, :, 0:DV], HEADS * DV, HEADS)
                    to_tokens_act(act, TOK["mk"], lambda i, n: m_kT[0:n, i, :, :], HEADS * DK, HEADS)
                    branch_act(act, step, 0, (ACT.Silu, A[:, 4:8, :]))

                def gla_dve(dve, step):
                    def ml_out(n):
                        if n == 0:
                            dve.wait_ge(s.spilled, 16)
                        take(dve, OUT["ml"] + n, B[:, n, :] if n < 4 else mvf[:, n - 4, :] if n < 8 else B[:, n - 4, :])

                    taken = Between(ml_out, 12)
                    for n in range(12):
                        take(dve, n, A[:, n, :] if n < 4 else gvf[:, n - 4, :] if n < 8 else A[:, n - 4, :])
                    dve.wait_ge(s.chunk_done, 13)
                    ps = out2(0)
                    for at_row, rows in ((0, RANK), (32, HEADS), (64, HEADS)):
                        ins = dve.tensor_tensor(halves(small[at_row:at_row + rows, :]), ps[at_row:at_row + rows],
                                                halves(rB[at_row:at_row + rows, :]), ALU.mult)
                        if at_row < 64:
                            step(ins)
                    ins.then_inc(s.out_taken, 1)
                    for m in range(2):
                        dve.wait_ge(s.gz_abs, m + 1)
                        step(dve.tensor_scalar(halves(g_E[:, m, :]), M01, bgk[:, m:m + 1], 0.0, ALU.add, ALU.min))
                        dve.sem_inc(s.gz_min, 1)
                        dve.wait_ge(s.gz_ln, m + 1)
                        step(dve.tensor_tensor(g_E[:, m, :], g_E[:, m, :], g_az[:, :], ALU.subtract))
                        dve.sem_inc(s.gz_min, 1)
                        if m == 0:
                            dve.wait_ge(s.greset_in, 16)
                        dve.tensor_tensor_scan(g_b[:, m, :], g_reset[:, :], g_E[:, m, :], 0.0, ALU.mult,
                                               ALU.add).then_inc(s.g_b_ready, 1)
                        taken()
                    dve.wait_ge(s.g_b_ready, 2)
                    dve.wait_ge(s.g_e, 1)
                    step(dve.tensor_copy(g_dec[:, :, 0:NCH], g_E[:, :, CH - 1:SEQ:CH]))
                    step(dve.tensor_copy(g_dec[:, :, NCH:NCH + DEC_BATCH], g_E[:, :, SEQ + DEC_SEQ - 1:T:DEC_SEQ]))
                    dve.wait_ge(s.tok_copied, TOK["gv"] + 5)
                    for q in range(2):
                        step(dve.memset(g_qz[lo64[1 - q], q:HEADS:2, :], 0.0))
                        step(dve.scalar_tensor_tensor(out=g_qz[lo64[q], q:HEADS:2, :], in0=A[lo64[q], 0:2, :], scalar=DK ** -0.5,
                                                      in1=g_E[lo64[q], :, :], op0=ALU.mult, op1=ALU.mult))
                    dve.sem_inc(s.g_qg, 1)
                    taken()
                    dve.wait_ge(s.g_e, 2)
                    dve.tensor_tensor(g_kg[:, :, :], A[:, 2:4, :], g_E[:, :, :], ALU.mult).then_inc(s.g_kg, 1)
                    for m in range(2):
                        step(dve.tensor_copy(g_az[:, m * 16:m * 16 + NCH], g_b[:, m, CH - 1:SEQ:CH]))
                        step(dve.tensor_copy(g_az[:, m * 16 + 8:m * 16 + 16], g_b[:, m, SEQ + DEC_SEQ - 1:T:DEC_SEQ]))
                        for lo, hi, n, width in ((0, SEQ, NCH, CH), (SEQ, T, DEC_BATCH, DEC_SEQ)):
                            v = g_b[:, m, lo:hi].rearrange("p (n t) -> p n t", n=n)
                            last = g_az[:, m * 16 + (8 if lo else 0):m * 16 + (16 if lo else 8)].unsqueeze(2).to_broadcast([P, n, width])
                            step(dve.tensor_tensor(v, last, v, ALU.subtract))
                    dve.sem_inc(s.g_kg, 1)
                    dve.wait_ge(s.g_e, 3)
                    dve.tensor_tensor(A[:, 2:4, :], A[:, 2:4, :], g_E[:, :, :], ALU.mult).then_inc(s.g_kd, 1)
                    taken()
                    dve.wait_ge(s.tok_copied, TOK["kd"] + 5)
                    dve.tensor_tensor(g_kdm[:, :, :], g_kdT[0:NS, PT, :].unsqueeze(1).to_broadcast([NS, DEC_BATCH, HEADS * DK]),
                                      seqm[:, :].unsqueeze(2).to_broadcast([NS, DEC_BATCH, HEADS * DK]),
                                      ALU.mult).then_inc(s.g_kdm_ready, 1)

                    def masked(i):
                        dve.wait_ge(s.g_at_ps, i + 1)
                        if i >= 2:
                            dve.wait_ge(s.g_o_ps, i - 1)
                        dve.tensor_tensor(g_A[:, i % 2, :, :],
                                          M[:, 0, :].rearrange("p (h t) -> p h t", h=HEADS),
                                          gmask[:, :].unsqueeze(1).to_broadcast([P, HEADS, P]), ALU.mult).then_inc(s.g_at, 1)

                    masked(0)
                    for n in range(NCH):
                        if n % 2 == 0 and n // 2 + 1 < PT:
                            masked(n // 2 + 1)
                        if n % 2:
                            taken()
                        dve.wait_ge(s.g_ds_ps, n + 1)
                        ps = M[:, 2 + n % 2, 0:2 * DV].rearrange("p (q v) -> p q v", q=2)
                        if n == 0:
                            dve.tensor_copy(g_S[:, 0, :, :], ps).then_inc(s.g_s, 1)
                            continue
                        dve.wait_ge(s.g_s, n)
                        step(dve.scalar_tensor_tensor(out=g_S[:, n, 0, :], in0=g_S[:, n - 1, 0, :], scalar=g_dec[:, 0, n:n + 1],
                                                      in1=ps[:, 0, :], op0=ALU.mult, op1=ALU.add))
                        dve.scalar_tensor_tensor(out=g_S[:, n, 1, :], in0=g_S[:, n - 1, 1, :], scalar=g_dec[:, 1, n:n + 1],
                                                 in1=ps[:, 1, :], op0=ALU.mult, op1=ALU.add).then_inc(s.g_s, 1)
                    dve.wait_ge(s.g_at_ps, PT + 1)
                    dve.tensor_tensor(g_As[:, :, :], M[0:NS, 0, 0:HEADS * NS].rearrange("p (h t) -> p h t", h=HEADS),
                                      smask[:, :].unsqueeze(1).to_broadcast([NS, HEADS, NS]), ALU.mult).then_inc(s.g_at, 1)
                    dve.wait_ge(s.g_o_ps, PT + 1)
                    dve.wait_ge(s.gst_in, 32)
                    for b in range(DEC_BATCH):
                        n = NCH + b
                        dve.wait_ge(s.g_ds_ps, n + 1)
                        ps = M[:, 2 + n % 2, 0:2 * DV].rearrange("p (q v) -> p q v", q=2)
                        step(dve.scalar_tensor_tensor(out=g_Sin[:, b, 0, :], in0=g_Sin[:, b, 0, :], scalar=g_dec[:, 0, n:n + 1],
                                                      in1=ps[:, 0, :], op0=ALU.mult, op1=ALU.add))
                        dve.scalar_tensor_tensor(out=g_Sin[:, b, 1, :], in0=g_Sin[:, b, 1, :], scalar=g_dec[:, 1, n:n + 1],
                                                 in1=ps[:, 1, :], op0=ALU.mult, op1=ALU.add).then_inc(s.g_s, 1)
                        if b % 2:
                            taken()
                    taken.rest()

                def gla_pe(pe, fill):
                    pe.wait_ge(s.out_taken, 12)
                    to_tokens_pe(pe, TOK["gv"], [gvf[:, m, :] for m in range(4)])
                    pe.wait_ge(s.out_taken, 13)
                    for m in range(2):
                        if m:
                            fill(4)
                            pe.wait_ge(s.gz_min, 2)
                            pe.wait_ge(s.gz_abs, 1)
                        for half in range(2):
                            mm = pe.matmul(M[:, half, 0:HALF], wgk[:, m * P:(m + 1) * P], small[0:RANK, half * HALF:(half + 1) * HALF],
                                           start=True, stop=True)
                        mm.then_inc(s.gz_ps, 1)
                    fill(14)
                    pe.wait_ge(s.g_kd, 1)
                    to_tokens_pe(pe, TOK["kd"], [A[:, 2 + m, :] for m in range(2)])
                    fill(1)
                    pe.wait_ge(s.tok_copied, TOK["kd"] + 5)

                    def scores(i):
                        if i:
                            pe.wait_ge(s.g_at, i)
                        for hd in range(HEADS):
                            mm = pe.matmul(M[:, 0, hd * P:(hd + 1) * P], g_kg[:, hd // 2, i * P:(i + 1) * P],
                                           g_qz[:, hd, i * P:(i + 1) * P], start=True, stop=True)
                        mm.then_inc(s.g_at_ps, 1)

                    scores(0)
                    for n in range(NCH):
                        i, q = n // 2, lo64[n % 2]
                        if n % 2 == 0 and i + 1 < PT:
                            scores(i + 1)
                        fill(1)
                        if n >= 2:
                            pe.wait_ge(s.g_s, n - 1)
                        for hd in range(HEADS):
                            c0 = (hd // 2) * DV
                            mm = pe.matmul(M[lo64[hd % 2], 2 + n % 2, c0:c0 + DV], g_kdT[q, i, hd * DK:(hd + 1) * DK], gv[q, i, hd, :],
                                           start=True, stop=True)
                        mm.then_inc(s.g_ds_ps, 1)
                        if n % 2 == 0:
                            continue
                        fill(2)
                        pe.wait_ge(s.g_at, i + 1)
                        pe.wait_ge(s.g_s, n)
                        if i:
                            pe.wait_ge(s.g_o, i)
                        for hd in range(HEADS):
                            pe.matmul(M[:, 1, hd * P:(hd + 1) * P], gv[:, i, hd, :], g_A[:, i % 2, hd, :], start=True, stop=False,
                                      skip_group_check=True)
                            for m in (n - 1, n):
                                if m:
                                    t0 = m * CH
                                    mm = pe.matmul(M[:, 1, hd * P + t0 % P:hd * P + t0 % P + CH], g_S[:, m - 1, hd // 2, :],
                                                   g_qz[:, hd, t0:t0 + CH], start=False, stop=(m == n), skip_group_check=True)
                        mm.then_inc(s.g_o_ps, 1)
                    pe.wait_ge(s.g_at, PT)
                    for hd in range(HEADS):
                        mm = pe.matmul(M[0:NS, 0, hd * NS:(hd + 1) * NS], g_kg[:, hd // 2, SEQ:T], g_qz[:, hd, SEQ:T],
                                       start=True, stop=True)
                    mm.then_inc(s.g_at_ps, 1)
                    fill(1)
                    pe.wait_ge(s.g_at, PT + 1)
                    pe.wait_ge(s.gst_in, 32)
                    pe.wait_ge(s.g_o, PT)
                    for hd in range(HEADS):
                        pe.matmul(M[:, 1, hd * NS:(hd + 1) * NS], gv[0:NS, PT, hd, :], g_As[:, hd, :], start=(hd == 0), stop=False,
                                  skip_group_check=True)
                    for b in range(DEC_BATCH):
                        for hd in range(HEADS):
                            t0 = b * DEC_SEQ
                            mm = pe.matmul(M[:, 1, hd * NS + t0:hd * NS + t0 + DEC_SEQ], g_Sin[:, b, hd // 2, :],
                                           g_qz[:, hd, SEQ + t0:SEQ + t0 + DEC_SEQ], start=False,
                                           stop=(b == DEC_BATCH - 1), skip_group_check=True)
                    mm.then_inc(s.g_o_ps, 1)
                    pe.wait_ge(s.g_kdm_ready, 1)
                    for b in range(DEC_BATCH):
                        n = NCH + b
                        fill(2)
                        pe.wait_ge(s.g_s, n - 1)
                        for hd in range(HEADS):
                            c0 = (hd // 2) * DV
                            mm = pe.matmul(M[lo64[hd % 2], 2 + n % 2, c0:c0 + DV], g_kdm[:, b, hd * DK:(hd + 1) * DK], gv[0:NS, PT, hd, :],
                                           start=True, stop=True)
                        mm.then_inc(s.g_ds_ps, 1)
                    fill.rest()
                    pe.wait_ge(s.out_taken, OUT["ml"] + 12)
                    to_tokens_pe(pe, TOK["mv"], [mvf[:, m, :] for m in range(4)])
                    to_tokens_pe(pe, TOK["mk"], [B[:, 2 + m, :] for m in range(2)])

                def mlstm_act(act, step):
                    act.wait_ge(s.ml_rows, 1)
                    step(act.activation(r_en[:, :], r_m[:, :], ACT.Abs))
                    step(act.activation(r_en[:, :], r_en[:, :], ACT.Exp, scale=-1.0))
                    act.activation(r_en[:, :], r_en[:, :], ACT.Ln, bias=1.0).then_inc(s.ml_ln, 1)
                    act.wait_ge(s.ml_rows, 4)
                    step(act.activation(r_wi[:, :], r_wi[:, :], ACT.Exp))
                    step(act.activation(r_d[:, :], r_d[:, :], ACT.Exp))
                    act.activation(r_en[:, :], r_m[:, :], ACT.Exp, scale=-1.0).then_inc(s.ml_ex, 1)
                    for i, n in enumerate(TILES):
                        act.wait_ge(s.ml_d_ps, i + 1)
                        act.wait_ge(s.ml_col, 1)
                        if i:
                            act.wait_ge(s.ml_sd, i)
                        for hd in range(HEADS):
                            act.activation(m_D[0:n, hd * n:(hd + 1) * n], M[0:n, 0, hd * n:(hd + 1) * n], ACT.Exp, scale=-1.0,
                                           bias=m_cols[0:n, i, hd:hd + 1]).then_inc(s.ml_d, 1)
                        if i:
                            act.wait_ge(s.ml_t_ps, i)
                            act.activation(oraw[1][:, :, (i - 1) * P:i * P], M[:, 2, :].rearrange("p (h t) -> p h t", h=HEADS),
                                           ACT.Copy).then_inc(s.ml_o, 1)
                    act.wait_ge(s.ml_den_ps, 1)
                    act.activation(m_ad[:, 0:HEADS * NS], M[:, 3, 0:HEADS * NS], ACT.Abs).then_inc(s.ml_ad, 1)
                    act.wait_ge(s.ml_o, 5)
                    act.wait_ge(s.ml_c, PT + DEC_BATCH)
                    branch_act(act, step, 1, (ACT.Sigmoid, B[:, 4:8, :]))

                def mlstm_dve(dve, step):
                    def df_out(n):
                        if n == 0:
                            dve.wait_ge(s.gstore, 32)
                        take(dve, OUT["df"] + n, C[:, n, :] if n < 8 else dvf[:, n - 8, :])

                    taken = Between(df_out, 12)
                    branch_dve(dve, step, 0, A[:, 4:8, :], taken)
                    step(dve.memset(mv[:, :, :, DV:DV + 1], 1.0))
                    step(dve.tensor_scalar(r_a[:, :], small[32:32 + HEADS, :], bif[32:32 + HEADS, 0:1], None, ALU.add))
                    step(dve.tensor_scalar(r_m[:, :], small[64:64 + HEADS, :], bif[64:64 + HEADS, 0:1], None, ALU.add))
                    dve.sem_inc(s.ml_rows, 1)
                    taken()
                    step(dve.tensor_scalar(r_F[:, :], r_m[:, :], 0.0, None, ALU.min))
                    dve.wait_ge(s.ml_ln, 1)
                    step(dve.tensor_tensor(r_m[:, :], r_F[:, :], r_en[:, :], ALU.subtract))
                    dve.wait_ge(s.rreset_in, 16)
                    step(dve.tensor_tensor_scan(r_F[:, :], r_reset[:, :], r_m[:, :], 0.0, ALU.mult, ALU.add))
                    step(dve.tensor_tensor(r_a[:, :], r_a[:, :], r_F[:, :], ALU.subtract))
                    step(dve.memset(r_d[:, :], 0.0))
                    step(dve.tensor_copy(r_d[:, P:SEQ:P], r_F[:, P - 1:SEQ - P:P]))
                    step(dve.tensor_tensor_scan(r_g[:, 0:SEQ], r_d[:, 0:SEQ], r_a[:, 0:SEQ], 0.0, ALU.add, ALU.max))
                    for b in range(DEC_BATCH):
                        t0 = SEQ + b * DEC_SEQ
                        step(dve.tensor_tensor_scan(r_g[:, t0:t0 + DEC_SEQ], r_d[:, t0:t0 + DEC_SEQ], r_a[:, t0:t0 + DEC_SEQ],
                                                    m_in[:, b:b + 1], ALU.add, ALU.max))
                    step(dve.tensor_tensor(r_m[:, :], r_F[:, :], r_g[:, :], ALU.add))
                    step(dve.memset(m_prev[:, 0:1], 0.0))
                    step(dve.tensor_copy(m_prev[:, 1:PT], r_m[:, P - 1:SEQ - P:P]))
                    step(dve.tensor_copy(m_prev[:, PT:12], m_in[:, :]))
                    dve.sem_inc(s.ml_rows, 1)
                    for lo, hi, n, width, k in ((0, SEQ, PT, P, 0), (SEQ, T, DEC_BATCH, DEC_SEQ, PT)):
                        g3 = r_g[:, lo:hi].rearrange("p (n t) -> p n t", n=n)
                        step(dve.tensor_tensor(r_wi[:, lo:hi].rearrange("p (n t) -> p n t", n=n),
                                               m_prev[:, k:k + n].unsqueeze(2).to_broadcast([HEADS, n, width]), g3, ALU.subtract))
                        step(dve.tensor_tensor(r_d[:, lo:hi].rearrange("p (n t) -> p n t", n=n),
                                               r_a[:, lo:hi].rearrange("p (n t) -> p n t", n=n),
                                               g3[:, :, width - 1:width].to_broadcast([HEADS, n, width]), ALU.subtract))
                    dve.sem_inc(s.ml_rows, 2)
                    taken()
                    dve.wait_ge(s.ml_col_ps, 1)
                    step(dve.tensor_copy(m_cols[:, 0:PT, :], M[:, 0, 0:12 * PT].rearrange("p (i k) -> p i k", i=PT)))
                    dve.tensor_copy(m_cols[0:NS, PT, :], M[0:NS, 0, 12 * PT:12 * PT + 12]).then_inc(s.ml_col, 1)
                    dve.wait_ge(s.ml_col, 1)
                    for p in range(2):
                        ps = M01 if p == 0 else M23
                        dve.wait_ge(s.ml_wi_ps, p + 1)
                        for q in range(2):
                            r, hd = lo64[q], 2 * p + q
                            step(dve.memset(m_qwz[lo64[1 - q], hd, :], 0.0))
                            step(dve.tensor_tensor(halves(m_qwz[r, hd, :]), halves(B[r, p, :]), ps[r], ALU.mult))
                            step(dve.memset(m_qz[lo64[1 - q], hd, :], 0.0))
                            step(dve.tensor_copy(m_qz[r, hd, :], B[r, p, :]))
                        step(dve.tensor_copy(m_dec[:, p, 0:2], ps[:, 0, P - 1:2 * P:P]))
                        step(dve.tensor_copy(m_dec[:, p, 2:4], ps[:, 1, 3 * P - 1 - HALF:4 * P - HALF:P]))
                        dve.tensor_copy(m_dec[:, p, 4:12], ps[:, 1, SEQ + DEC_SEQ - 1 - HALF:HALF:DEC_SEQ]).then_inc(s.ml_wi, 1)
                        if p == 0:
                            taken()
                    dve.wait_ge(s.ml_wi, 2)
                    dve.wait_ge(s.tok_copied, TOK["mk"] + 5)
                    for i, n in enumerate(TILES):
                        step(dve.scalar_tensor_tensor(out=m_kw[0:n, i, :, :], in0=m_kT[0:n, i, :, :], scalar=DK ** -0.5,
                                                      in1=m_cols[0:n, i, 4:8].unsqueeze(2).to_broadcast([n, HEADS, DK]),
                                                      op0=ALU.mult, op1=ALU.mult))
                    dve.sem_inc(s.ml_kw, 1)
                    taken()
                    dve.wait_ge(s.mst_in, 48)
                    for p in range(2):
                        for hd in (2 * p, 2 * p + 1):
                            step(dve.tensor_tensor(m_qns[:, hd, :].rearrange("p (b t) -> p b t", b=DEC_BATCH),
                                                   m_qwz[:, hd, SEQ:T].rearrange("p (b t) -> p b t", b=DEC_BATCH),
                                                   m_Cin[:, :, p, DV:DV + 1].to_broadcast([P, DEC_BATCH, DEC_SEQ]), ALU.mult))
                    dve.sem_inc(s.ml_qn, 1)
                    for i, n in enumerate(TILES):
                        w = HEADS * n
                        if i in (1, 3):
                            taken()
                        dve.wait_ge(s.ml_s_ps, i + 1)
                        dve.wait_ge(s.ml_d, HEADS * (i + 1))
                        if i:
                            dve.wait_ge(s.ml_n_ps, i)
                        dve.scalar_tensor_tensor(out=m_SD[0:n, 0:w], in0=M[0:n, 1, 0:w], scalar=DK ** -0.5, in1=m_D[0:n, 0:w],
                                                 op0=ALU.mult, op1=ALU.mult).then_inc(s.ml_sd, 1)
                        if n != P:
                            continue
                        dve.wait_ge(s.ml_c_ps, i + 1)
                        ps = M[:, 1, 0:2 * (DV + 1)].rearrange("p (q v) -> p q v", q=2)
                        if i == 0:
                            dve.tensor_copy(m_C[:, 0, :, :], ps).then_inc(s.ml_c, 1)
                        else:
                            for p in range(2):
                                ins = dve.scalar_tensor_tensor(out=m_C[:, i % 2, p, :], in0=m_C[:, (i - 1) % 2, p, :],
                                                               scalar=m_dec[:, p, i:i + 1], in1=ps[:, p, :],
                                                               op0=ALU.mult, op1=ALU.add)
                                if p == 0:
                                    step(ins)
                            ins.then_inc(s.ml_c, 1)
                        dve.wait_ge(s.ml_c, i + 1)
                        dve.wait_ge(s.ml_n_ps, i + 1)
                        if i:
                            dve.wait_ge(s.ml_t_ps, i)
                        num = M[:, 2:4, 0:2 * (DV + 1)].rearrange("p b (h v) -> p b h v", h=2)
                        den, m4 = num[:, :, :, DV], m_den[:, :].rearrange("p (b h) -> p b h", b=2)
                        step(dve.tensor_copy(m4, den))
                        step(dve.scalar_tensor_tensor(out=m_den[:, :], in0=m_den[:, :], scalar=-1.0, in1=m_den[:, :],
                                                      op0=ALU.mult, op1=ALU.max))
                        step(dve.tensor_tensor(m_den[:, :], m_den[:, :], m_cols[:, i, 8:12], ALU.max))
                        step(dve.reciprocal(m_den[:, :], m_den[:, :]))
                        dve.tensor_tensor(m_tok[:, :, :].rearrange("p (b h) v -> p b h v", b=2), num[:, :, :, 0:DV],
                                          m4.unsqueeze(3).to_broadcast([P, 2, 2, DV]), ALU.mult).then_inc(s.ml_tok, 1)
                    w = HEADS * NS
                    dve.wait_ge(s.ml_ad, 1)
                    dve.wait_ge(s.ml_e_ps, 1)
                    step(dve.tensor_tensor(m_ad[:, 0:w], m_ad[:, 0:w], M[:, 0, 0:w], ALU.max))
                    step(dve.reciprocal(m_ad[:, 0:w], m_ad[:, 0:w]))
                    dve.wait_ge(s.ml_n_ps, PT + 1)
                    dve.tensor_tensor(oraw[1][:, :, SEQ:T], M[:, 2, 0:w].rearrange("p (h t) -> p h t", h=HEADS),
                                      m_ad[:, 0:w].rearrange("p (h t) -> p h t", h=HEADS), ALU.mult).then_inc(s.ml_o, 1)
                    dve.tensor_tensor(m_kwm[:, :, :], m_kw[0:NS, PT, :, :].rearrange("p h d -> p (h d)").unsqueeze(1).to_broadcast(
                        [NS, DEC_BATCH, HEADS * DK]), seqm[:, :].unsqueeze(2).to_broadcast([NS, DEC_BATCH, HEADS * DK]),
                        ALU.mult).then_inc(s.ml_kwm_ready, 1)
                    taken(2)
                    for b in range(DEC_BATCH):
                        n = PT + b
                        dve.wait_ge(s.ml_c_ps, n + 1)
                        ps = M[:, b % 2, 0:2 * (DV + 1)].rearrange("p (q v) -> p q v", q=2)
                        for p in range(2):
                            ins = dve.scalar_tensor_tensor(out=m_Cin[:, b, p, :], in0=m_Cin[:, b, p, :], scalar=m_dec[:, p, n:n + 1],
                                                           in1=ps[:, p, :], op0=ALU.mult, op1=ALU.add)
                            if p == 0:
                                step(ins)
                        ins.then_inc(s.ml_c, 1)
                        if b % 4 == 3:
                            taken()
                    branch_dve(dve, step, 1, B[:, 4:8, :], taken)
                    taken.rest()

                def mlstm_pe(pe, fill):
                    fill(3)
                    branch_pe(pe, 0, fill)
                    fill(12)
                    pe.wait_ge(s.ml_ex, 1)
                    pe.wait_ge(s.tok_copied, TOK["mk"] + 5)
                    for i, n in enumerate(TILES):
                        for j, row in enumerate((r_a, r_d, r_en)):
                            mm = pe.matmul(M[0:n, 0, 12 * i + 4 * j:12 * i + 4 * j + 4], row[:, i * P:i * P + n], ident[0:HEADS, 0:HEADS],
                                           start=True, stop=True)
                    mm.then_inc(s.ml_col_ps, 1)
                    fill(1)
                    pe.wait_ge(s.ml_col, 1)
                    for p in range(2):
                        for half in range(2):
                            mm = pe.matmul(M[:, 2 * p + half, 0:HALF], selp[:, p, :], r_wi[:, half * HALF:(half + 1) * HALF],
                                           start=True, stop=True)
                        mm.then_inc(s.ml_wi_ps, 1)
                    fill(4)
                    pe.wait_ge(s.ml_wi, 2)
                    def decays_scores(i):
                        n, t0 = TILES[i], i * P
                        mask = big if n == P else sbig
                        for hd in range(HEADS):
                            dst = M[0:n, 0, hd * n:(hd + 1) * n]
                            pe.matmul(dst, ident[0:n, 0:n], mask[:, :], start=True, stop=False)
                            mm = pe.matmul(dst, sel[:, hd, 0:n], r_g[:, t0:t0 + n], start=False, stop=True)
                        mm.then_inc(s.ml_d_ps, 1)
                        if i:
                            fill(1)
                            pe.wait_ge(s.ml_c, i)
                        for hd in range(HEADS):
                            mm = pe.matmul(M[0:n, 1, hd * n:(hd + 1) * n], B[:, 2 + hd // 2, t0:t0 + n], m_qz[:, hd, t0:t0 + n],
                                           start=True, stop=True)
                        mm.then_inc(s.ml_s_ps, 1)

                    decays_scores(0)
                    fill(2)
                    for i in range(PT):
                        t0 = i * P
                        pe.wait_ge(s.ml_sd, i + 1)
                        pe.wait_ge(s.ml_kw, 1)
                        for hd in range(HEADS):
                            c0 = (hd // 2) * (DV + 1)
                            mm = pe.matmul(M[lo64[hd % 2], 1, c0:c0 + DV + 1], m_kw[:, i, hd, :], mv[:, i, hd, :],
                                           start=True, stop=True)
                        mm.then_inc(s.ml_c_ps, 1)
                        if i:
                            pe.wait_ge(s.ml_o, i)
                        for hd in range(HEADS):
                            c0 = (hd % 2) * (DV + 1)
                            dst = M[:, 2 + hd // 2, c0:c0 + DV + 1]
                            mm = pe.matmul(dst, m_SD[:, hd * P:(hd + 1) * P], mv[:, i, hd, :], start=True, stop=(i == 0))
                            if i:
                                mm = pe.matmul(dst, m_qwz[:, hd, t0:t0 + P], m_C[:, (i - 1) % 2, hd // 2, :], start=False, stop=True)
                        mm.then_inc(s.ml_n_ps, 1)
                        decays_scores(i + 1)
                        fill(1)
                        pe.wait_ge(s.ml_tok, i + 1)
                        for hd in range(HEADS):
                            mm = pe.transpose(M[:, 2, hd * P:(hd + 1) * P], m_tok[:, hd, :], ident[:, :])
                        mm.then_inc(s.ml_t_ps, 1)
                        fill(1)
                    i = PT
                    pe.wait_ge(s.ml_d, HEADS * (PT + 1))
                    for hd in range(HEADS):
                        mm = pe.matmul(M[:, 0, hd * NS:(hd + 1) * NS], sel[:, hd, :], r_en[:, SEQ:T], start=True, stop=True)
                    mm.then_inc(s.ml_e_ps, 1)
                    fill(1)
                    pe.wait_ge(s.ml_sd, PT + 1)
                    pe.wait_ge(s.ml_o, PT)
                    pe.wait_ge(s.ml_qn, 1)
                    for hd in range(HEADS):
                        pe.matmul(M[:, 2, hd * NS:(hd + 1) * NS], mv[0:NS, i, hd, 0:DV], m_SD[0:NS, hd * NS:(hd + 1) * NS],
                                  start=(hd == 0), stop=False, skip_group_check=True)
                    for b in range(DEC_BATCH):
                        for hd in range(HEADS):
                            q0 = b * DEC_SEQ
                            mm = pe.matmul(M[:, 2, hd * NS + q0:hd * NS + q0 + DEC_SEQ], m_Cin[:, b, hd // 2, 0:DV],
                                           m_qwz[:, hd, SEQ + q0:SEQ + q0 + DEC_SEQ], start=False,
                                           stop=(b == DEC_BATCH - 1), skip_group_check=True)
                    mm.then_inc(s.ml_n_ps, 1)
                    for hd in range(HEADS):
                        dst = M[:, 3, hd * NS:(hd + 1) * NS]
                        pe.matmul(dst, ones[0:NS, :], m_SD[0:NS, hd * NS:(hd + 1) * NS], start=True, stop=False)
                        mm = pe.matmul(dst, ones[:, :], m_qns[:, hd, :], start=False, stop=True)
                    mm.then_inc(s.ml_den_ps, 1)
                    fill(2)
                    pe.wait_ge(s.ml_kwm_ready, 1)
                    pe.wait_ge(s.ml_o, 5)
                    for b in range(DEC_BATCH):
                        if b >= 2:
                            pe.wait_ge(s.ml_c, PT + b - 1)
                        for hd in range(HEADS):
                            c0 = (hd // 2) * (DV + 1)
                            mm = pe.matmul(M[lo64[hd % 2], b % 2, c0:c0 + DV + 1], m_kwm[:, b, hd * DK:(hd + 1) * DK],
                                           mv[0:NS, PT, hd, :], start=True, stop=True)
                        mm.then_inc(s.ml_c_ps, 1)
                        fill(1)
                    fill(2)
                    branch_pe(pe, 1, fill)
                    fill.rest()

                def attention_act(act, step, gates):
                    act.wait_ge(s.lam_sum, 1)
                    act.activation(lam[:, 2:4], lam[:, 0:2], ACT.Exp).then_inc(s.lam_exp, 1)
                    to_tokens_act(act, TOK["dv"], lambda i, n: dv[0:n, i, :, :], HEADS * DV, HEADS)
                    for i, n in enumerate(TILES):
                        act.wait_ge(s.tok_ps, TOK["dk"] + i + 1)
                        if i:
                            act.wait_ge(s.kstore, 16 * i)
                        act.activation(d_kout[0:n, :], M[0:n, 2 + (TOK["dk"] + i) % 2, :], ACT.Copy).then_inc(s.tok_copied, 1)

                    gates(2)

                    def exps(n):
                        width = P * (n // HEADS + 1)
                        act.wait_ge(s.nm_ready, n + 1)
                        if n:
                            act.wait_ge(s.w_ready, n)
                        for m in range(2):
                            act.activation(d_e[:, m, 0:width], M[:, m, 0:width], ACT.Exp, bias=d_nm[:, m:m + 1],
                                           accum_out=d_l[:, m:m + 1]).then_inc(s.e_ready, 1)

                    def turned(n):
                        width = P * (n // HEADS + 1)
                        act.wait_ge(s.wt_ps, n + 1)
                        if n:
                            act.wait_ge(s.pv_ps, n)
                        act.activation(d_wT[:, 0:width], M[:, 2, 0:width], ACT.Copy).then_inc(s.wt_copied, 1)

                    for n in range(PT * HEADS + 1):
                        if n < PT * HEADS:
                            exps(n)
                        if n:
                            turned(n - 1)
                        if n % 4 == 3:
                            gates(2)
                    for g in range(2):
                        for j in range(4 * PAGES):
                            n = 4 * PAGES * g + j
                            act.wait_ge(s.tok_ps, TOK["page"] + n + 1)
                            if j % PAGES == 0 and n:
                                act.wait_ge(s.ss_ps, n // PAGES)
                            if n == 4 * PAGES + 7:
                                gates(2)
                            act.activation(d_KT[:, :, (j % PAGES) * PAGE:(j % PAGES + 1) * PAGE],
                                           M[:, 2 + n % 2, :].rearrange("p (h k) -> p h k", h=HEADS), ACT.Copy).then_inc(s.tok_copied, 1)
                        act.wait_ge(s.ss_nm, g + 1)
                        act.activation(d_es[:, :], M[:, 0, 0:2 * PAGE + NS], ACT.Exp, bias=d_nm[:, 0:1],
                                       accum_out=d_l[:, 0:1]).then_inc(s.ss_e, 1)
                        gates(2)
                    act.wait_ge(s.sp_copied, 2)
                    branch_act(act, step, 2, None)

                def attention_dve(dve, step, outputs):
                    for j in range(2):
                        step(dve.tensor_tensor(lamp[:, :], lamv[:, 2 * j, :], lamv[:, 2 * j + 1, :], ALU.mult))
                        step(dve.tensor_reduce(lam[:, j:j + 1], lamp[:, :], AX.X, ALU.add))
                    dve.sem_inc(s.lam_sum, 1)
                    dve.wait_ge(s.lam_exp, 1)
                    step(dve.tensor_tensor(lam[:, 4:5], lam[:, 3:4], lam[:, 2:3], ALU.subtract))
                    step(dve.tensor_tensor(lam[:, 5:6], lam[:, 4:5], lamc[:, 0:1], ALU.subtract))
                    step(dve.tensor_tensor(ghead[:, 2:3], ghead[:, 2:3], lamc[:, 1:2], ALU.mult))
                    step(dve.scalar_tensor_tensor(out=lam[:, 6:7], in0=sign[:, 1:2], scalar=lam[:, 5:6], in1=sign[:, 0:1],
                                                  op0=ALU.mult, op1=ALU.add))
                    dve.wait_ge(s.trig_in, 32)
                    for n in range(8):
                        ps, f = (M01 if n % 2 == 0 else M23), (DK ** -0.5 if n < 4 else 1.0)
                        dve.wait_ge(s.rope_ps, n + 1)
                        step(dve.scalar_tensor_tensor(out=halves(d_t1[:, :]), in0=ps, scalar=f, in1=halves(d_sin[:, :]),
                                                      op0=ALU.mult, op1=ALU.mult))
                        step(dve.scalar_tensor_tensor(out=C[:, n, :], in0=C[:, n, :], scalar=f, in1=d_cos[:, :],
                                                      op0=ALU.mult, op1=ALU.mult))
                        step(dve.tensor_tensor(C[:, n, :], C[:, n, :], d_t1[:, :], ALU.add))
                        dve.sem_inc(s.rope_done, 1)
                        if n in (5, 7):
                            outputs()
                    step(dve.memset(d_qbd[:, :, :, :, :], 0.0))
                    for m in range(2):
                        for hd in range(HEADS):
                            q0 = hd * 2 * DEC_SEQ + m * DEC_SEQ
                            flat = d_qbd[lo64[m], :, hd, :, :].rearrange("p b x y -> p b (x y)")
                            step(dve.tensor_copy(flat[:, :, q0:q0 + DEC_SEQ],
                                                 C[lo64[m], hd, SEQ:T].rearrange("p (b t) -> p b t", b=DEC_BATCH)))
                    dve.sem_inc(s.qbd_ready, 1)

                    def maxima(n):
                        width = P * (n // HEADS + 1)
                        dve.wait_ge(s.sc_ps, n + 1)
                        if n:
                            dve.wait_ge(s.e_ready, 2 * n)
                        dve.tensor_reduce(d_nm[:, 0:2], M[:, 0:2, 0:width], AX.X, ALU.max, negate=True).then_inc(s.nm_ready, 1)

                    def weights(n):
                        width = P * (n // HEADS + 1)
                        dve.wait_ge(s.e_ready, 2 * n + 2)
                        if n:
                            dve.wait_ge(s.wt_ps, n)
                        step(dve.reciprocal(d_rc[:, :], d_l[:, :]))
                        step(dve.tensor_tensor(d_rc[:, 1:2], d_rc[:, 1:2], lam[:, 5:6], ALU.mult))
                        step(dve.tensor_scalar(d_w[:, 0:width], d_e[:, 0, 0:width], d_rc[:, 0:1], None, ALU.mult))
                        dve.scalar_tensor_tensor(out=d_w[:, 0:width], in0=d_e[:, 1, 0:width], scalar=d_rc[:, 1:2],
                                                 in1=d_w[:, 0:width], op0=ALU.mult, op1=ALU.add).then_inc(s.w_ready, 1)

                    def values(n):
                        i, hd = n // HEADS, n % HEADS
                        dve.wait_ge(s.pv_ps, n + 1)
                        dve.tensor_copy(oraw[2][:, hd, i * P:(i + 1) * P], M[:, 3, 0:P]).then_inc(s.pv_copied, 1)

                    for n in range(PT * HEADS + 2):
                        if n < PT * HEADS:
                            maxima(n)
                            weights(n)
                        if n >= 2:
                            values(n - 2)
                        if n < PT * HEADS:
                            outputs()
                    for g in range(2):
                        outputs(3 + g)
                        dve.wait_ge(s.ss_ps, 4 * (g + 1))
                        if g == 0:
                            dve.wait_ge(s.e_ready, 2 * PT * HEADS)
                            dve.wait_ge(s.w_ready, PT * HEADS)
                        dve.tensor_reduce(d_nm[:, 0:1], M[:, 0, 0:2 * PAGE + NS], AX.X, ALU.max, negate=True).then_inc(s.ss_nm, 1)
                        dve.wait_ge(s.ss_e, g + 1)
                        step(dve.reciprocal(d_rc[:, 0:1], d_l[:, 0:1]))
                        step(dve.tensor_tensor(d_rc[:, 0:1], d_rc[:, 0:1], lam[:, 6:7], ALU.mult))
                        dve.tensor_scalar(d_es[:, :], d_es[:, :], d_rc[:, 0:1], None, ALU.mult).then_inc(s.ss_w, 1)
                        dve.wait_ge(s.st_ps, g + 1)
                        for pg in range(PAGES):
                            v = M[:, 1, pg * P:(pg + 1) * P].rearrange("p (j h c t) -> p (j h) t c", j=4, h=HEADS, c=2)
                            step(dve.tensor_reduce(d_wTs[:, pg, :, :, :].rearrange("p j h t -> p (j h) t"), v, AX.X, ALU.add))
                        v = M[0:NS, 1, 2 * P:3 * P].rearrange("p (j h c t) -> p (j h) t c", j=4, h=HEADS, c=2)
                        dve.tensor_reduce(d_wTn[:, :, :, :].rearrange("p j h t -> p (j h) t"), v, AX.X, ALU.add).then_inc(s.st_red, 1)
                        outputs(2)
                        dve.wait_ge(s.sp_ps, g + 1)
                        dve.tensor_copy(oraw[2][:, :, SEQ + 16 * g:SEQ + 16 * (g + 1)],
                                        M[:, 0, 2 * PAGE + NS:2 * PAGE + NS + 64].rearrange("p (h t) -> p h t", h=HEADS)
                                        ).then_inc(s.sp_copied, 1)
                    outputs(2 * 16 - outputs.n)
                    branch_dve(dve, step, 2, None, outputs)

                def attention_pe(pe, fill):
                    pe.wait_ge(s.out_taken, OUT["df"] + 12)
                    to_tokens_pe(pe, TOK["dv"], [dvf[:, m, :] for m in range(4)])
                    for n in range(8):
                        if n >= 2:
                            fill(1)
                            pe.wait_ge(s.rope_done, n - 1)
                        if n == 1:
                            pe.wait_ge(s.tok_copied, TOK["dv"] + 5)
                        for half in range(2):
                            mm = pe.matmul(M[:, 2 * (n % 2) + half, 0:HALF], rot[:, :], C[:, n, half * HALF:(half + 1) * HALF],
                                           start=True, stop=True)
                        mm.then_inc(s.rope_ps, 1)
                    fill(6)
                    pe.wait_ge(s.rope_done, 8)
                    to_tokens_pe(pe, TOK["dk"], [C[:, 4 + m, :] for m in range(4)])

                    def scores(n):
                        i, hd = n // HEADS, n % HEADS
                        if n:
                            pe.wait_ge(s.e_ready, 2 * n)
                        for m in range(2):
                            r = lo64[m]
                            pe.matmul(M[:, m, 0:(i + 1) * P], C[r, hd, i * P:(i + 1) * P], C[r, 4 + hd, 0:(i + 1) * P],
                                      start=True, stop=False)
                            mm = pe.matmul(M[:, m, i * P:(i + 1) * P], ident[:, :], neg[:, :], start=False, stop=True)
                        mm.then_inc(s.sc_ps, 1)

                    def turn(n):
                        i = n // HEADS
                        fill(2)
                        pe.wait_ge(s.w_ready, n + 1)
                        pe.wait_ge(s.tok_copied, TOK["dk"] + 5)
                        if n:
                            pe.wait_ge(s.wt_copied, n)
                        for j in range(i + 1):
                            mm = pe.transpose(M[:, 2, j * P:(j + 1) * P], d_w[:, j * P:(j + 1) * P], ident[:, :])
                        mm.then_inc(s.wt_ps, 1)

                    def value(n):
                        i, hd = n // HEADS, n % HEADS
                        fill(1)
                        pe.wait_ge(s.wt_copied, n + 1)
                        if n:
                            pe.wait_ge(s.pv_copied, n)
                        for j in range(i + 1):
                            mm = pe.matmul(M[:, 3, 0:P], dv[:, j, hd, :], d_wT[:, j * P:(j + 1) * P],
                                           start=(j == 0), stop=(j == i))
                        mm.then_inc(s.pv_ps, 1)

                    for n in range(PT * HEADS + 1):
                        if n < PT * HEADS:
                            scores(n)
                        if n:
                            turn(n - 1)
                            value(n - 1)
                    pe.wait_ge(s.qbd_ready, 1)
                    pe.wait_ge(s.e_ready, 2 * PT * HEADS)
                    pe.wait_ge(s.pv_copied, PT * HEADS)
                    for g in range(2):
                        if g:
                            pe.wait_ge(s.sp_copied, g)
                        for j in range(4):
                            b = 4 * g + j
                            for pg in range(PAGES):
                                n = PAGES * b + pg
                                pe.wait_ge(s.page[n % 2], 16 * (n // 2 + 1))
                                pe.wait_ge(s.tok_copied, TOK["page"] + n - 1)
                                for hd in range(HEADS):
                                    mm = pe.transpose(M[:, 2 + n % 2, hd * P:(hd + 1) * P], d_kr[:, n % 2, hd, :], ident[:, :])
                                mm.then_inc(s.tok_ps, 1)
                                fill(1)
                            pe.wait_ge(s.tok_copied, TOK["page"] + PAGES * (b + 1))
                            rows = slice(32 * j, 32 * (j + 1))
                            for hd in range(HEADS):
                                q = d_qbd[:, b, hd, :, :].rearrange("p x y -> p (x y)")
                                pe.matmul(M[rows, 0, 0:2 * PAGE], q, d_KT[:, hd, :], start=(hd == 0), stop=False,
                                          skip_group_check=True)
                                pe.matmul(M[rows, 0, 2 * PAGE:2 * PAGE + NS], q, C[:, 4 + hd, SEQ:T], start=False, stop=False,
                                          skip_group_check=True)
                            mm = pe.matmul(M[rows, 0, 2 * PAGE:2 * PAGE + NS], ident[:, 32 * j:32 * (j + 1)], sneg[:, g, :],
                                           start=False, stop=True, skip_group_check=True)
                            mm.then_inc(s.ss_ps, 1)
                        fill(2)
                        pe.wait_ge(s.ss_w, g + 1)
                        for pg in range(PAGES):
                            pe.transpose(M[:, 1, pg * P:(pg + 1) * P], d_es[:, pg * P:(pg + 1) * P], ident[:, :])
                        pe.transpose(M[0:NS, 1, 2 * P:3 * P], d_es[:, 2 * P:2 * P + NS], ident[:, :]).then_inc(s.st_ps, 1)
                        fill(1)
                        pe.wait_ge(s.st_red, g + 1)
                        base = 2 * PAGE + NS
                        for hd in range(HEADS):
                            pe.matmul(M[:, 0, base + 16 * hd:base + 16 * (hd + 1)], dv[0:NS, PT, hd, :], d_wTn[:, :, hd, :],
                                      start=(hd == 0), stop=False, skip_group_check=True)
                        for j in range(4):
                            for pg in range(PAGES):
                                n = PAGES * (4 * g + j) + pg
                                pe.wait_ge(s.vpage[n % 2], 16 * (n // 2 + 1))
                                if pg:
                                    fill(1)
                                for hd in range(HEADS):
                                    c0 = base + 16 * hd + DEC_SEQ * j
                                    mm = pe.matmul(M[:, 0, c0:c0 + DEC_SEQ], d_V[:, n % 2, hd * DV:(hd + 1) * DV],
                                                   d_wTs[:, pg, j, hd, :], start=False, stop=(j == 3 and pg == 1),
                                                   skip_group_check=True)
                                mm.then_inc(s.v_used, 1)
                        pe.matmul(M[0:1, 1, 500:502], ones[:, 0:1], ones[:, 0:2], start=True, stop=True).then_inc(s.sp_ps, 1)
                    fill(2 * 48 - fill.n)
                    branch_pe(pe, 2, fill)

                def gate_sigmoid(act, b, m):
                    act.wait_ge(s.u_lin, KD * b + m + 1)
                    act.activation(u_g[:, m % 2, :], u_g[:, m % 2, :], ACT.Sigmoid).then_inc(s.u_sig, 1)

                def merge_output(dve, step, b, at):
                    q, kind = at // 4, at % 4
                    n, out, m = CHUNK[f"merge{b}"] + 3 * q, OUT[f"merge{b}"] + at, 2 * q + kind % 2
                    done, u = KD * b + m, u_g[:, m % 2, :]
                    if kind < 2:
                        if at == 0 and b == 0:
                            dve.wait_ge(s.tok_copied, TOK["dv"] + 5)
                        dve.wait_ge(s.chunk_done, n + kind + 1)
                        if done >= 2:
                            dve.wait_ge(s.u_mul, done - 1)
                        dve.tensor_tensor(halves(u), out2(out % 2), halves(rB[:, :]), ALU.mult).then_inc(s.u_lin, 1)
                        dve.wait_ge(s.u_lin, done + 1)
                        dve.sem_inc(s.out_taken, 1)
                        return
                    dve.wait_ge(s.u_sig, done + 1)
                    if kind == 2:
                        dve.wait_ge(s.first_done, done // 2 + 1)
                    else:
                        dve.wait_ge(s.chunk_done, n + 3)
                    if b == 0:
                        step(dve.tensor_tensor(halves(MG[:, m, :]), out2(out % 2), halves(u), ALU.mult))
                        dve.sem_inc(s.out_taken, 1)
                        dve.sem_inc(s.u_mul, 1)
                    else:
                        step(dve.tensor_tensor(halves(u), out2(out % 2), halves(u), ALU.mult))
                        dve.sem_inc(s.out_taken, 1)
                        dve.tensor_tensor(MG[:, m, :], MG[:, m, :], u, ALU.add).then_inc(s.mg_ready, 1)
                        dve.wait_ge(s.mg_ready, KD * (b - 1) + m + 1)
                        dve.sem_inc(s.u_mul, 1)

                def merge_piece(pe, b, at):
                    c, part = at // 4, at % 4
                    q, kind = c // 3, c % 3
                    n, out = CHUNK[f"merge{b}"] + c, OUT[f"merge{b}"] + 4 * q
                    if part == 0:
                        pe.wait_ge(s.wl_split, n + 1)
                    if at == 8:
                        pe.wait_ge(s.bn_l, b + 1)
                    if kind < 2:
                        out += kind
                        blocks = [(2 * part, 2 * part), (2 * part + 1, 2 * part + 1)]
                        begin, end, hi, lo = part == 0, part == 3, xH, xL
                    else:
                        o, part = part // 2, part % 2
                        out += 2 + o
                        blocks = [(2 * k + o, k) for k in (2 * part, 2 * part + 1)]
                        begin, end, hi, lo = part == 0, part == 1, oH[b], oL[b]
                    if begin:
                        pe.wait_ge(s.out_taken, out - 1)
                    mm = blocks_product(pe, n, out % 2, hi, lo, blocks, begin, end)
                    if end:
                        mm.then_inc(s.first_done if kind == 2 and o == 0 else s.chunk_done, 1)

                def merged_act(act):
                    act.wait_ge(s.chunk_done, CHUNK["merge2"])
                    for m in range(KD):
                        act.wait_ge(s.mg_ready, KD + m + 1)
                        act.activation(mH[:, m, :], MG[:, m, :], ACT.Copy).then_inc(s.mh_ready, 1)
                    act.wait_ge(s.ml_split, KD)
                    act.dma_start(h[:, :, :], spill).then_inc(s.h_back, 16)

                def merged_dve(dve):
                    for m in range(KD):
                        dve.wait_ge(s.mh_ready, m + 1)
                        dve.tensor_tensor(mL[:, m, :], MG[:, m, :], mH[:, m, :].bitcast(F32), ALU.subtract).then_inc(s.ml_split, 1)

                def add_to_h(dve, n, name, sem, gain, per=1):
                    if n == 1:
                        dve.wait_ge(s.h_back, 16)
                    for m in range(KD):
                        dve.wait_ge(s.chunk_done, CHUNK[name] + per * (m + 1))
                        dve.tensor_tensor(halves(h[:, m, :]), out2((OUT[name] + m) % 2), halves(h[:, m, :]), ALU.add).then_inc(sem, 1)
                        dve.wait_ge(sem, m + 1)
                        dve.sem_inc(s.out_taken, 1)
                        if m:
                            x_low(dve, n, m - 1, gain)
                    x_low(dve, n, KD - 1, gain)

                def embed_pe(pe):
                    pe.wait_ge(s.ptok_in, 32)
                    pe.wait_ge(s.bn_ln, 12)
                    for m in range(KP):
                        for i, n in enumerate(TILES):
                            mm = pe.transpose(M[:, 2 * m + i // PT, (i % PT) * P:(i % PT) * P + n],
                                              p_tok[0:n, i, m * P:(m + 1) * P], ident[0:n, 0:n])
                    mm.then_inc(s.p_ps, 1)

                def embed_act(act):
                    act.wait_ge(s.p_copied, 1)
                    act.activation(pH[:, :, :], p_raw[:, :, :], ACT.Copy).then_inc(s.ph_ready, 1)

                def embed_dve(dve, step):
                    dve.wait_ge(s.p_ps, 1)
                    for m in range(KP):
                        step(dve.tensor_copy(p_raw[:, m, 0:SEQ], M[:, 2 * m, :]))
                        step(dve.tensor_copy(p_raw[:, m, SEQ:T], M[:, 2 * m + 1, 0:NS]))
                    dve.sem_inc(s.p_copied, 1)
                    dve.wait_ge(s.ph_ready, 1)
                    dve.tensor_tensor(pL[:, :, :], p_raw[:, :, :], pH[:, :, :].bitcast(F32), ALU.subtract).then_inc(s.pl_ready, 1)

                def ffn_act(act):
                    base = CHUNK["ffn"]

                    def high(j, i):
                        n = base + j
                        act.wait_ge(s.w_in[n % RAW], w_count(n, i, 4))
                        act.wait_ge(s.chunk_done, n + 4 * i - (SPLIT - 1))
                        act.activation(wH[n % SPLIT][:, :, :], raw[n % RAW][:, :, :], ACT.Copy).then_inc(s.wh_split, 1)

                    def silu(u, at):
                        act.wait_ge(s.f_lin, at + 1)
                        act.activation(f_g[:, u, :], f_g[:, u, :], ACT.Silu).then_inc(s.f_silu, 1)

                    def hidden(u, at):
                        act.wait_ge(s.f_hid, at + 1)
                        blk = hidH[:, at:at + 1, :] if isinstance(at, int) else hidH[:, bass.ds(at, 1), :]
                        act.activation(blk.rearrange("p o n -> p (o n)"), f_u[:, u, :], ACT.Copy).then_inc(s.fh_ready, 1)

                    high(2, 0)
                    silu(0, 0)
                    high(3, 0)
                    hidden(0, 0)
                    with act.Fori(1, KF // 2) as i:
                        high(0, i)
                        silu(1, 2 * i - 1)
                        high(1, i)
                        hidden(1, 2 * i - 1)
                        high(2, i)
                        silu(0, 2 * i)
                        high(3, i)
                        hidden(0, 2 * i)
                    high_chunk(act, CHUNK["down"], DOWN_K[0][1])
                    silu(1, KF - 1)
                    high_chunk(act, CHUNK["down"] + 1, DOWN_K[1][1])
                    hidden(1, KF - 1)

                def ffn_dve(dve):
                    base, out = CHUNK["ffn"], OUT["ffn"]

                    def unit(u, at):
                        dve.wait_ge(s.chunk_done, base + 2 * at + 1)
                        dve.tensor_tensor(halves(f_g[:, u, :]), out2(out % 2), halves(rB[:, :]), ALU.mult).then_inc(s.f_lin, 1)
                        dve.wait_ge(s.f_lin, at + 1)
                        dve.sem_inc(s.out_taken, 1)
                        dve.wait_ge(s.chunk_done, base + 2 * at + 2)
                        dve.tensor_tensor(halves(f_u[:, u, :]), out2((out + 1) % 2), halves(rB[:, :]), ALU.mult
                                          ).then_inc(s.out_taken, 1)
                        dve.wait_ge(s.out_taken, out + 2 * at + 2)
                        dve.wait_ge(s.f_silu, at + 1)
                        dve.tensor_tensor(f_u[:, u, :], f_u[:, u, :], f_g[:, u, :], ALU.mult).then_inc(s.f_hid, 1)

                    def low(u, at):
                        dve.wait_ge(s.fh_ready, at + 1)
                        one = isinstance(at, int)
                        lo, hi = (x[:, at:at + 1, :] if one else x[:, bass.ds(at, 1), :] for x in (hidL, hidH))
                        dve.tensor_tensor(lo.rearrange("p o n -> p (o n)"), f_u[:, u, :],
                                          hi.rearrange("p o n -> p (o n)").bitcast(F32), ALU.subtract).then_inc(s.fl_ready, 1)
                        dve.wait_ge(s.fl_ready, at + 1)

                    unit(0, 0)
                    unit(1, 1)
                    low(0, 0)
                    with dve.Fori(1, KF // 2) as i:
                        unit(0, 2 * i)
                        low(1, 2 * i - 1)
                        unit(1, 2 * i + 1)
                        low(0, 2 * i)
                    low(1, KF - 1)

                def ple_act(act):
                    base = CHUNK["ple"]
                    for at in range(2, 2 + KD + 2):
                        if at < 2 + KD:
                            high_chunk(act, base + at)
                        m = at - 4
                        if m >= 0:
                            act.wait_ge(s.e_lin, m + 1)
                            act.activation(e_g[:, m % 2, :], e_g[:, m % 2, :], ACT.Sigmoid).then_inc(s.e_sig, 1)

                def proj_dve(dve):
                    for m in range(KD):
                        dve.wait_ge(s.proj_done, m + 1)
                        dve.tensor_copy(halves(e_p[:, m, :]), out2((OUT["ple"] + m) % 2)).then_inc(s.proj_taken, 1)
                        dve.wait_ge(s.proj_taken, m + 1)
                        dve.sem_inc(s.out_taken, 1)

                def ple_dve(dve, step):
                    out = OUT["ple"]
                    for m in range(KD + 1):
                        if m < KD:
                            dve.wait_ge(s.chunk_done, CHUNK["ple"] + 2 + m + 1)
                            if m >= 2:
                                dve.wait_ge(s.e_mul, m - 1)
                            dve.tensor_tensor(halves(e_g[:, m % 2, :]), out2((out + m) % 2), halves(rB[:, :]), ALU.mult).then_inc(s.e_lin, 1)
                            dve.wait_ge(s.e_lin, m + 1)
                            dve.sem_inc(s.out_taken, 1)
                        if m:
                            u = m - 1
                            dve.wait_ge(s.e_sig, u + 1)
                            dve.tensor_tensor(e_p[:, u, :], e_p[:, u, :], e_g[:, u % 2, :], ALU.mult).then_inc(s.e_mul, 1)
                            dve.wait_ge(s.e_mul, u + 1)
                            dve.tensor_tensor(h[:, u, :], h[:, u, :], e_p[:, u, :], ALU.add).then_inc(s.h_ple, 1)

                def proj_pe(pe):
                    for q in range(2):
                        n = CHUNK["ple"] + q
                        pe.wait_ge(s.wl_split, n + 1)
                        for o_at in range(4):
                            out = OUT["ple"] + 4 * q + o_at
                            pe.wait_ge(s.out_taken, out - 1)
                            mm = blocks_product(pe, n, out % 2, pH, pL, [(4 * k + o_at, k) for k in range(KP)], True, True)
                            mm.then_inc(s.proj_done, 1)
                        pe.wait_ge(s.proj_done, 4 * (q + 1))
                        pe.sem_inc(s.chunk_done, 1)

                def down_pe(pe):
                    def output(m, i, per):
                        for j, (k0, kb) in enumerate(DOWN_K):
                            n = CHUNK["down"] + 4 * m + j
                            pe.wait_ge(s.wl_split, n + 1 + 4 * per * i)
                            if j == 0:
                                pe.wait_ge(s.out_taken, OUT["down"] + m - 1 + per * i)
                            mm = blocks_product(pe, n, (OUT["down"] + m) % 2, hidH, hidL, [(k, k0 + k) for k in range(kb)],
                                                j == 0, j == 3)
                            mm.then_inc(s.chunk_done, 1)

                    output(0, 0, 0)
                    output(1, 0, 0)
                    stat(pe, 2, 0, sq2)
                    with pe.Fori(1, KD // 2) as i:
                        output(0, i, 2)
                        for odd in range(2):
                            pe.wait_ge(s.sq_ready, 2 * KD + 2 * i + odd)
                            for half in range(2):
                                mm = pe.matmul(M[:, half, 0:HALF], ones[:, :], sq2[:, 1 - odd, half * HALF:(half + 1) * HALF],
                                               start=False, stop=False, skip_group_check=True)
                            mm.then_inc(s.sq_used, 1)
                            if not odd:
                                output(1, i, 2)

                @block.scalar
                def _(act):
                    step = Steps(act, s.act_step)
                    act.wait_ge(s.gain_in, 16 * 3)
                    high_chunk(act, 0)
                    high_chunk(act, 1)
                    for k in range(KD):
                        x_high(act, 0, k, sq0, gains[:, 0, :])
                    norm_factor(act, step, 0)
                    high_loop(act, "gla", 12)
                    high_chunk(act, CHUNK["small"])
                    act.wait_ge(s.par_in, 16 * 10)
                    gla_act(act, step)
                    mlstm_act(act, step)
                    gates = Between(lambda n: gate_sigmoid(act, n // KD, n % KD), 3 * KD)
                    attention_act(act, step, gates)
                    gates(2)
                    embed_act(act)
                    gates.rest()
                    act.wait_ge(s.wl_split, CHUNK["out"])
                    for j in range(SPLIT):
                        high_chunk(act, CHUNK["out"] + j)
                    merged_act(act)
                    for m in range(KD):
                        if m < KD - SPLIT:
                            high_chunk(act, CHUNK["out"] + SPLIT + m)
                        else:
                            high_chunk(act, CHUNK["ffn"] + m - (KD - SPLIT))
                        x_high(act, 1, m, sq1, gains[:, 1, :], s.h_mix)
                    norm_factor(act, step, 1)
                    ffn_act(act)
                    for n in range(SPLIT, 4 * KD + SPLIT):
                        if n < 4 * KD:
                            high_chunk(act, CHUNK["down"] + n, DOWN_K[n % 4][1])
                        else:
                            high_chunk(act, CHUNK["ple"] + n - 4 * KD)
                        if n % 4 == 1 and n > SPLIT:
                            x_high(act, 2, n // 4 - 1, sq2, gains[:, 2, :], s.h_ffn)
                    norm_factor(act, step, 2)
                    ple_act(act)

                @block.tensor
                def _(pe):
                    def x_and_stat(k):
                        if k:
                            stat(pe, 0, k - 1, sq0)
                        pe.wait_ge(s.xl_ready, k + 1)

                    panel_chunk(pe, 0, 0, xH, xL, before=x_and_stat)
                    stat(pe, 0, KD - 1, sq0)
                    stats_done(pe, 0)
                    panel_chunk(pe, 1, 1, xH, xL)
                    panel_loop(pe, "gla", 12, xH, xL, 2)
                    pe.wait_ge(s.par_in, 16 * 10)
                    panel_chunk(pe, CHUNK["small"], OUT["small"], xH, xL)
                    gla_pe(pe, Between(lambda n: panel_piece(pe, "ml", n), 48))
                    mlstm_pe(pe, Between(lambda n: panel_piece(pe, "df", n), 48))
                    fill = Between(lambda n: merge_piece(pe, n // 48, n % 48), 3 * 48)
                    attention_pe(pe, fill)
                    fill(4)
                    embed_pe(pe)
                    fill.rest()
                    panel_chunk(pe, CHUNK["out"], OUT["out"], mH, mL, before=lambda k: pe.wait_ge(s.ml_split, k + 1))
                    for m in range(1, KD):
                        panel_chunk(pe, CHUNK["out"] + m, OUT["out"] + m, mH, mL)
                        stat(pe, 1, m - 1, sq1)
                    panel_chunk(pe, CHUNK["ffn"], OUT["ffn"], xH, xL, before=x_there(pe, 1))
                    stat(pe, 1, KD - 1, sq1)
                    stats_done(pe, 1)
                    panel_chunk(pe, CHUNK["ffn"] + 1, OUT["ffn"] + 1, xH, xL)
                    panel_loop(pe, "ffn", 2 * KF, xH, xL, 2)
                    pe.wait_ge(s.fl_ready, KF)
                    down_pe(pe)
                    pe.wait_ge(s.pl_ready, 1)
                    proj_pe(pe)
                    stat(pe, 2, KD - 1, sq2)
                    stats_done(pe, 2)
                    for m in range(KD):
                        panel_chunk(pe, CHUNK["ple"] + 2 + m, OUT["ple"] + KD + m, xH, xL, before=x_there(pe, 2) if m == 0 else None)

                @block.vector
                def _(dve):
                    step = Steps(dve, s.dve_step)
                    dve.wait_ge(s.gain_in, 16 * 3)
                    for k in range(KD):
                        x_low(dve, 0, k, gains[:, 0, :])
                    dve.wait_ge(s.par_in, 16 * 10)
                    dve.wait_ge(s.r_ready, 1)
                    gla_dve(dve, step)
                    mlstm_dve(dve, step)
                    outputs = Between(lambda n: merge_output(dve, step, n // 16, n % 16), 48)
                    attention_dve(dve, step, outputs)
                    embed_dve(dve, step)
                    outputs.rest()
                    merged_dve(dve)
                    add_to_h(dve, 1, "out", s.h_mix, gains[:, 1, :])
                    dve.wait_ge(s.r_ready, 2)
                    ffn_dve(dve)
                    add_to_h(dve, 2, "down", s.h_ffn, gains[:, 2, :], 4)
                    proj_dve(dve)
                    dve.wait_ge(s.r_ready, 3)
                    ple_dve(dve, step)

            clear_all()

        with nc.Block() as block:

            @block.scalar
            def _(act):
                step = Steps(act, s.act_step)
                for k in range(KD):
                    if k >= 2:
                        act.wait_ge(s.sq_used, k - 1)
                    act.activation(sq0[:, k % 2, :], h[:, k, :], ACT.Square).then_inc(s.sq_ready, 1)
                norm_factor(act, step, 0)

            @block.vector
            def _(dve):
                dve.wait_ge(s.r_ready, 1)
                for k in range(KD):
                    dve.scalar_tensor_tensor(out=y_f[:, k, :], in0=h[:, k, :], scalar=gfin[:, k:k + 1], in1=rB[:, :],
                                             op0=ALU.mult, op1=ALU.mult).then_inc(s.y_ready, 1)
                for i, n in enumerate(TILES):
                    for half in range(2):
                        dve.wait_ge(s.y_ps, 2 * i + half + 1)
                        dve.tensor_copy(io_tok[0:n, i, half * 512:(half + 1) * 512], M[0:n, 2 * (i % 2) + half, :]).then_inc(s.io_copied, 1)

            @block.tensor
            def _(pe):
                for k in range(KD):
                    stat(pe, 0, k, sq0)
                stats_done(pe, 0)
                pe.wait_ge(s.y_ready, KD)
                for i, n in enumerate(TILES):
                    for half in range(2):
                        if i >= 2:
                            pe.wait_ge(s.io_copied, 2 * (i - 2) + half + 1)
                        for k in range(4):
                            mm = pe.transpose(M[0:n, 2 * (i % 2) + half, k * P:(k + 1) * P], y_f[:, 4 * half + k, i * P:i * P + n],
                                              ident[:, :])
                        mm.then_inc(s.y_ps, 1)

            @block.sync
            def _(sp):
                for i, n in enumerate(TILES):
                    sp.wait_ge(s.io_copied, 2 * (i + 1))
                    dst = o["y_prompt"][0, i * P:(i + 1) * P, :] if n == P else o["y_sample"].rearrange("b t d -> (b t) d")
                    sp.dma_start(dst, io_tok[0:n, i, :]).then_inc(s.io_out, 16)
                sp.wait_ge(s.io_out, 16 * 5)


_INS = ["x_prompt", "x_sample", "cache_k", "cache_v", "state_gla", "state_mlstm_c", "state_mlstm_n", "state_mlstm_m",
        "page_table", "p_prompt", "p_sample", "g_mix", "w_in", "w_gla_gk", "b_gla_gk", "g_gla_norm", "b_mlstm_if",
        "g_mlstm_norm", "diff_lambda", "g_diff_norm", "w_branch", "w_gate", "w_out", "g_ffn", "w_ffn_gate", "w_ffn_up",
        "w_ffn_down", "g_ple", "w_ple_gate", "w_ple_proj", "g_final"]
_OUTS = [("y_prompt", (1, SEQ, D)), ("y_sample", (DEC_BATCH, DEC_SEQ, D)),
         ("k_prompt", (DEPTH, 1, SEQ, 2 * HEADS, DK)), ("v_prompt", (DEPTH, 1, SEQ, HEADS, DV)),
         ("gla_prompt", (DEPTH, 1, HEADS, DK, DV)), ("c_prompt", (DEPTH, 1, HEADS, DK, DV)),
         ("n_prompt", (DEPTH, 1, HEADS, DK)), ("m_prompt", (DEPTH, 1, HEADS)),
         ("k_sample", (DEPTH, DEC_BATCH, DEC_SEQ, 2 * HEADS, DK)), ("v_sample", (DEPTH, DEC_BATCH, DEC_SEQ, HEADS, DV)),
         ("gla_sample", (DEPTH, DEC_BATCH, HEADS, DK, DV)), ("c_sample", (DEPTH, DEC_BATCH, HEADS, DK, DV)),
         ("n_sample", (DEPTH, DEC_BATCH, HEADS, DK)), ("m_sample", (DEPTH, DEC_BATCH, HEADS))]


def constants():
    import math
    import numpy as np
    f = np.float32
    i = np.arange(P)
    k = {"ident": np.eye(P), "ones": np.ones((P, P)), "epsc": np.full((P, 1), EPS)}
    k["big"] = np.where(i[:, None] > i[None, :], BIG, 0.0)
    k["neg"] = np.where(i[None, :] > i[:, None], -BIG, 0.0)
    k["gmask"] = (i[:, None] // CH == i[None, :] // CH) & (i[:, None] <= i[None, :])
    n = np.arange(NS)
    seen = (n[:, None] // DEC_SEQ == n[None, :] // DEC_SEQ) & (n[:, None] <= n[None, :])
    k["smask"] = seen
    k["sbig"] = np.where(seen, 0.0, BIG)
    row_seq, row_t = i // NS, i % DEC_SEQ
    k["sneg"] = np.stack([np.where(seen[:, (4 * g + row_seq) * DEC_SEQ + row_t].T, 0.0, -BIG) for g in range(2)], 1)
    k["sel"] = np.repeat(np.eye(HEADS)[:, :, None], P, 2)
    k["selp"] = np.stack([(np.arange(HEADS)[:, None] == 2 * p + i[None, :] // DK) for p in range(2)], 1)
    k["seqm"] = (n[:, None] // DEC_SEQ == np.arange(DEC_BATCH)[None, :])
    k["sign"] = np.stack([(i // DEC_SEQ) % 2 == 0, (i // DEC_SEQ) % 2 == 1], 1)
    half = DK // 8
    rot = np.zeros((P, P))
    for h0 in (0, DK):
        for j in range(half):
            rot[h0 + half + j, h0 + j] = -1.0
            rot[h0 + j, h0 + half + j] = 1.0
    k["rot"] = rot
    pos = np.concatenate([np.arange(SEQ), PAGE * PAGES + n % DEC_SEQ]).astype(f)
    inv = f(500000.0) ** (-np.arange(half, dtype=f) * f(2.0) / f(2 * half))
    ang = (pos[:, None] * inv[None, :]).astype(f)
    cos, sin = np.ones((P, T), f), np.zeros((P, T), f)
    for h0 in (0, DK):
        for q in range(2):
            cos[h0 + half * q:h0 + half * (q + 1)] = np.cos(ang).T
            sin[h0 + half * q:h0 + half * (q + 1)] = np.sin(ang).T
    k["cos"], k["sin"] = cos, sin
    t = np.arange(SEQ)
    k["greset"] = np.repeat(np.concatenate([t % CH != 0, n % DEC_SEQ != 0])[None], P, 0)
    k["rreset"] = np.repeat(np.concatenate([t % P != 0, n % DEC_SEQ != 0])[None], HEADS, 0)
    init = [0.8 - 0.6 * math.exp(-0.3 * layer) for layer in range(DEPTH)]
    k["lamc"] = np.repeat(np.array([[x, 1.0 - x] for x in init])[:, None, :], P, 1)
    return {name: np.ascontiguousarray(v, dtype=f) for name, v in k.items()}


def kernel(**inputs):
    import numpy as _np
    import concourse.bacc as _bacc
    from concourse import mybir as _mybir
    from concourse.bass_utils import run_bass_kernel_spmd as _run

    nc = _bacc.Bacc("TRN2", target_bir_lowering=False, num_devices=1)
    arrays, args, consts, outs = {}, {}, {}, {}
    for name in _INS:
        x = _np.ascontiguousarray(inputs[name])
        arrays[f"in_{name}"] = x
        args[name] = nc.dram_tensor(f"in_{name}", x.shape, _mybir.dt.from_np(x.dtype), kind="ExternalInput").ap()
    for name, x in constants().items():
        arrays[f"const_{name}"] = x
        consts[name] = nc.dram_tensor(f"const_{name}", x.shape, _mybir.dt.from_np(x.dtype), kind="ExternalInput").ap()
    for name, shape in _OUTS:
        outs[name] = nc.dram_tensor(f"out_{name}", shape, F32, kind="ExternalOutput").ap()
    outs["spill"] = nc.dram_tensor("spill", (P, KD, T), F32).ap()
    program(nc, args, consts, outs)
    r = _run(nc, [arrays], core_ids=[0])
    return tuple(r.results[0][f"out_{name}"] for name, _ in _OUTS)
```

```python
from contextlib import ExitStack

import concourse.bass as bass
from concourse import mybir

F32 = mybir.dt.float32
F32R = mybir.dt.float32r
I32 = mybir.dt.int32
ALU = mybir.AluOpType
ACT = mybir.ActivationFunctionType
AX = mybir.AxisListType

P = 128
D = 1024
KD = D // P
SEQ, DEC_BATCH, DEC_SEQ = 512, 8, 4
NS = DEC_BATCH * DEC_SEQ
T = SEQ + NS
HALF = T // 2
PT = SEQ // P
TILES = [P] * PT + [NS]
DEPTH = 2
PAGE, PAGES = 128, 2
HEADS, DK, DV = 4, 64, 128
CH = 64
NCH = SEQ // CH
DFF = 2816
KF = DFF // P
PLE = 256
KP = PLE // P
RANK = 16
EPS = 1e-6
BIG = 1e30
COL_GLA, COL_LR, COL_ML, COL_IF, COL_DF = 0, 1536, 1552, 3088, 3096
RAW, SPLIT = 4, 2
KMAX = 8
DOWN_K = [(0, 6), (6, 6), (12, 5), (17, 5)]


class Steps:

    def __init__(self, eng, sem):
        self.eng, self.sem, self.n = eng, sem, 0

    def __call__(self, ins):
        ins.then_inc(self.sem, 1)
        self.n = self.n + 1
        self.eng.wait_ge(self.sem, self.n)


class Between:

    def __init__(self, piece, total):
        self.piece, self.total, self.n = piece, total, 0

    def __call__(self, count=1):
        for _ in range(min(count, self.total - self.n)):
            self.piece(self.n)
            self.n = self.n + 1

    def rest(self):
        self(self.total - self.n)


def halves(ap):
    return ap.rearrange("p (h n) -> p h n", h=2)


def program(nc, a, c, o):
    ctx = ExitStack()
    with ctx:
        ctx.enter_context(nc.allow_non_contiguous_dma(reason="gains and states' columns, a few kilobytes"))
        arena_size = (nc.sbuf_usable_end - nc.sbuf_base - 64) // 64 * 64
        arena = ctx.enter_context(nc.sbuf_tensor("arena", [P, arena_size // 4], F32, align_bytes=64))
        start = nc.sbuf_base - arena_size
        assert start >= 0

        class Area:

            def __init__(self, at, size):
                self.at, self.size, self.used = at, size, 0

            def put(self, name, shape, dt=F32):
                n = 4
                for s in shape[1:]:
                    n *= s
                n = (n + 31) // 32 * 32
                assert self.used + n <= self.size, (name, self.used + n, self.size)
                t = nc.alloc_sbuf_tensor_at(name, shape, dt, offset=self.at + self.used)
                self.used += n
                return t

            def again(self, skip=0):
                return Area(self.at + skip, self.size - skip)

        whole = Area(start, arena_size)

        def area(size):
            r = Area(whole.at + whole.used, size)
            whole.used += size
            assert whole.used <= whole.size, (whole.used, whole.size)
            return r

        BLK = T * 4
        fixed = area(10368)
        ident = fixed.put("ident", [P, P])
        ones = fixed.put("ones", [P, P])
        rot = fixed.put("rot", [P, P])
        big = fixed.put("big", [P, P])
        neg = fixed.put("neg", [P, P])
        gmask = fixed.put("gmask", [P, P])
        smask = fixed.put("smask", [NS, NS])
        sbig = fixed.put("sbig", [NS, NS])
        sneg = fixed.put("sneg", [P, 2, NS])
        sel = fixed.put("sel", [HEADS, HEADS, P])
        selp = fixed.put("selp", [HEADS, 2, P])
        seqm = fixed.put("seqm", [NS, DEC_BATCH])
        sign = fixed.put("sign", [P, 2])
        epsc = fixed.put("epsc", [P, 1])
        gains = fixed.put("gains", [P, 3, KD])
        gfin = fixed.put("gfin", [P, KD])
        ghead = fixed.put("ghead", [P, 3])
        bgk = fixed.put("bgk", [P, 2])
        bif = fixed.put("bif", [P, 1])
        wgk = fixed.put("wgk", [RANK, HEADS * DK])
        lamv = fixed.put("lamv", [P, 4, DK])
        lamp = fixed.put("lamp", [P, DK])
        lam = fixed.put("lam", [P, 8])
        lamc = fixed.put("lamc", [P, 2])
        m_in = fixed.put("m_in", [HEADS, DEC_BATCH])
        g_dec = fixed.put("g_dec", [P, 2, NCH + DEC_BATCH])
        pages = fixed.put("pages", [1, DEC_BATCH * PAGES], I32)

        rB = area(BLK).put("rB", [P, T])
        a_H = area(KD * BLK)
        h = a_H.again().put("h", [P, KD, T])
        xs = area(2 * KD * BLK)
        xH, xL = xs.put("xH", [P, KD, T], F32R), xs.put("xL", [P, KD, T], F32R)
        ws = area((RAW + 2 * SPLIT) * KMAX * P * 4)
        raw = [ws.put(f"raw{i}", [P, KMAX, P]) for i in range(RAW)]
        wH = [ws.put(f"wH{i}", [P, KMAX, P], F32R) for i in range(SPLIT)]
        wL = [ws.put(f"wL{i}", [P, KMAX, P], F32R) for i in range(SPLIT)]
        a_oA, a_oM, a_A, a_B, a_MG = (area(8 * BLK) for _ in range(5))
        a_VA = area(5 * 4 * DV * 4)
        a_VM = area(10336)
        a_T = area(whole.size - whole.used)
        hid_area = Area(a_oA.at, 5 * 8 * BLK + a_VA.size)
        tail = Area(a_VM.at, a_VM.size + a_T.size)

        oH, oL, oraw, rO = [], [], [], []
        for n, ar in zip(("g", "m", "d"), (a_oA, a_oM, a_A)):
            oH.append(ar.again().put(f"oH_{n}", [P, HEADS, T], F32R))
            oL.append(ar.again(4 * BLK).put(f"oL_{n}", [P, HEADS, T], F32R))
            rO.append(ar.again().put(f"rO_{n}", [P, HEADS, T]))
            oraw.append(ar.again(4 * BLK).put(f"oraw_{n}", [P, HEADS, T]))
        A = a_A.again().put("A", [P, 8, T])
        B = a_H.again().put("B", [P, 8, T])
        C = a_B.again().put("C", [P, 8, T])
        MG = a_H.again().put("MG", [P, 8, T])
        gvf = a_MG.again().put("gvf", [P, 4, T])
        mvf = a_oA.again().put("mvf", [P, 4, T])
        dvf = a_MG.again(4 * BLK).put("dvf", [P, 4, T])
        gv = a_VA.again().put("gv", [P, 5, HEADS, DV])
        dv = a_VA.again().put("dv", [P, 5, HEADS, DV])
        mv = a_VM.again().put("mv", [P, 5, HEADS, DV + 1])
        small = a_T.put("small", [P, T])
        tmp_at = a_T.used
        sq0 = a_T.again().put("sq0", [P, 3, T])

        t = a_oM.again()
        g_b, g_E, g_kg = (t.put(n, [P, 2, T]) for n in ("g_b", "g_E", "g_kg"))
        g_az, g_reset = t.put("g_az", [P, T]), t.put("g_reset", [P, T])
        t = a_B.again()
        g_S, g_Sin = t.put("g_S", [P, NCH, 2, DV]), t.put("g_Sin", [P, DEC_BATCH, 2, DV])
        t = a_VM.again()
        g_kdT, g_A = t.put("g_kdT", [P, 5, HEADS * DK]), t.put("g_A", [P, 2, HEADS, P])
        g_As = t.put("g_As", [NS, HEADS, NS])
        g_qz = a_MG.again().put("g_qz", [P, HEADS, T])
        g_kdm = a_MG.again(4 * BLK).put("g_kdm", [NS, DEC_BATCH, HEADS * DK])
        t = a_A.again()
        r_a, r_m, r_en, r_F, r_d, r_g, r_wi, r_reset = (
            t.put(n, [HEADS, T]) for n in ("r_a", "r_m", "r_en", "r_F", "r_d", "r_g", "r_wi", "r_reset"))
        t = a_MG.again(4 * BLK)
        m_qwz = t.put("m_qwz", [P, HEADS, T])
        m_qz = a_oM.again().put("m_qz", [P, HEADS, T])
        t = a_H.again()
        m_qns, m_den = t.put("m_qns", [P, HEADS, NS]), t.put("m_den", [P, HEADS])
        m_Cin = a_MG.again().put("m_Cin", [P, DEC_BATCH, 2, DV + 1])
        t = a_VA.again()
        m_kT, m_kw = t.put("m_kT", [P, 5, HEADS, DK]), t.put("m_kw", [P, 5, HEADS, DK])
        m_kwm = a_oM.again().put("m_kwm", [NS, DEC_BATCH, HEADS * DK])
        t = a_T.again(tmp_at)
        m_D = t.put("m_D", [P, HEADS * P])
        m_C = a_T.again(2 * BLK).put("m_C", [P, 2, 2, DV + 1])
        t = a_MG.again(DEC_BATCH * 2 * (DV + 1) * 4)
        m_dec, m_cols = t.put("m_dec", [P, 2, 12]), t.put("m_cols", [P, 5, 12])
        m_prev = t.put("m_prev", [HEADS, 12])
        m_SD = a_A.again(3 * BLK).put("m_SD", [P, HEADS * P])
        m_ad = a_A.again(7 * BLK).put("m_ad", [P, HEADS * P])
        m_tok = a_A.again(7 * BLK).put("m_tok", [P, HEADS, DV])
        t = a_VM.again()
        d_e, d_w, d_wT = t.put("d_e", [P, 2, SEQ]), t.put("d_w", [P, SEQ]), t.put("d_wT", [P, SEQ])
        d_kout = t.put("d_kout", [P, 8 * DK])
        t = a_T.again()
        d_cos, d_sin = t.put("d_cos", [P, T]), t.put("d_sin", [P, T])
        d_t1 = a_VM.again().put("d_t1", [P, T])
        t = a_T.again()
        d_qbd = t.put("d_qbd", [P, DEC_BATCH, HEADS, 2, DEC_SEQ * HEADS])
        d_es = t.put("d_es", [P, 2 * PAGE + NS])
        d_wTs, d_wTn = t.put("d_wTs", [P, PAGES, 4, HEADS, DEC_SEQ]), t.put("d_wTn", [NS, 4, HEADS, DEC_SEQ])
        d_nm, d_l, d_rc = t.put("d_nm", [P, 2]), t.put("d_l", [P, 2]), t.put("d_rc", [P, 2])
        d_V = a_VM.again().put("d_V", [P, 4, HEADS * DV])
        t = a_MG.again()
        d_kr = t.put("d_kr", [P, 4, HEADS, P])
        d_KT = t.put("d_KT", [P, HEADS, PAGES * PAGE])
        u_g = t.put("u_g", [P, 2, T])
        mH = a_oA.again().put("mH", [P, KD, T], F32R)
        mL = a_oM.again().put("mL", [P, KD, T], F32R)
        p_tok = a_B.again().put("p_tok", [P, 5, PLE])
        t = tail.again()
        pH, pL = t.put("pH", [P, KP, T], F32R), t.put("pL", [P, KP, T], F32R)
        p_raw = a_B.again(5120).put("p_raw", [P, KP, T])
        f_g, f_u = t.put("f_g", [P, 2, T]), t.put("f_u", [P, 2, T])
        t2 = hid_area.again()
        hidH, hidL = t2.put("hidH", [P, KF, T], F32R), t2.put("hidL", [P, KF, T], F32R)
        t = tail.again(4 * BLK)
        sq2 = t.put("sq2", [P, 3, T])
        e_g = tail.again(6 * BLK).put("e_g", [P, 2, T])
        e_p = hid_area.again().put("e_p", [P, KD, T])
        io_tok = hid_area.again().put("io_tok", [P, 5, D])
        y_f = hid_area.again(5 * D * 4).put("y_f", [P, KD, T])

        spill = o["spill"]
        G = ctx.enter_context(nc.psum_tensor("G", [P, 2, 2, 512], F32))
        M = ctx.enter_context(nc.psum_tensor("M", [P, 4, 512], F32))

        def out2(slot):
            return G[:, slot, :, 0:HALF]

        M01 = M[:, 0:2, 0:HALF]
        M23 = M[:, 2:4, 0:HALF]

        class Semaphores:
            pass

        s, sems = Semaphores(), []

        def signals(names):
            new = [ctx.enter_context(nc.semaphore(n)) for n in names.split()]
            sems.extend(new)
            return new

        s.const_in, s.io_in, s.io_turned, s.io_copied, s.io_out = signals("const_in io_in io_turned io_copied io_out")
        s.y_ready, s.y_ps = signals("y_ready y_ps")
        s.gain_in, s.par_in, s.greset_in = signals("gain_in par_in greset_in")
        s.rreset_in, s.trig_in = signals("rreset_in trig_in")
        s.gst_in, s.mst_in, s.ptok_in = signals("gst_in mst_in ptok_in")
        s.gstore, s.mstore, s.kstore = signals("gstore mstore kstore")
        s.vstore, s.spilled, s.h_back = signals("vstore spilled h_back")
        s.w_in0, s.w_in1, s.w_in2 = signals("w_in0 w_in1 w_in2")
        s.w_in3, s.wh_split, s.wl_split = signals("w_in3 wh_split wl_split")
        s.chunk_done, s.out_taken = signals("chunk_done out_taken")
        s.xh_ready, s.xl_ready, s.sq_ready = signals("xh_ready xl_ready sq_ready")
        s.sq_used, s.stat_ps, s.r_ready = signals("sq_used stat_ps r_ready")
        s.h_mix, s.h_ffn, s.h_ple = signals("h_mix h_ffn h_ple")
        s.tok_ps, s.tok_copied = signals("tok_ps tok_copied")
        s.gz_ps, s.gz_abs, s.gz_ln, s.gz_min, s.g_b_ready = signals("gz_ps gz_abs gz_ln gz_min g_b_ready")
        s.g_e, s.g_qg, s.g_kg, s.g_kd, s.g_kdm_ready = signals("g_e g_qg g_kg g_kd g_kdm_ready")
        s.g_at_ps, s.g_at, s.g_ds_ps, s.g_s, s.g_o_ps, s.g_o = signals("g_at_ps g_at g_ds_ps g_s g_o_ps g_o")
        s.bn_sq, s.bn_ps, s.bn_ln, s.bn_r = signals("bn_sq bn_ps bn_ln bn_r")
        s.bn_gate, s.bn_o, s.bn_h, s.bn_l = signals("bn_gate bn_o bn_h bn_l")
        s.ml_rows, s.ml_ln, s.ml_ex = signals("ml_rows ml_ln ml_ex")
        s.ml_col_ps, s.ml_col, s.ml_wi_ps, s.ml_wi = signals("ml_col_ps ml_col ml_wi_ps ml_wi")
        s.ml_qz, s.ml_kw, s.ml_kwm_ready = signals("ml_qz ml_kw ml_kwm_ready")
        s.ml_d_ps, s.ml_d, s.ml_s_ps, s.ml_sd = signals("ml_d_ps ml_d ml_s_ps ml_sd")
        s.ml_n_ps, s.ml_tok, s.ml_t_ps = signals("ml_n_ps ml_tok ml_t_ps")
        s.ml_c_ps, s.ml_c, s.ml_o = signals("ml_c_ps ml_c ml_o")
        s.ml_qn, s.ml_e_ps, s.ml_den_ps, s.ml_ad = signals("ml_qn ml_e_ps ml_den_ps ml_ad")
        s.lam_sum, s.lam_exp, s.rope_ps, s.rope_done = signals("lam_sum lam_exp rope_ps rope_done")
        s.sc_ps, s.nm_ready, s.e_ready, s.w_ready = signals("sc_ps nm_ready e_ready w_ready")
        s.wt_ps, s.wt_copied, s.pv_ps, s.pv_copied = signals("wt_ps wt_copied pv_ps pv_copied")
        s.page0, s.page1, s.page2, s.page3, s.vpage0 = signals("page0 page1 page2 page3 vpage0")
        s.vpage1, s.vpage2, s.vpage3, s.v_used = signals("vpage1 vpage2 vpage3 v_used")
        s.qbd_ready, s.ss_ps, s.ss_nm, s.ss_e, s.ss_w = signals("qbd_ready ss_ps ss_nm ss_e ss_w")
        s.st_ps, s.st_red, s.sp_ps, s.sp_copied = signals("st_ps st_red sp_ps sp_copied")
        s.u_lin, s.u_sig, s.first_done, s.u_mul = signals("u_lin u_sig first_done u_mul")
        s.mg_ready, s.mh_ready, s.ml_split = signals("mg_ready mh_ready ml_split")
        s.f_lin, s.f_silu, s.f_hid, s.fh_ready, s.fl_ready = signals("f_lin f_silu f_hid fh_ready fl_ready")
        s.p_ps, s.p_copied, s.ph_ready = signals("p_ps p_copied ph_ready")
        s.pl_ready, s.proj_done, s.proj_taken = signals("pl_ready proj_done proj_taken")
        s.e_lin, s.e_sig, s.e_mul = signals("e_lin e_sig e_mul")
        s.act_step, s.dve_step = signals("act_step dve_step")
        s.w_in = [s.w_in0, s.w_in1, s.w_in2, s.w_in3]
        s.page = [s.page0, s.page1, s.page2, s.page3]
        s.vpage = [s.vpage0, s.vpage1, s.vpage2, s.vpage3]

        def clear_all():
            nc.all_engine_barrier()
            numbers = [x.num for x in sems]
            assert max(numbers) - min(numbers) + 1 == len(numbers)
            nc.sync.sem_clear(range(min(numbers), max(numbers) + 1))
            nc.all_engine_barrier()

        with nc.Block() as block:

            @block.sync
            def _(sp):
                sp.dma_start(ident[:], c["ident"]).then_inc(s.io_in, 16)
                sp.dma_start(io_tok[:, 0:PT, :],
                             a["x_prompt"].rearrange("a (i p) d -> p (a i) d", p=P)).then_inc(s.io_in, 16)
                sp.dma_start(io_tok[0:NS, PT, :], a["x_sample"].rearrange("b t d -> (b t) d")).then_inc(s.io_in, 16)
                for dst, src in ((ones, "ones"), (rot, "rot"), (big, "big"), (neg, "neg"),
                                 (gmask, "gmask"), (smask, "smask"), (sbig, "sbig"), (sneg, "sneg"), (sel, "sel"),
                                 (selp, "selp"), (seqm, "seqm"), (sign, "sign"), (epsc, "epsc")):
                    sp.dma_start(dst[:], c[src]).then_inc(s.const_in, 16)
                sp.dma_start(gfin[:, :], a["g_final"].rearrange("(k p) -> p k", p=P)).then_inc(s.const_in, 16)
                sp.dma_start(pages[:, :], a["page_table"].rearrange("(o b) n -> o (b n)", o=1)).then_inc(s.const_in, 16)
                sp.wait_ge(s.const_in, 15 * 16)

            @block.tensor
            def _(pe):
                pe.wait_ge(s.io_in, 3 * 16)
                for k in range(KD):
                    if k >= 2:
                        pe.wait_ge(s.io_copied, 2 * (k - 1))
                    for i, n in enumerate(TILES):
                        bank, col = (2 * (k % 2) + i // PT, (i % PT) * P)
                        pe.transpose(M[:, bank, col:col + n], io_tok[0:n, i, k * P:(k + 1) * P],
                                     ident[0:n, 0:n]).then_inc(s.io_turned, 1)

            @block.vector
            def _(dve):
                for k in range(KD):
                    dve.wait_ge(s.io_turned, 5 * (k + 1))
                    dve.tensor_copy(h[:, k, 0:SEQ], M[:, 2 * (k % 2), :]).then_inc(s.io_copied, 1)
                    dve.tensor_copy(h[:, k, SEQ:T], M[:, 2 * (k % 2) + 1, 0:NS]).then_inc(s.io_copied, 1)

        clear_all()

        CHUNK, OUT, cc, oo = {}, {}, 0, 0
        for name, chunks, outs in (("gla", 12, 12), ("small", 1, 1), ("ml", 12, 12), ("df", 12, 12),
                                   ("merge0", 12, 16), ("merge1", 12, 16), ("merge2", 12, 16), ("out", 8, 8),
                                   ("ffn", 2 * KF, 2 * KF), ("down", 4 * KD, KD), ("ple", 10, 16)):
            CHUNK[name], OUT[name] = cc, oo
            cc, oo = cc + chunks, oo + outs
        TOK = {"gv": 0, "kd": 5, "mv": 10, "mk": 15, "dv": 20, "dk": 25, "page": 30}

        def load_chunk(sp, n, view, src):
            if n >= RAW:
                sp.wait_ge(s.wl_split, n - (RAW - 1))
            sp.dma_start(view(raw[n % RAW]), src).then_inc(s.w_in[n % RAW], 16)

        def high_chunk(act, n, kb=KD):
            act.wait_ge(s.w_in[n % RAW], w_count(n, 0, 4))
            if n >= SPLIT:
                act.wait_ge(s.chunk_done, n - (SPLIT - 1))
            act.activation(wH[n % SPLIT][:, 0:kb, :], raw[n % RAW][:, 0:kb, :], ACT.Copy).then_inc(s.wh_split, 1)

        def low_chunk(pool, n, kb=KD):
            pool.wait_ge(s.wh_split, n + 1)
            pool.tensor_tensor(wL[n % SPLIT][:, 0:kb, :], raw[n % RAW][:, 0:kb, :], wH[n % SPLIT][:, 0:kb, :].bitcast(F32),
                               ALU.subtract).then_inc(s.wl_split, 1)

        def both_loop(pool, name, count=12, per=4):
            base = CHUNK[name]
            with pool.Fori(0, count // per) as i:
                for j in range(per):
                    n = base + j
                    pool.wait_ge(s.w_in[n % RAW], w_count(n, i, per))
                    pool.wait_ge(s.chunk_done, n + per * i - (SPLIT - 1))
                    pool.tensor_tensor(wH[n % SPLIT][:, :, :], raw[n % RAW][:, :, :],
                                       ones[:, 0:1].unsqueeze(1).to_broadcast([P, KD, P]), ALU.mult).then_inc(s.wh_split, 1)
                    pool.wait_ge(s.wh_split, n + 1 + per * i)
                    pool.tensor_tensor(wL[n % SPLIT][:, :, :], raw[n % RAW][:, :, :], wH[n % SPLIT][:, :, :].bitcast(F32),
                                       ALU.subtract).then_inc(s.wl_split, 1)

        def w_count(slot_chunk, i, per):
            slot = slot_chunk % RAW
            more = 48 if slot == CHUNK["small"] % RAW and slot_chunk >= CHUNK["small"] else 0
            return 16 * (slot_chunk // RAW + 1) + more + 16 * (per // RAW) * i

        def load_loop(sp, name, count, kb, source, per=4, first=0):
            base = CHUNK[name]

            def turn(i, start):
                for j in range(per):
                    n = base + j + per * i
                    if start + j >= RAW:
                        sp.wait_ge(s.wl_split, n - (RAW - 1))
                    k = kb(j)
                    sp.dma_start(raw[(base + j) % RAW][:, 0:k, :], source(i, j)).then_inc(s.w_in[(base + j) % RAW], 16)

            with sp.Fori(1 if base < RAW else 0, count // per) as i:
                turn(i, RAW)

        def high_loop(act, name, count, per=4):
            base = CHUNK[name]
            for n in range(base + SPLIT, base + per):
                high_chunk(act, n)
            with act.Fori(1, count // per) as i:
                for j in range(per):
                    n = base + j
                    act.wait_ge(s.w_in[n % RAW], w_count(n, i, per))
                    act.wait_ge(s.chunk_done, n + per * i - (SPLIT - 1))
                    act.activation(wH[n % SPLIT][:, :, :], raw[n % RAW][:, :, :], ACT.Copy).then_inc(s.wh_split, 1)

        def low_loop(pool, name, count, kb, per=4, first=0):
            base = CHUNK[name]
            with pool.Fori(first, count // per) as i:
                for j in range(per):
                    n = base + j
                    pool.wait_ge(s.wh_split, n + 1 + per * i)
                    pool.tensor_tensor(wL[n % SPLIT][:, 0:kb(j), :], raw[n % RAW][:, 0:kb(j), :],
                                       wH[n % SPLIT][:, 0:kb(j), :].bitcast(F32), ALU.subtract).then_inc(s.wl_split, 1)

        def blocks_product(pe, n, slot, hi, lo, blocks, start, stop):
            for at, (wk, xk) in enumerate(blocks):
                for w, x in ((wH, hi), (wH, lo), (wL, hi)):
                    for half in range(2):
                        mm = pe.matmul(G[:, slot, half, 0:HALF], w[n % SPLIT][:, wk, :],
                                       x[:, xk, half * HALF:(half + 1) * HALF],
                                       start=(start and at == 0 and w is wH and x is hi),
                                       stop=(stop and at == len(blocks) - 1 and w is wL))
            return mm

        def panel_chunk(pe, n, out, hi, lo, i=0, per=0, before=None):
            pe.wait_ge(s.wl_split, n + 1 + per * i)
            if out >= 2 or per:
                pe.wait_ge(s.out_taken, out - 1 + per * i)
            blocks = [(k, k) for k in range(KD)]
            if before is None:
                mm = blocks_product(pe, n, out % 2, hi, lo, blocks, True, True)
            else:
                for k in range(KD):
                    before(k)
                    mm = blocks_product(pe, n, out % 2, hi, lo, blocks[k:k + 1], k == 0, k == KD - 1)
            mm.then_inc(s.chunk_done, 1)

        def panel_piece(pe, name, at):
            j, part = at // 4, at % 4
            n, out = CHUNK[name] + j, OUT[name] + j
            if part == 0:
                pe.wait_ge(s.wl_split, n + 1)
                pe.wait_ge(s.out_taken, out - 1)
            mm = blocks_product(pe, n, out % 2, xH, xL, [(2 * part, 2 * part), (2 * part + 1, 2 * part + 1)],
                                part == 0, part == 3)
            if part == 3:
                mm.then_inc(s.chunk_done, 1)

        def panel_loop(pe, name, count, hi, lo, first=0, per=4):
            base, out = CHUNK[name], OUT[name]
            for j in range(first, per if first else 0):
                panel_chunk(pe, base + j, out + j, hi, lo)
            with pe.Fori(1 if first else 0, count // per) as i:
                for j in range(per):
                    panel_chunk(pe, base + j, out + j, hi, lo, i, per)

        def x_high(act, n, k, sq, gain, h_ready=None):
            if h_ready is not None:
                act.wait_ge(h_ready, k + 1)
            act.activation(xH[:, k, :], h[:, k, :], ACT.Copy, scale=gain[:, k:k + 1]).then_inc(s.xh_ready, 1)
            if k >= 3:
                act.wait_ge(s.sq_used, (KD - 1) * n + k - 2)
            act.activation(sq[:, k % 2 if k else 2, :], h[:, k, :], ACT.Square).then_inc(s.sq_ready, 1)

        def add_square(eng, n, k, sq):
            eng.wait_ge(s.sq_ready, KD * n + k + 1)
            if k > 1:
                eng.wait_ge(s.sq_used, (KD - 1) * n + k - 1)
            eng.tensor_tensor(sq[:, 2, :], sq[:, 2, :], sq[:, k % 2, :], ALU.add).then_inc(s.sq_used, 1)

        def x_low(dve, n, k, gain):
            dve.wait_ge(s.xh_ready, KD * n + k + 1)
            dve.scalar_tensor_tensor(out=xL[:, k, :], in0=h[:, k, :], scalar=gain[:, k:k + 1],
                                     in1=xH[:, k, :].bitcast(F32), op0=ALU.mult,
                                     op1=ALU.subtract).then_inc(s.xl_ready, 1)

        def norm_factor(act, step, n):
            act.wait_ge(s.stat_ps, n + 1)
            step(act.activation(halves(rB[:, :]), M01, ACT.Ln, scale=1.0 / D, bias=epsc[:, 0:1]))
            act.activation(rB[:, :], rB[:, :], ACT.Exp, scale=-0.5).then_inc(s.r_ready, 1)

        def stats(pe, n, sq):
            pe.wait_ge(s.sq_used, (KD - 1) * (n + 1))
            for half in range(2):
                mm = pe.matmul(M[:, half, 0:HALF], ones[:, :], sq[:, 2, half * HALF:(half + 1) * HALF], start=True, stop=True)
            mm.then_inc(s.stat_ps, 1)

        def x_there(pe, n):
            return lambda k: pe.wait_ge(s.xl_ready, KD * n + k + 1)

        def to_tokens_pe(pe, first, blocks, width=P):
            for i, n in enumerate(TILES):
                if first + i >= 2:
                    pe.wait_ge(s.tok_copied, first + i - 1)
                for m, src in enumerate(blocks):
                    mm = pe.transpose(M[0:n, 2 + (first + i) % 2, m * P:(m + 1) * P], src[:, i * P:i * P + n], ident[:, :])
                mm.then_inc(s.tok_ps, 1)

        def to_tokens_act(act, first, dst, cols, shape=None):
            for i, n in enumerate(TILES):
                act.wait_ge(s.tok_ps, first + i + 1)
                src = M[0:n, 2 + (first + i) % 2, 0:cols]
                if shape:
                    src = src.rearrange("p (h v) -> p h v", h=shape)
                act.activation(dst(i, n), src, ACT.Copy).then_inc(s.tok_copied, 1)

        def branch_pe(pe, b, fill):
            for hd in range(HEADS):
                fill(1)
                pe.wait_ge(s.bn_sq, b * HEADS + hd + 1)
                if hd or b:
                    pe.wait_ge(s.bn_ln, b * HEADS + hd)
                for half in range(2):
                    mm = pe.matmul(M[:, half, 0:HALF], ones[:, :], rO[b][:, hd, half * HALF:(half + 1) * HALF],
                                   start=True, stop=True)
                mm.then_inc(s.bn_ps, 1)

        def branch_act(act, b):
            for hd in range(HEADS):
                act.activation(rO[b][:, hd, :], oraw[b][:, hd, :], ACT.Square).then_inc(s.bn_sq, 1)
            for hd in range(HEADS):
                act.wait_ge(s.bn_ps, b * HEADS + hd + 1)
                act.activation(halves(rO[b][:, hd, :]), M01, ACT.Ln, scale=1.0 / DV,
                               bias=epsc[:, 0:1]).then_inc(s.bn_ln, 1)
            for q, pair in enumerate((slice(0, 2), slice(2, 4))):
                act.wait_ge(s.bn_ln, b * HEADS + 2 * (q + 1))
                act.activation(rO[b][:, pair, :], rO[b][:, pair, :], ACT.Exp, scale=-0.5).then_inc(s.bn_r, 1)
            for q, pair in enumerate((slice(0, 2), slice(2, 4))):
                act.wait_ge(s.bn_o, 2 * b + q + 1)
                act.activation(oH[b][:, pair, :], oraw[b][:, pair, :], ACT.Copy).then_inc(s.bn_h, 1)

        def branch_dve(dve, step, b, gate, between):
            if gate is not None:
                dve.wait_ge(s.bn_gate, b + 1)
                dve.wait_ge(s.bn_sq, HEADS * (b + 1))
                step(dve.tensor_tensor(oraw[b][:, :, :], oraw[b][:, :, :], gate, ALU.mult))
            between()
            pairs = (slice(0, 2), slice(2, 4))
            for q, pair in enumerate(pairs):
                dve.wait_ge(s.bn_r, 2 * b + q + 1)
                dve.scalar_tensor_tensor(out=oraw[b][:, pair, :], in0=oraw[b][:, pair, :], scalar=ghead[:, b:b + 1],
                                         in1=rO[b][:, pair, :], op0=ALU.mult, op1=ALU.mult).then_inc(s.bn_o, 1)
            between()
            dve.wait_ge(s.bn_o, 2 * (b + 1))
            for q, pair in enumerate(pairs):
                dve.wait_ge(s.bn_h, 2 * b + q + 1)
                ins = dve.tensor_tensor(oL[b][:, pair, :], oraw[b][:, pair, :], oH[b][:, pair, :].bitcast(F32), ALU.subtract)
                if q == 0:
                    step(ins)
            ins.then_inc(s.bn_l, 1)

        def take(dve, out, dst):
            dve.wait_ge(s.chunk_done, out + 1)
            dve.tensor_tensor(halves(dst), out2(out % 2), halves(rB[:, :]), ALU.mult).then_inc(s.out_taken, 1)

        def merge_chunks(b):
            n = CHUNK[f"merge{b}"]
            for q in range(KD // 2):
                yield n + 3 * q, "gate", 2 * q
                yield n + 3 * q + 1, "gate", 2 * q + 1
                yield n + 3 * q + 2, "branch", 2 * q

        def two_outputs(r):
            return r[:, :, :].rearrange("p (k o) n -> p k (o n)", k=HEADS)

        KEYS_AT = (1, 4, 7, 10, 13)
        LOAD_PROMPT = 11

        lo64 = [slice(0, DK), slice(DK, P)]

        with nc.Fori(0, DEPTH) as layer:

            def at(x):
                return x[bass.ds(layer, 1)]

            with nc.Block() as block:

                @block.sync
                def _(sp):
                    for j, n in enumerate(("g_mix", "g_ffn", "g_ple")):
                        sp.dma_start(gains[:, j, :], at(a[n]).rearrange("o (k p) -> p (o k)", p=P)).then_inc(s.gain_in, 16)
                    win = at(a["w_in"]).rearrange("o (k p) e -> p (o k) e", p=P)
                    for j in range(4):
                        load_chunk(sp, CHUNK["gla"] + j, lambda r: r[:, :, :], win[:, :, COL_GLA + P * j:COL_GLA + P * (j + 1)])
                    for j, n in enumerate(("g_gla_norm", "g_mlstm_norm", "g_diff_norm")):
                        sp.dma_start(ghead[:, j:j + 1], at(a[n]).rearrange("o p -> p o")).then_inc(s.par_in, 16)
                    sp.dma_start(bgk[:, :], at(a["b_gla_gk"]).rearrange("o (k p) -> p (o k)", p=P)).then_inc(s.par_in, 16)
                    for j in range(2):
                        sp.dma_start(bif[32 + 32 * j:32 + 32 * j + HEADS, :],
                                     at(a["b_mlstm_if"])[:, HEADS * j:HEADS * (j + 1)].rearrange("o p -> p o")).then_inc(s.par_in, 16)
                    sp.dma_start(wgk[:, :], at(a["w_gla_gk"]).rearrange("o r e -> (o r) e")).then_inc(s.par_in, 16)
                    sp.dma_start(lamv[:, :, :], at(a["diff_lambda"]).partition_broadcast(P).rearrange("p o r d -> p (o r) d")
                                 ).then_inc(s.par_in, 16)
                    sp.dma_start(lamc[:, :], at(c["lamc"]).rearrange("o p n -> (o p) n")).then_inc(s.par_in, 16)
                    sp.dma_start(m_in[:, :], at(a["state_mlstm_m"]).rearrange("o b h -> h (o b)")).then_inc(s.par_in, 16)
                    load_loop(sp, "gla", 12, lambda j: KD, lambda i, j: win[:, :, bass.ds(COL_GLA + 4 * P * i + P * j, P)])
                    n = CHUNK["small"]
                    sp.wait_ge(s.wl_split, n - (RAW - 1))
                    for at_col, col in ((0, COL_LR), (32, COL_IF), (64, COL_IF + HEADS), (96, COL_IF)):
                        sp.dma_start(raw[n % RAW][:, :, at_col:at_col + 32], win[:, :, col:col + 32]).then_inc(s.w_in[n % RAW], 16)
                    sp.dma_start(spill, h[:, :, :]).then_inc(s.spilled, 16)
                    sp.dma_start(g_reset[:, :], c["greset"]).then_inc(s.greset_in, 16)
                    for q in range(2):
                        sp.dma_start(g_Sin[lo64[q], :, :, :], at(a["state_gla"])[:, :, q:HEADS:2].rearrange(
                            "o b p d v -> d (o b) p v")).then_inc(s.gst_in, 16)
                    load_loop(sp, "ml", 12, lambda j: KD, lambda i, j: win[:, :, bass.ds(COL_ML + 4 * P * i + P * j, P)])
                    sp.wait_ge(s.g_s, NCH + DEC_BATCH)
                    sp.dma_start(at(o["gla_prompt"]).rearrange("o b (p q) d v -> (q d) (o b p) v", q=2),
                                 g_S[:, NCH - 1, :, :]).then_inc(s.gstore, 16)
                    sp.dma_start(at(o["gla_sample"]).rearrange("o b (p q) d v -> (q d) (o b) p v", q=2),
                                 g_Sin[:, :, :, :]).then_inc(s.gstore, 16)
                    load_df = Between(lambda j: load_chunk(sp, CHUNK["df"] + j, lambda r: r[:, :, :],
                                                           win[:, :, COL_DF + P * j:COL_DF + P * (j + 1)]), 12)
                    load_df(4)
                    sp.wait_ge(s.bn_l, 1)
                    sp.dma_start(r_reset[:, :], c["rreset"]).then_inc(s.rreset_in, 16)
                    sp.wait_ge(s.tok_copied, TOK["mv"] + 5)
                    for q in range(2):
                        sp.dma_start(m_Cin[lo64[q], :, :, 0:DV], at(a["state_mlstm_c"])[:, :, q:HEADS:2].rearrange(
                            "o b p d v -> d (o b) p v")).then_inc(s.mst_in, 16)
                    sp.dma_start(m_Cin[:, :, :, DV:DV + 1], at(a["state_mlstm_n"]).rearrange(
                        "o b (p q) (d u) -> (q d) (o b) p u", q=2, u=1)).then_inc(s.mst_in, 16)
                    load_df(12 - 4)
                    sp.wait_ge(s.ml_rows, 4)
                    sp.dma_start(at(o["m_prompt"]).rearrange("o b h -> h (o b)"), r_m[:, SEQ - 1:SEQ]).then_inc(s.mstore, 16)
                    sp.dma_start(at(o["m_sample"]).rearrange("o b h -> h (o b)"),
                                 r_m[:, SEQ + DEC_SEQ - 1:T:DEC_SEQ]).then_inc(s.mstore, 16)
                    wg = at(a["w_gate"]).rearrange("o (k p) e -> p (o k) e", p=P)
                    wb = at(a["w_branch"]).rearrange("o (k p) e -> p (o k) e", p=P)

                    def merge_load(b, chunk):
                        n, what, m = chunk
                        if what == "gate":
                            load_chunk(sp, n, lambda r: r[:, :, :], wg[:, :, D * b + P * m:D * b + P * (m + 1)])
                        else:
                            load_chunk(sp, n, two_outputs, wb[:, HEADS * b:HEADS * (b + 1), P * m:P * (m + 2)])

                    chunks01 = [(b, chunk) for b in range(2) for chunk in merge_chunks(b)]
                    load_next = Between(lambda at_chunk: merge_load(*chunks01[at_chunk]), len(chunks01))
                    load_next(4)
                    sp.dma_start(d_cos[:, :], c["cos"]).then_inc(s.trig_in, 16)
                    sp.wait_ge(s.ml_sd, PT + 1)
                    sp.dma_start(d_sin[:, :], c["sin"]).then_inc(s.trig_in, 16)
                    sp.wait_ge(s.ml_c, PT + DEC_BATCH)
                    sp.dma_start(at(o["c_prompt"]).rearrange("o b (p q) d v -> (q d) (o b p) v", q=2),
                                 m_C[:, (PT - 1) % 2, :, 0:DV]).then_inc(s.mstore, 16)
                    sp.dma_start(at(o["n_prompt"]).rearrange("o b (p q) (d u) -> (q d) (o b p) u", q=2, u=1),
                                 m_C[:, (PT - 1) % 2, :, DV:DV + 1]).then_inc(s.mstore, 16)
                    sp.dma_start(at(o["c_sample"]).rearrange("o b (p q) d v -> (q d) (o b) p v", q=2),
                                 m_Cin[:, :, :, 0:DV]).then_inc(s.mstore, 16)
                    sp.dma_start(at(o["n_sample"]).rearrange("o b (p q) (d u) -> (q d) (o b) p u", q=2, u=1),
                                 m_Cin[:, :, :, DV:DV + 1]).then_inc(s.mstore, 16)
                    load_next(1)
                    for i, n in enumerate(TILES):
                        sp.wait_ge(s.tok_copied, TOK["dv"] + i + 1)
                        dst = (at(o["v_prompt"])[:, :, i * P:(i + 1) * P].rearrange("o b t h v -> (o b t) h v") if n == P
                               else at(o["v_sample"]).rearrange("o b t h v -> (o b t) h v"))
                        sp.dma_start(dst, dv[0:n, i, :, :]).then_inc(s.vstore, 16)
                    load_next(2)
                    ck, cv = at(a["cache_k"]), at(a["cache_v"])
                    pool_n = a["cache_k"].shape[1]

                    def key_pages(first):
                        for n in range(first, first + 4):
                            if n >= 4:
                                sp.wait_ge(s.tok_ps, TOK["page"] + n - 3)
                            page = sp.value_load(pages[0:1, n:n + 1], min_val=0, max_val=pool_n - 1)
                            sp.dma_start(d_kr[:, n % 4, :, :], ck[:, bass.ds(page, 1)].rearrange(
                                "o q p (m c) d -> (o q p) m (c d)", c=2)).then_inc(s.page[n % 4], 16)

                    def value_pages(first):
                        for n in range(first, first + 4):
                            if n >= 4:
                                sp.wait_ge(s.v_used, n - 3)
                            page = sp.value_load(pages[0:1, n:n + 1], min_val=0, max_val=pool_n - 1)
                            sp.dma_start(d_V[:, n % 4, :], cv[:, bass.ds(page, 1)].rearrange(
                                "o q p h v -> (o q p) (h v)")).then_inc(s.vpage[n % 4], 16)

                    sp.wait_ge(s.tok_copied, TOK["dv"] + 5)
                    key_pages(0)
                    load_next(LOAD_PROMPT)
                    sp.wait_ge(s.pv_copied, PT * HEADS)
                    value_pages(0)
                    key_pages(4)
                    load_next(2)
                    key_pages(8)
                    load_next()
                    value_pages(4)
                    load_next()
                    key_pages(12)
                    load_next()
                    value_pages(8)
                    load_next()
                    value_pages(12)
                    load_next.rest()
                    sp.wait_ge(s.sp_copied, 2)
                    sp.wait_ge(s.pv_copied, PT * HEADS)
                    sp.dma_start(p_tok[:, 0:PT, :], at(a["p_prompt"]).rearrange("o b (i p) e -> p (o b i) e", p=P)).then_inc(s.ptok_in, 16)
                    sp.dma_start(p_tok[0:NS, PT, :], at(a["p_sample"]).rearrange("o b t e -> (o b t) e")).then_inc(s.ptok_in, 16)
                    for chunk in merge_chunks(2):
                        merge_load(2, chunk)
                    wo = at(a["w_out"]).rearrange("o (k p) e -> p (o k) e", p=P)
                    load_loop(sp, "out", 8, lambda j: KD, lambda i, j: wo[:, :, bass.ds(4 * P * i + P * j, P)])
                    fg = at(a["w_ffn_gate"]).rearrange("o (k p) e -> p (o k) e", p=P)
                    fu = at(a["w_ffn_up"]).rearrange("o (k p) e -> p (o k) e", p=P)
                    load_loop(sp, "ffn", 2 * KF, lambda j: KD, lambda i, j: (fg, fu)[j % 2][:, :, bass.ds(2 * P * i + P * (j // 2), P)])
                    fd = at(a["w_ffn_down"]).rearrange("o (k p) e -> p (o k) e", p=P)
                    load_loop(sp, "down", 4 * KD, lambda j: DOWN_K[j % 4][1],
                              lambda i, j: fd[:, DOWN_K[j % 4][0]:DOWN_K[j % 4][0] + DOWN_K[j % 4][1], bass.ds(2 * P * i + P * (j // 4), P)], per=8)
                    pg = at(a["w_ple_gate"]).rearrange("o (k p) e -> p (o k) e", p=P)
                    pp = at(a["w_ple_proj"]).rearrange("o (k p) e -> p (o k) e", p=P)
                    for q in range(2):
                        load_chunk(sp, CHUNK["ple"] + q, lambda r: r[:, :, :].rearrange("p (k o) n -> p k (o n)", k=KP),
                                   pp[:, :, 4 * P * q:4 * P * (q + 1)])
                    for m in range(KD):
                        load_chunk(sp, CHUNK["ple"] + 2 + m, lambda r: r[:, :, :], pg[:, :, P * m:P * (m + 1)])
                    sp.wait_ge(s.gstore, 32)
                    sp.wait_ge(s.mstore, 16 * 6)
                    sp.wait_ge(s.vstore, 16 * 5)
                    sp.wait_ge(s.kstore, 16 * 5)

                @block.gpsimd
                def _(pool):
                    for n in range(SPLIT):
                        low_chunk(pool, n)
                    for k in range(1, KD):
                        add_square(pool, 0, k, sq0)
                    for n in range(SPLIT, 4):
                        low_chunk(pool, n)
                    low_loop(pool, "gla", 12, lambda j: KD, first=1)
                    low_loop(pool, "small", 1, lambda j: KD, per=1)
                    for name in ("ml", "df", "merge0", "merge1", "merge2"):
                        both_loop(pool, name)
                    low_loop(pool, "out", 8, lambda j: KD)
                    low_loop(pool, "ffn", 2 * KF, lambda j: KD)
                    low_loop(pool, "down", 4 * KD, lambda j: DOWN_K[j % 4][1], per=8)
                    for n in range(10):
                        low_chunk(pool, CHUNK["ple"] + n)

                def gla_act(act, step):
                    to_tokens_act(act, TOK["gv"], lambda i, n: gv[0:n, i, :, :], HEADS * DV, HEADS)
                    for m in range(2):
                        act.wait_ge(s.gz_ps, m + 1)
                        if m:
                            act.wait_ge(s.gz_min, 2 * m)
                        step(act.activation(halves(g_az[:, :]), M01, ACT.Abs, bias=bgk[:, m:m + 1]))
                        act.sem_inc(s.gz_abs, 1)
                        step(act.activation(g_az[:, :], g_az[:, :], ACT.Exp, scale=-1.0))
                        act.activation(g_az[:, :], g_az[:, :], ACT.Ln, bias=1.0).then_inc(s.gz_ln, 1)
                    act.wait_ge(s.g_b_ready, 2)
                    act.activation(g_E[:, :, :], g_b[:, :, :], ACT.Exp, scale=1.0 / 16).then_inc(s.g_e, 1)
                    act.wait_ge(s.g_qg, 1)
                    act.activation(g_E[:, :, :], g_b[:, :, :], ACT.Exp, scale=-1.0 / 16).then_inc(s.g_e, 1)
                    act.wait_ge(s.g_kg, 2)
                    act.activation(g_E[:, :, :], g_b[:, :, :], ACT.Exp, scale=1.0 / 16).then_inc(s.g_e, 1)
                    to_tokens_act(act, TOK["kd"], lambda i, n: g_kdT[0:n, i, :], HEADS * DK)
                    act.activation(A[:, 4:8, :], A[:, 4:8, :], ACT.Silu).then_inc(s.bn_gate, 1)
                    for i in range(PT):
                        act.wait_ge(s.g_o_ps, i + 1)
                        act.activation(oraw[0][:, :, i * P:(i + 1) * P], M[:, 1, :].rearrange("p (h t) -> p h t", h=HEADS),
                                       ACT.Copy).then_inc(s.g_o, 1)
                    act.wait_ge(s.g_o_ps, PT + 1)
                    act.activation(oraw[0][:, :, SEQ:T], M[:, 1, 0:HEADS * NS].rearrange("p (h t) -> p h t", h=HEADS),
                                   ACT.Copy).then_inc(s.g_o, 1)
                    act.wait_ge(s.g_o, PT + 1)
                    to_tokens_act(act, TOK["mv"], lambda i, n: mv[0:n, i, :, 0:DV], HEADS * DV, HEADS)
                    to_tokens_act(act, TOK["mk"], lambda i, n: m_kT[0:n, i, :, :], HEADS * DK, HEADS)
                    branch_act(act, 0)

                def gla_dve(dve, step):
                    def ml_out(n):
                        if n == 0:
                            dve.wait_ge(s.spilled, 16)
                        take(dve, OUT["ml"] + n, B[:, n, :] if n < 4 else mvf[:, n - 4, :] if n < 8 else B[:, n - 4, :])

                    taken = Between(ml_out, 12)
                    for n in range(12):
                        take(dve, n, A[:, n, :] if n < 4 else gvf[:, n - 4, :] if n < 8 else A[:, n - 4, :])
                    dve.wait_ge(s.chunk_done, 13)
                    ps = out2(0)
                    for at_row, rows in ((0, RANK), (32, HEADS), (64, HEADS)):
                        ins = dve.tensor_tensor(halves(small[at_row:at_row + rows, :]), ps[at_row:at_row + rows],
                                                halves(rB[at_row:at_row + rows, :]), ALU.mult)
                        if at_row < 64:
                            step(ins)
                    ins.then_inc(s.out_taken, 1)
                    for m in range(2):
                        dve.wait_ge(s.gz_abs, m + 1)
                        step(dve.tensor_scalar(halves(g_E[:, m, :]), M01, bgk[:, m:m + 1], 0.0, ALU.add, ALU.min))
                        dve.sem_inc(s.gz_min, 1)
                        dve.wait_ge(s.gz_ln, m + 1)
                        step(dve.tensor_tensor(g_E[:, m, :], g_E[:, m, :], g_az[:, :], ALU.subtract))
                        dve.sem_inc(s.gz_min, 1)
                        if m == 0:
                            dve.wait_ge(s.greset_in, 16)
                        dve.tensor_tensor_scan(g_b[:, m, :], g_reset[:, :], g_E[:, m, :], 0.0, ALU.mult,
                                               ALU.add).then_inc(s.g_b_ready, 1)
                        taken()
                    dve.wait_ge(s.g_b_ready, 2)
                    dve.wait_ge(s.g_e, 1)
                    step(dve.tensor_copy(g_dec[:, :, 0:NCH], g_E[:, :, CH - 1:SEQ:CH]))
                    step(dve.tensor_copy(g_dec[:, :, NCH:NCH + DEC_BATCH], g_E[:, :, SEQ + DEC_SEQ - 1:T:DEC_SEQ]))
                    dve.wait_ge(s.tok_copied, TOK["gv"] + 5)
                    for q in range(2):
                        step(dve.memset(g_qz[lo64[1 - q], q:HEADS:2, :], 0.0))
                        step(dve.scalar_tensor_tensor(out=g_qz[lo64[q], q:HEADS:2, :], in0=A[lo64[q], 0:2, :], scalar=DK ** -0.5,
                                                      in1=g_E[lo64[q], :, :], op0=ALU.mult, op1=ALU.mult))
                    dve.sem_inc(s.g_qg, 1)
                    taken()
                    dve.wait_ge(s.g_e, 2)
                    dve.tensor_tensor(g_kg[:, :, :], A[:, 2:4, :], g_E[:, :, :], ALU.mult).then_inc(s.g_kg, 1)
                    for m in range(2):
                        step(dve.tensor_copy(g_az[:, m * 16:m * 16 + NCH], g_b[:, m, CH - 1:SEQ:CH]))
                        step(dve.tensor_copy(g_az[:, m * 16 + 8:m * 16 + 16], g_b[:, m, SEQ + DEC_SEQ - 1:T:DEC_SEQ]))
                        for lo, hi, n, width in ((0, SEQ, NCH, CH), (SEQ, T, DEC_BATCH, DEC_SEQ)):
                            v = g_b[:, m, lo:hi].rearrange("p (n t) -> p n t", n=n)
                            last = g_az[:, m * 16 + (8 if lo else 0):m * 16 + (16 if lo else 8)].unsqueeze(2).to_broadcast([P, n, width])
                            step(dve.tensor_tensor(v, last, v, ALU.subtract))
                    dve.sem_inc(s.g_kg, 1)
                    dve.wait_ge(s.g_e, 3)
                    dve.tensor_tensor(A[:, 2:4, :], A[:, 2:4, :], g_E[:, :, :], ALU.mult).then_inc(s.g_kd, 1)
                    taken()
                    dve.wait_ge(s.tok_copied, TOK["kd"] + 5)
                    dve.tensor_tensor(g_kdm[:, :, :], g_kdT[0:NS, PT, :].unsqueeze(1).to_broadcast([NS, DEC_BATCH, HEADS * DK]),
                                      seqm[:, :].unsqueeze(2).to_broadcast([NS, DEC_BATCH, HEADS * DK]),
                                      ALU.mult).then_inc(s.g_kdm_ready, 1)

                    def masked(i):
                        dve.wait_ge(s.g_at_ps, i + 1)
                        if i >= 2:
                            dve.wait_ge(s.g_o_ps, i - 1)
                        dve.tensor_tensor(g_A[:, i % 2, :, :],
                                          M[:, 0, :].rearrange("p (h t) -> p h t", h=HEADS),
                                          gmask[:, :].unsqueeze(1).to_broadcast([P, HEADS, P]), ALU.mult).then_inc(s.g_at, 1)

                    masked(0)
                    for n in range(NCH):
                        if n % 2 == 0 and n // 2 + 1 < PT:
                            masked(n // 2 + 1)
                        if n % 2:
                            taken()
                        dve.wait_ge(s.g_ds_ps, n + 1)
                        ps = M[:, 2 + n % 2, 0:2 * DV].rearrange("p (q v) -> p q v", q=2)
                        if n == 0:
                            dve.tensor_copy(g_S[:, 0, :, :], ps).then_inc(s.g_s, 1)
                            continue
                        dve.wait_ge(s.g_s, n)
                        step(dve.scalar_tensor_tensor(out=g_S[:, n, 0, :], in0=g_S[:, n - 1, 0, :], scalar=g_dec[:, 0, n:n + 1],
                                                      in1=ps[:, 0, :], op0=ALU.mult, op1=ALU.add))
                        dve.scalar_tensor_tensor(out=g_S[:, n, 1, :], in0=g_S[:, n - 1, 1, :], scalar=g_dec[:, 1, n:n + 1],
                                                 in1=ps[:, 1, :], op0=ALU.mult, op1=ALU.add).then_inc(s.g_s, 1)
                    dve.wait_ge(s.g_at_ps, PT + 1)
                    dve.tensor_tensor(g_As[:, :, :], M[0:NS, 0, 0:HEADS * NS].rearrange("p (h t) -> p h t", h=HEADS),
                                      smask[:, :].unsqueeze(1).to_broadcast([NS, HEADS, NS]), ALU.mult).then_inc(s.g_at, 1)
                    dve.wait_ge(s.g_o_ps, PT + 1)
                    dve.wait_ge(s.gst_in, 32)
                    for b in range(DEC_BATCH):
                        n = NCH + b
                        dve.wait_ge(s.g_ds_ps, n + 1)
                        ps = M[:, 2 + n % 2, 0:2 * DV].rearrange("p (q v) -> p q v", q=2)
                        step(dve.scalar_tensor_tensor(out=g_Sin[:, b, 0, :], in0=g_Sin[:, b, 0, :], scalar=g_dec[:, 0, n:n + 1],
                                                      in1=ps[:, 0, :], op0=ALU.mult, op1=ALU.add))
                        dve.scalar_tensor_tensor(out=g_Sin[:, b, 1, :], in0=g_Sin[:, b, 1, :], scalar=g_dec[:, 1, n:n + 1],
                                                 in1=ps[:, 1, :], op0=ALU.mult, op1=ALU.add).then_inc(s.g_s, 1)
                        if b % 2:
                            taken()
                    for q in range(2):
                        step(dve.memset(m_qwz[lo64[1 - q], q:HEADS:2, :], 0.0))
                        step(dve.memset(m_qz[lo64[1 - q], q:HEADS:2, :], 0.0))
                    taken.rest()

                def gla_pe(pe, fill):
                    pe.wait_ge(s.out_taken, 12)
                    to_tokens_pe(pe, TOK["gv"], [gvf[:, m, :] for m in range(4)])
                    pe.wait_ge(s.out_taken, 13)
                    for m in range(2):
                        if m:
                            fill(4)
                            pe.wait_ge(s.gz_min, 2)
                            pe.wait_ge(s.gz_abs, 1)
                        for half in range(2):
                            mm = pe.matmul(M[:, half, 0:HALF], wgk[:, m * P:(m + 1) * P], small[0:RANK, half * HALF:(half + 1) * HALF],
                                           start=True, stop=True)
                        mm.then_inc(s.gz_ps, 1)
                    fill(14)
                    pe.wait_ge(s.g_kd, 1)
                    to_tokens_pe(pe, TOK["kd"], [A[:, 2 + m, :] for m in range(2)])
                    fill(2)
                    pe.wait_ge(s.tok_copied, TOK["kd"] + 5)

                    def scores(i):
                        if i:
                            pe.wait_ge(s.g_at, i)
                        for hd in range(HEADS):
                            mm = pe.matmul(M[:, 0, hd * P:(hd + 1) * P], g_kg[:, hd // 2, i * P:(i + 1) * P],
                                           g_qz[:, hd, i * P:(i + 1) * P], start=True, stop=True)
                        mm.then_inc(s.g_at_ps, 1)

                    scores(0)
                    for n in range(NCH):
                        i, q = n // 2, lo64[n % 2]
                        if n % 2 == 0 and i + 1 < PT:
                            scores(i + 1)
                        fill(1)
                        if n >= 2:
                            pe.wait_ge(s.g_s, n - 1)
                        for hd in range(HEADS):
                            c0 = (hd // 2) * DV
                            mm = pe.matmul(M[lo64[hd % 2], 2 + n % 2, c0:c0 + DV], g_kdT[q, i, hd * DK:(hd + 1) * DK], gv[q, i, hd, :],
                                           start=True, stop=True)
                        mm.then_inc(s.g_ds_ps, 1)
                        if n % 2 == 0:
                            continue
                        fill(2)
                        pe.wait_ge(s.g_at, i + 1)
                        pe.wait_ge(s.g_s, n)
                        if i:
                            pe.wait_ge(s.g_o, i)
                        for hd in range(HEADS):
                            pe.matmul(M[:, 1, hd * P:(hd + 1) * P], gv[:, i, hd, :], g_A[:, i % 2, hd, :], start=True, stop=False,
                                      skip_group_check=True)
                            for m in (n - 1, n):
                                if m:
                                    t0 = m * CH
                                    mm = pe.matmul(M[:, 1, hd * P + t0 % P:hd * P + t0 % P + CH], g_S[:, m - 1, hd // 2, :],
                                                   g_qz[:, hd, t0:t0 + CH], start=False, stop=(m == n), skip_group_check=True)
                        mm.then_inc(s.g_o_ps, 1)
                    pe.wait_ge(s.g_at, PT)
                    for hd in range(HEADS):
                        mm = pe.matmul(M[0:NS, 0, hd * NS:(hd + 1) * NS], g_kg[:, hd // 2, SEQ:T], g_qz[:, hd, SEQ:T],
                                       start=True, stop=True)
                    mm.then_inc(s.g_at_ps, 1)
                    fill(1)
                    pe.wait_ge(s.g_at, PT + 1)
                    pe.wait_ge(s.gst_in, 32)
                    pe.wait_ge(s.g_o, PT)
                    for hd in range(HEADS):
                        pe.matmul(M[:, 1, hd * NS:(hd + 1) * NS], gv[0:NS, PT, hd, :], g_As[:, hd, :], start=(hd == 0), stop=False,
                                  skip_group_check=True)
                    for b in range(DEC_BATCH):
                        for p in range(2):
                            t0 = b * DEC_SEQ
                            dst = M[:, 1, 0:HEADS * NS].rearrange("p (h t) -> p h t", h=HEADS)[:, 2 * p:2 * p + 2, t0:t0 + DEC_SEQ]
                            mm = pe.matmul(dst, g_Sin[:, b, p, :], g_qz[:, 2 * p:2 * p + 2, SEQ + t0:SEQ + t0 + DEC_SEQ],
                                           start=False, stop=(b == DEC_BATCH - 1), skip_group_check=True)
                    mm.then_inc(s.g_o_ps, 1)
                    pe.wait_ge(s.g_kdm_ready, 1)
                    for b in range(DEC_BATCH):
                        n = NCH + b
                        fill(1)
                        pe.wait_ge(s.g_s, n - 1)
                        for hd in range(HEADS):
                            c0 = (hd // 2) * DV
                            mm = pe.matmul(M[lo64[hd % 2], 2 + n % 2, c0:c0 + DV], g_kdm[:, b, hd * DK:(hd + 1) * DK], gv[0:NS, PT, hd, :],
                                           start=True, stop=True)
                        mm.then_inc(s.g_ds_ps, 1)
                    fill.rest()
                    pe.wait_ge(s.out_taken, OUT["ml"] + 12)
                    to_tokens_pe(pe, TOK["mv"], [mvf[:, m, :] for m in range(4)])
                    to_tokens_pe(pe, TOK["mk"], [B[:, 2 + m, :] for m in range(2)])

                def mlstm_act(act, step):
                    act.wait_ge(s.out_taken, OUT["ml"] + 2)
                    for q in range(2):
                        act.activation(m_qz[lo64[q], q:HEADS:2, :], B[lo64[q], 0:2, :], ACT.Copy).then_inc(s.ml_qz, 1)
                    act.wait_ge(s.ml_rows, 1)
                    step(act.activation(r_en[:, :], r_m[:, :], ACT.Abs))
                    step(act.activation(r_en[:, :], r_en[:, :], ACT.Exp, scale=-1.0))
                    act.activation(r_en[:, :], r_en[:, :], ACT.Ln, bias=1.0).then_inc(s.ml_ln, 1)
                    act.wait_ge(s.ml_rows, 4)
                    step(act.activation(r_wi[:, :], r_wi[:, :], ACT.Exp))
                    step(act.activation(r_d[:, :], r_d[:, :], ACT.Exp))
                    act.activation(r_en[:, :], r_m[:, :], ACT.Exp, scale=-1.0).then_inc(s.ml_ex, 1)
                    for i, n in enumerate(TILES):
                        act.wait_ge(s.ml_d_ps, i + 1)
                        act.wait_ge(s.ml_col, 1)
                        if i:
                            act.wait_ge(s.ml_sd, i)
                        for hd in range(HEADS):
                            act.activation(m_D[0:n, hd * n:(hd + 1) * n], M[0:n, 0, hd * n:(hd + 1) * n], ACT.Exp, scale=-1.0,
                                           bias=m_cols[0:n, i, hd:hd + 1]).then_inc(s.ml_d, 1)
                        if i:
                            act.wait_ge(s.ml_t_ps, i)
                            act.activation(oraw[1][:, :, (i - 1) * P:i * P], M[:, 2, :].rearrange("p (h t) -> p h t", h=HEADS),
                                           ACT.Copy).then_inc(s.ml_o, 1)
                    act.activation(B[:, 4:8, :], B[:, 4:8, :], ACT.Sigmoid).then_inc(s.bn_gate, 1)
                    act.wait_ge(s.ml_den_ps, 1)
                    act.activation(m_ad[:, 0:HEADS * NS], M[:, 3, 0:HEADS * NS], ACT.Abs).then_inc(s.ml_ad, 1)

                def mlstm_dve(dve, step):
                    def df_out(n):
                        if n == 0:
                            dve.wait_ge(s.gstore, 32)
                        take(dve, OUT["df"] + n, C[:, n, :] if n < 8 else dvf[:, n - 8, :])

                    taken = Between(df_out, 12)
                    branch_dve(dve, step, 0, A[:, 4:8, :], taken)
                    step(dve.memset(mv[:, :, :, DV:DV + 1], 1.0))
                    step(dve.tensor_scalar(r_a[:, :], small[32:32 + HEADS, :], bif[32:32 + HEADS, 0:1], None, ALU.add))
                    step(dve.tensor_scalar(r_m[:, :], small[64:64 + HEADS, :], bif[64:64 + HEADS, 0:1], None, ALU.add))
                    dve.sem_inc(s.ml_rows, 1)
                    taken()
                    step(dve.tensor_scalar(r_F[:, :], r_m[:, :], 0.0, None, ALU.min))
                    dve.wait_ge(s.ml_ln, 1)
                    step(dve.tensor_tensor(r_m[:, :], r_F[:, :], r_en[:, :], ALU.subtract))
                    dve.wait_ge(s.rreset_in, 16)
                    step(dve.tensor_tensor_scan(r_F[:, :], r_reset[:, :], r_m[:, :], 0.0, ALU.mult, ALU.add))
                    step(dve.tensor_tensor(r_a[:, :], r_a[:, :], r_F[:, :], ALU.subtract))
                    step(dve.memset(r_d[:, :], 0.0))
                    step(dve.tensor_copy(r_d[:, P:SEQ:P], r_F[:, P - 1:SEQ - P:P]))
                    step(dve.tensor_tensor_scan(r_g[:, 0:SEQ], r_d[:, 0:SEQ], r_a[:, 0:SEQ], 0.0, ALU.add, ALU.max))
                    step(dve.memset(r_d[:, SEQ:T:DEC_SEQ], -BIG))
                    step(dve.tensor_copy(r_wi[:, SEQ:T], r_a[:, SEQ:T]))
                    step(dve.tensor_tensor(r_wi[:, SEQ:T:DEC_SEQ], r_wi[:, SEQ:T:DEC_SEQ], m_in[:, :], ALU.max))
                    step(dve.tensor_tensor_scan(r_g[:, SEQ:T], r_d[:, SEQ:T], r_wi[:, SEQ:T], 0.0, ALU.add, ALU.max))
                    step(dve.tensor_tensor(r_m[:, :], r_F[:, :], r_g[:, :], ALU.add))
                    step(dve.memset(m_prev[:, 0:1], 0.0))
                    step(dve.tensor_copy(m_prev[:, 1:PT], r_m[:, P - 1:SEQ - P:P]))
                    step(dve.tensor_copy(m_prev[:, PT:12], m_in[:, :]))
                    dve.sem_inc(s.ml_rows, 1)
                    for lo, hi, n, width, k in ((0, SEQ, PT, P, 0), (SEQ, T, DEC_BATCH, DEC_SEQ, PT)):
                        g3 = r_g[:, lo:hi].rearrange("p (n t) -> p n t", n=n)
                        step(dve.tensor_tensor(r_wi[:, lo:hi].rearrange("p (n t) -> p n t", n=n),
                                               m_prev[:, k:k + n].unsqueeze(2).to_broadcast([HEADS, n, width]), g3, ALU.subtract))
                        step(dve.tensor_tensor(r_d[:, lo:hi].rearrange("p (n t) -> p n t", n=n),
                                               r_a[:, lo:hi].rearrange("p (n t) -> p n t", n=n),
                                               g3[:, :, width - 1:width].to_broadcast([HEADS, n, width]), ALU.subtract))
                    dve.sem_inc(s.ml_rows, 2)
                    taken()
                    dve.wait_ge(s.ml_col_ps, 1)
                    step(dve.tensor_copy(m_cols[:, 0:PT, :], M[:, 0, 0:12 * PT].rearrange("p (i k) -> p i k", i=PT)))
                    dve.tensor_copy(m_cols[0:NS, PT, :], M[0:NS, 0, 12 * PT:12 * PT + 12]).then_inc(s.ml_col, 1)
                    dve.wait_ge(s.ml_col, 1)
                    for p in range(2):
                        ps = M01 if p == 0 else M23
                        dve.wait_ge(s.ml_wi_ps, p + 1)
                        for q in range(2):
                            r, hd = lo64[q], 2 * p + q
                            step(dve.tensor_tensor(halves(m_qwz[r, hd, :]), halves(B[r, p, :]), ps[r], ALU.mult))
                        step(dve.tensor_copy(m_dec[:, p, 0:2], ps[:, 0, P - 1:2 * P:P]))
                        step(dve.tensor_copy(m_dec[:, p, 2:4], ps[:, 1, 3 * P - 1 - HALF:4 * P - HALF:P]))
                        dve.tensor_copy(m_dec[:, p, 4:12], ps[:, 1, SEQ + DEC_SEQ - 1 - HALF:HALF:DEC_SEQ]).then_inc(s.ml_wi, 1)
                        if p == 0:
                            taken()
                    dve.wait_ge(s.ml_wi, 2)
                    dve.wait_ge(s.tok_copied, TOK["mk"] + 5)
                    for i, n in enumerate(TILES):
                        step(dve.scalar_tensor_tensor(out=m_kw[0:n, i, :, :], in0=m_kT[0:n, i, :, :], scalar=DK ** -0.5,
                                                      in1=m_cols[0:n, i, 4:8].unsqueeze(2).to_broadcast([n, HEADS, DK]),
                                                      op0=ALU.mult, op1=ALU.mult))
                    dve.sem_inc(s.ml_kw, 1)
                    taken()
                    dve.wait_ge(s.mst_in, 48)
                    for p in range(2):
                        for hd in (2 * p, 2 * p + 1):
                            step(dve.tensor_tensor(m_qns[:, hd, :].rearrange("p (b t) -> p b t", b=DEC_BATCH),
                                                   m_qwz[:, hd, SEQ:T].rearrange("p (b t) -> p b t", b=DEC_BATCH),
                                                   m_Cin[:, :, p, DV:DV + 1].to_broadcast([P, DEC_BATCH, DEC_SEQ]), ALU.mult))
                    dve.sem_inc(s.ml_qn, 1)
                    for i, n in enumerate(TILES):
                        w = HEADS * n
                        if i in (1, 3):
                            taken()
                        dve.wait_ge(s.ml_s_ps, i + 1)
                        dve.wait_ge(s.ml_d, HEADS * (i + 1))
                        if i:
                            dve.wait_ge(s.ml_n_ps, i)
                        dve.scalar_tensor_tensor(out=m_SD[0:n, 0:w], in0=M[0:n, 1, 0:w], scalar=DK ** -0.5, in1=m_D[0:n, 0:w],
                                                 op0=ALU.mult, op1=ALU.mult).then_inc(s.ml_sd, 1)
                        if n != P:
                            continue
                        dve.wait_ge(s.ml_c_ps, i + 1)
                        ps = M[:, 1, 0:2 * (DV + 1)].rearrange("p (q v) -> p q v", q=2)
                        if i == 0:
                            dve.tensor_copy(m_C[:, 0, :, :], ps).then_inc(s.ml_c, 1)
                        else:
                            for p in range(2):
                                ins = dve.scalar_tensor_tensor(out=m_C[:, i % 2, p, :], in0=m_C[:, (i - 1) % 2, p, :],
                                                               scalar=m_dec[:, p, i:i + 1], in1=ps[:, p, :],
                                                               op0=ALU.mult, op1=ALU.add)
                                if p == 0:
                                    step(ins)
                            ins.then_inc(s.ml_c, 1)
                        dve.wait_ge(s.ml_c, i + 1)
                        dve.wait_ge(s.ml_n_ps, i + 1)
                        if i:
                            dve.wait_ge(s.ml_t_ps, i)
                        num = M[:, 2:4, 0:2 * (DV + 1)].rearrange("p b (h v) -> p b h v", h=2)
                        den, m4 = num[:, :, :, DV], m_den[:, :].rearrange("p (b h) -> p b h", b=2)
                        step(dve.tensor_copy(m4, den))
                        step(dve.scalar_tensor_tensor(out=m_den[:, :], in0=m_den[:, :], scalar=-1.0, in1=m_den[:, :],
                                                      op0=ALU.mult, op1=ALU.max))
                        step(dve.tensor_tensor(m_den[:, :], m_den[:, :], m_cols[:, i, 8:12], ALU.max))
                        step(dve.reciprocal(m_den[:, :], m_den[:, :]))
                        dve.tensor_tensor(m_tok[:, :, :].rearrange("p (b h) v -> p b h v", b=2), num[:, :, :, 0:DV],
                                          m4.unsqueeze(3).to_broadcast([P, 2, 2, DV]), ALU.mult).then_inc(s.ml_tok, 1)
                    dve.tensor_tensor(m_kwm[:, :, :], m_kw[0:NS, PT, :, :].rearrange("p h d -> p (h d)").unsqueeze(1).to_broadcast(
                        [NS, DEC_BATCH, HEADS * DK]), seqm[:, :].unsqueeze(2).to_broadcast([NS, DEC_BATCH, HEADS * DK]),
                        ALU.mult).then_inc(s.ml_kwm_ready, 1)
                    w = HEADS * NS
                    dve.wait_ge(s.ml_ad, 1)
                    dve.wait_ge(s.ml_e_ps, 1)
                    step(dve.tensor_tensor(m_ad[:, 0:w], m_ad[:, 0:w], M[:, 0, 0:w], ALU.max))
                    step(dve.reciprocal(m_ad[:, 0:w], m_ad[:, 0:w]))
                    dve.wait_ge(s.ml_n_ps, PT + 1)
                    dve.tensor_tensor(oraw[1][:, :, SEQ:T], M[:, 2, 0:w].rearrange("p (h t) -> p h t", h=HEADS),
                                      m_ad[:, 0:w].rearrange("p (h t) -> p h t", h=HEADS), ALU.mult).then_inc(s.ml_o, 1)
                    taken(2)
                    for b in range(DEC_BATCH):
                        n = PT + b
                        dve.wait_ge(s.ml_c_ps, n + 1)
                        ps = M[:, b % 2, 0:2 * (DV + 1)].rearrange("p (q v) -> p q v", q=2)
                        for p in range(2):
                            ins = dve.scalar_tensor_tensor(out=m_Cin[:, b, p, :], in0=m_Cin[:, b, p, :], scalar=m_dec[:, p, n:n + 1],
                                                           in1=ps[:, p, :], op0=ALU.mult, op1=ALU.add)
                            if p == 0:
                                step(ins)
                        ins.then_inc(s.ml_c, 1)
                        if b % 4 == 3:
                            taken()
                    taken.rest()

                def mlstm_pe(pe, fill):
                    fill(2)
                    branch_pe(pe, 0, fill)
                    fill(12)
                    pe.wait_ge(s.ml_ex, 1)
                    pe.wait_ge(s.tok_copied, TOK["mk"] + 5)
                    for i, n in enumerate(TILES):
                        for j, row in enumerate((r_a, r_d, r_en)):
                            mm = pe.matmul(M[0:n, 0, 12 * i + 4 * j:12 * i + 4 * j + 4], row[:, i * P:i * P + n], ident[0:HEADS, 0:HEADS],
                                           start=True, stop=True)
                    mm.then_inc(s.ml_col_ps, 1)
                    fill(1)
                    pe.wait_ge(s.ml_col, 1)
                    for p in range(2):
                        for half in range(2):
                            mm = pe.matmul(M[:, 2 * p + half, 0:HALF], selp[:, p, :], r_wi[:, half * HALF:(half + 1) * HALF],
                                           start=True, stop=True)
                        mm.then_inc(s.ml_wi_ps, 1)
                    fill(4)
                    pe.wait_ge(s.ml_wi, 2)
                    def decays_scores(i):
                        n, t0 = TILES[i], i * P
                        mask = big if n == P else sbig
                        for hd in range(HEADS):
                            dst = M[0:n, 0, hd * n:(hd + 1) * n]
                            pe.matmul(dst, ident[0:n, 0:n], mask[:, :], start=True, stop=False)
                            mm = pe.matmul(dst, sel[:, hd, 0:n], r_g[:, t0:t0 + n], start=False, stop=True)
                        mm.then_inc(s.ml_d_ps, 1)
                        if i:
                            fill(1)
                            pe.wait_ge(s.ml_c, i)
                        if i == 0:
                            pe.wait_ge(s.ml_qz, 2)
                        for hd in range(HEADS):
                            mm = pe.matmul(M[0:n, 1, hd * n:(hd + 1) * n], B[:, 2 + hd // 2, t0:t0 + n], m_qz[:, hd, t0:t0 + n],
                                           start=True, stop=True)
                        mm.then_inc(s.ml_s_ps, 1)

                    decays_scores(0)
                    fill(2)
                    for i in range(PT):
                        t0 = i * P
                        pe.wait_ge(s.ml_sd, i + 1)
                        pe.wait_ge(s.ml_kw, 1)
                        for hd in range(HEADS):
                            c0 = (hd // 2) * (DV + 1)
                            mm = pe.matmul(M[lo64[hd % 2], 1, c0:c0 + DV + 1], m_kw[:, i, hd, :], mv[:, i, hd, :],
                                           start=True, stop=True)
                        mm.then_inc(s.ml_c_ps, 1)
                        if i:
                            pe.wait_ge(s.ml_o, i)
                        for hd in range(HEADS):
                            c0 = (hd % 2) * (DV + 1)
                            dst = M[:, 2 + hd // 2, c0:c0 + DV + 1]
                            mm = pe.matmul(dst, m_SD[:, hd * P:(hd + 1) * P], mv[:, i, hd, :], start=True, stop=(i == 0))
                            if i:
                                mm = pe.matmul(dst, m_qwz[:, hd, t0:t0 + P], m_C[:, (i - 1) % 2, hd // 2, :], start=False, stop=True)
                        mm.then_inc(s.ml_n_ps, 1)
                        decays_scores(i + 1)
                        fill(1)
                        pe.wait_ge(s.ml_tok, i + 1)
                        for hd in range(HEADS):
                            mm = pe.transpose(M[:, 2, hd * P:(hd + 1) * P], m_tok[:, hd, :], ident[:, :])
                        mm.then_inc(s.ml_t_ps, 1)
                        fill(1)
                    i = PT
                    pe.wait_ge(s.ml_d, HEADS * (PT + 1))
                    for hd in range(HEADS):
                        mm = pe.matmul(M[:, 0, hd * NS:(hd + 1) * NS], sel[:, hd, :], r_en[:, SEQ:T], start=True, stop=True)
                    mm.then_inc(s.ml_e_ps, 1)
                    fill(1)
                    pe.wait_ge(s.ml_sd, PT + 1)
                    pe.wait_ge(s.ml_o, PT)
                    pe.wait_ge(s.ml_qn, 1)
                    for hd in range(HEADS):
                        pe.matmul(M[:, 2, hd * NS:(hd + 1) * NS], mv[0:NS, i, hd, 0:DV], m_SD[0:NS, hd * NS:(hd + 1) * NS],
                                  start=(hd == 0), stop=False, skip_group_check=True)
                    for b in range(DEC_BATCH):
                        for p in range(2):
                            q0 = b * DEC_SEQ
                            dst = M[:, 2, 0:HEADS * NS].rearrange("p (h t) -> p h t", h=HEADS)[:, 2 * p:2 * p + 2, q0:q0 + DEC_SEQ]
                            mm = pe.matmul(dst, m_Cin[:, b, p, 0:DV], m_qwz[:, 2 * p:2 * p + 2, SEQ + q0:SEQ + q0 + DEC_SEQ],
                                           start=False, stop=(b == DEC_BATCH - 1), skip_group_check=True)
                    mm.then_inc(s.ml_n_ps, 1)
                    for hd in range(HEADS):
                        dst = M[:, 3, hd * NS:(hd + 1) * NS]
                        pe.matmul(dst, ones[0:NS, :], m_SD[0:NS, hd * NS:(hd + 1) * NS], start=True, stop=False)
                        mm = pe.matmul(dst, ones[:, :], m_qns[:, hd, :], start=False, stop=True)
                    mm.then_inc(s.ml_den_ps, 1)
                    fill(2)
                    pe.wait_ge(s.ml_kwm_ready, 1)
                    pe.wait_ge(s.ml_o, 5)
                    for b in range(DEC_BATCH):
                        if b >= 2:
                            pe.wait_ge(s.ml_c, PT + b - 1)
                        for hd in range(HEADS):
                            c0 = (hd // 2) * (DV + 1)
                            mm = pe.matmul(M[lo64[hd % 2], b % 2, c0:c0 + DV + 1], m_kwm[:, b, hd * DK:(hd + 1) * DK],
                                           mv[0:NS, PT, hd, :], start=True, stop=True)
                        mm.then_inc(s.ml_c_ps, 1)
                        fill(1)
                    fill.rest()

                def attention_act(act, step, gates):
                    act.wait_ge(s.lam_sum, 1)
                    act.activation(lam[:, 2:4], lam[:, 0:2], ACT.Exp).then_inc(s.lam_exp, 1)
                    to_tokens_act(act, TOK["dv"], lambda i, n: dv[0:n, i, :, :], HEADS * DV, HEADS)
                    act.wait_ge(s.ml_o, 5)
                    act.wait_ge(s.ml_c, PT + DEC_BATCH)
                    branch_act(act, 1)
                    gates(2)

                    def keys_out(i):
                        n = TILES[i]
                        act.wait_ge(s.tok_ps, TOK["dk"] + i + 1)
                        if i:
                            act.wait_ge(s.kstore, 16 * i)
                        act.activation(d_kout[0:n, :], M[0:n, 3, :], ACT.Copy).then_inc(s.tok_copied, 1)
                        act.wait_ge(s.tok_copied, TOK["dk"] + i + 1)
                        dst = (at(o["k_prompt"])[:, :, i * P:(i + 1) * P].rearrange("o b t h v -> (o b t) (h v)") if n == P
                               else at(o["k_sample"]).rearrange("o b t h v -> (o b t) (h v)"))
                        act.dma_start(dst, d_kout[0:n, :]).then_inc(s.kstore, 16)

                    def exps(n):
                        width = P * (n // HEADS + 1)
                        act.wait_ge(s.nm_ready, n + 1)
                        if n:
                            act.wait_ge(s.w_ready, n)
                        for m in range(2):
                            act.activation(d_e[:, m, 0:width], M[:, m, 0:width], ACT.Exp, bias=d_nm[:, m:m + 1],
                                           accum_out=d_l[:, m:m + 1]).then_inc(s.e_ready, 1)

                    def turned(n):
                        width = P * (n // HEADS + 1)
                        act.wait_ge(s.wt_ps, n + 1)
                        if n:
                            act.wait_ge(s.pv_ps, n)
                        act.activation(d_wT[:, 0:width], M[:, 2, 0:width], ACT.Copy).then_inc(s.wt_copied, 1)

                    for n in range(PT * HEADS + 1):
                        if n < PT * HEADS:
                            exps(n)
                        if n:
                            turned(n - 1)
                        if n in KEYS_AT:
                            keys_out(KEYS_AT.index(n))
                        if n % 4 == 3:
                            gates(2)
                    for g in range(2):
                        for j in range(4 * PAGES):
                            n = 4 * PAGES * g + j
                            act.wait_ge(s.tok_ps, TOK["page"] + n + 1)
                            if j % PAGES == 0 and n:
                                act.wait_ge(s.ss_ps, n // PAGES)
                            if n == 4 * PAGES + 7:
                                gates(2)
                            act.activation(d_KT[:, :, (j % PAGES) * PAGE:(j % PAGES + 1) * PAGE],
                                           M[:, 2 + n % 2, :].rearrange("p (h k) -> p h k", h=HEADS), ACT.Copy).then_inc(s.tok_copied, 1)
                        act.wait_ge(s.ss_nm, g + 1)
                        act.activation(d_es[:, :], M[:, 0, 0:2 * PAGE + NS], ACT.Exp, bias=d_nm[:, 0:1],
                                       accum_out=d_l[:, 0:1]).then_inc(s.ss_e, 1)
                        gates(2)
                    act.wait_ge(s.sp_copied, 2)
                    branch_act(act, 2)

                def attention_dve(dve, step, outputs):
                    for j in range(2):
                        step(dve.tensor_tensor(lamp[:, :], lamv[:, 2 * j, :], lamv[:, 2 * j + 1, :], ALU.mult))
                        step(dve.tensor_reduce(lam[:, j:j + 1], lamp[:, :], AX.X, ALU.add))
                    dve.sem_inc(s.lam_sum, 1)
                    dve.wait_ge(s.lam_exp, 1)
                    step(dve.tensor_tensor(lam[:, 4:5], lam[:, 3:4], lam[:, 2:3], ALU.subtract))
                    step(dve.tensor_tensor(lam[:, 5:6], lam[:, 4:5], lamc[:, 0:1], ALU.subtract))
                    step(dve.tensor_tensor(ghead[:, 2:3], ghead[:, 2:3], lamc[:, 1:2], ALU.mult))
                    step(dve.scalar_tensor_tensor(out=lam[:, 6:7], in0=sign[:, 1:2], scalar=lam[:, 5:6], in1=sign[:, 0:1],
                                                  op0=ALU.mult, op1=ALU.add))
                    dve.wait_ge(s.trig_in, 32)
                    for n in range(8):
                        ps, f = (M01 if n % 2 == 0 else M23), (DK ** -0.5 if n < 4 else 1.0)
                        dve.wait_ge(s.rope_ps, n + 1)
                        step(dve.scalar_tensor_tensor(out=halves(d_t1[:, :]), in0=ps, scalar=f, in1=halves(d_sin[:, :]),
                                                      op0=ALU.mult, op1=ALU.mult))
                        step(dve.scalar_tensor_tensor(out=C[:, n, :], in0=C[:, n, :], scalar=f, in1=d_cos[:, :],
                                                      op0=ALU.mult, op1=ALU.mult))
                        step(dve.tensor_tensor(C[:, n, :], C[:, n, :], d_t1[:, :], ALU.add))
                        dve.sem_inc(s.rope_done, 1)
                        if n in (5, 7):
                            outputs()
                    branch_dve(dve, step, 1, B[:, 4:8, :], lambda: None)
                    step(dve.memset(d_qbd[:, :, :, :, :], 0.0))
                    for m in range(2):
                        for hd in range(HEADS):
                            q0 = hd * 2 * DEC_SEQ + m * DEC_SEQ
                            flat = d_qbd[lo64[m], :, hd, :, :].rearrange("p b x y -> p b (x y)")
                            step(dve.tensor_copy(flat[:, :, q0:q0 + DEC_SEQ],
                                                 C[lo64[m], hd, SEQ:T].rearrange("p (b t) -> p b t", b=DEC_BATCH)))
                    dve.sem_inc(s.qbd_ready, 1)
                    dve.wait_ge(s.mstore, 16 * 6)

                    def maxima(n):
                        width = P * (n // HEADS + 1)
                        dve.wait_ge(s.sc_ps, n + 1)
                        if n:
                            dve.wait_ge(s.e_ready, 2 * n)
                        dve.tensor_reduce(d_nm[:, 0:2], M[:, 0:2, 0:width], AX.X, ALU.max, negate=True).then_inc(s.nm_ready, 1)

                    def weights(n):
                        width = P * (n // HEADS + 1)
                        dve.wait_ge(s.e_ready, 2 * n + 2)
                        if n:
                            dve.wait_ge(s.wt_ps, n)
                        step(dve.reciprocal(d_rc[:, :], d_l[:, :]))
                        step(dve.tensor_tensor(d_rc[:, 1:2], d_rc[:, 1:2], lam[:, 5:6], ALU.mult))
                        step(dve.tensor_scalar(d_w[:, 0:width], d_e[:, 0, 0:width], d_rc[:, 0:1], None, ALU.mult))
                        dve.scalar_tensor_tensor(out=d_w[:, 0:width], in0=d_e[:, 1, 0:width], scalar=d_rc[:, 1:2],
                                                 in1=d_w[:, 0:width], op0=ALU.mult, op1=ALU.add).then_inc(s.w_ready, 1)

                    def values(n):
                        i, hd = n // HEADS, n % HEADS
                        dve.wait_ge(s.pv_ps, n + 1)
                        dve.tensor_copy(oraw[2][:, hd, i * P:(i + 1) * P], M[:, 3, 0:P]).then_inc(s.pv_copied, 1)

                    for n in range(PT * HEADS + 2):
                        if n < PT * HEADS:
                            maxima(n)
                            weights(n)
                        if n >= 2:
                            values(n - 2)
                        if n < PT * HEADS:
                            outputs()
                    for g in range(2):
                        outputs(3 + g)
                        dve.wait_ge(s.ss_ps, 4 * (g + 1))
                        if g == 0:
                            dve.wait_ge(s.e_ready, 2 * PT * HEADS)
                            dve.wait_ge(s.w_ready, PT * HEADS)
                        dve.tensor_reduce(d_nm[:, 0:1], M[:, 0, 0:2 * PAGE + NS], AX.X, ALU.max, negate=True).then_inc(s.ss_nm, 1)
                        dve.wait_ge(s.ss_e, g + 1)
                        step(dve.reciprocal(d_rc[:, 0:1], d_l[:, 0:1]))
                        step(dve.tensor_tensor(d_rc[:, 0:1], d_rc[:, 0:1], lam[:, 6:7], ALU.mult))
                        dve.tensor_scalar(d_es[:, :], d_es[:, :], d_rc[:, 0:1], None, ALU.mult).then_inc(s.ss_w, 1)
                        dve.wait_ge(s.st_ps, g + 1)
                        for pg in range(PAGES):
                            v = M[:, 1, pg * P:(pg + 1) * P].rearrange("p (j h c t) -> p (j h) t c", j=4, h=HEADS, c=2)
                            step(dve.tensor_reduce(d_wTs[:, pg, :, :, :].rearrange("p j h t -> p (j h) t"), v, AX.X, ALU.add))
                        v = M[0:NS, 1, 2 * P:3 * P].rearrange("p (j h c t) -> p (j h) t c", j=4, h=HEADS, c=2)
                        dve.tensor_reduce(d_wTn[:, :, :, :].rearrange("p j h t -> p (j h) t"), v, AX.X, ALU.add).then_inc(s.st_red, 1)
                        outputs(2)
                        dve.wait_ge(s.sp_ps, g + 1)
                        dve.tensor_copy(oraw[2][:, :, SEQ + 16 * g:SEQ + 16 * (g + 1)],
                                        M[:, 0, 2 * PAGE + NS:2 * PAGE + NS + 64].rearrange("p (h t) -> p h t", h=HEADS)
                                        ).then_inc(s.sp_copied, 1)
                    outputs(2 * 16 - outputs.n)
                    branch_dve(dve, step, 2, None, outputs)

                def attention_pe(pe, fill):
                    pe.wait_ge(s.out_taken, OUT["df"] + 12)
                    to_tokens_pe(pe, TOK["dv"], [dvf[:, m, :] for m in range(4)])
                    for n in range(8):
                        if n >= 2:
                            fill(1)
                            pe.wait_ge(s.rope_done, n - 1)
                        if n == 1:
                            pe.wait_ge(s.tok_copied, TOK["dv"] + 5)
                        if n == 4:
                            branch_pe(pe, 1, fill)
                            pe.wait_ge(s.bn_ln, 8)
                        for half in range(2):
                            mm = pe.matmul(M[:, 2 * (n % 2) + half, 0:HALF], rot[:, :], C[:, n, half * HALF:(half + 1) * HALF],
                                           start=True, stop=True)
                        mm.then_inc(s.rope_ps, 1)
                    fill(2)
                    pe.wait_ge(s.rope_done, 8)

                    def scores(n):
                        i, hd = n // HEADS, n % HEADS
                        if n:
                            pe.wait_ge(s.e_ready, 2 * n)
                        for m in range(2):
                            r = lo64[m]
                            pe.matmul(M[:, m, 0:(i + 1) * P], C[r, hd, i * P:(i + 1) * P], C[r, 4 + hd, 0:(i + 1) * P],
                                      start=True, stop=False)
                            mm = pe.matmul(M[:, m, i * P:(i + 1) * P], ident[:, :], neg[:, :], start=False, stop=True)
                        mm.then_inc(s.sc_ps, 1)

                    def turn(n):
                        i = n // HEADS
                        fill(2)
                        pe.wait_ge(s.w_ready, n + 1)
                        if n:
                            pe.wait_ge(s.wt_copied, n)
                        for j in range(i + 1):
                            mm = pe.transpose(M[:, 2, j * P:(j + 1) * P], d_w[:, j * P:(j + 1) * P], ident[:, :])
                        mm.then_inc(s.wt_ps, 1)

                    def keys_turn(i, n):
                        if n > 1:
                            pe.wait_ge(s.pv_copied, n - 1)
                        for m in range(4):
                            mm = pe.transpose(M[0:TILES[i], 3, m * P:(m + 1) * P], C[:, 4 + m, i * P:i * P + TILES[i]], ident[:, :])
                        mm.then_inc(s.tok_ps, 1)

                    def value(n):
                        i, hd = n // HEADS, n % HEADS
                        fill(1)
                        pe.wait_ge(s.wt_copied, n + 1)
                        if n:
                            pe.wait_ge(s.pv_copied, n)
                        if n + 1 in KEYS_AT:
                            pe.wait_ge(s.tok_copied, TOK["dk"] + KEYS_AT.index(n + 1) + 1)
                        for j in range(i + 1):
                            mm = pe.matmul(M[:, 3, 0:P], dv[:, j, hd, :], d_wT[:, j * P:(j + 1) * P],
                                           start=(j == 0), stop=(j == i))
                        mm.then_inc(s.pv_ps, 1)

                    for n in range(PT * HEADS + 1):
                        if n < PT * HEADS:
                            scores(n)
                        if n:
                            turn(n - 1)
                            if n in KEYS_AT:
                                keys_turn(KEYS_AT.index(n), n)
                            value(n - 1)
                    pe.wait_ge(s.qbd_ready, 1)
                    pe.wait_ge(s.e_ready, 2 * PT * HEADS)
                    pe.wait_ge(s.pv_copied, PT * HEADS)
                    for g in range(2):
                        if g:
                            pe.wait_ge(s.sp_copied, g)
                        for j in range(4):
                            b = 4 * g + j
                            for pg in range(PAGES):
                                n = PAGES * b + pg
                                pe.wait_ge(s.page[n % 4], 16 * (n // 4 + 1))
                                pe.wait_ge(s.tok_copied, TOK["page"] + n - 1)
                                for hd in range(HEADS):
                                    mm = pe.transpose(M[:, 2 + n % 2, hd * P:(hd + 1) * P], d_kr[:, n % 4, hd, :], ident[:, :])
                                mm.then_inc(s.tok_ps, 1)
                                fill(1)
                            pe.wait_ge(s.tok_copied, TOK["page"] + PAGES * (b + 1))
                            rows = slice(32 * j, 32 * (j + 1))
                            for hd in range(HEADS):
                                q = d_qbd[:, b, hd, :, :].rearrange("p x y -> p (x y)")
                                pe.matmul(M[rows, 0, 0:2 * PAGE], q, d_KT[:, hd, :], start=(hd == 0), stop=False,
                                          skip_group_check=True)
                                pe.matmul(M[rows, 0, 2 * PAGE:2 * PAGE + NS], q, C[:, 4 + hd, SEQ:T], start=False, stop=False,
                                          skip_group_check=True)
                            mm = pe.matmul(M[rows, 0, 2 * PAGE:2 * PAGE + NS], ident[:, 32 * j:32 * (j + 1)], sneg[:, g, :],
                                           start=False, stop=True, skip_group_check=True)
                            mm.then_inc(s.ss_ps, 1)
                        fill(1)
                        pe.wait_ge(s.ss_w, g + 1)
                        for pg in range(PAGES):
                            pe.transpose(M[:, 1, pg * P:(pg + 1) * P], d_es[:, pg * P:(pg + 1) * P], ident[:, :])
                        pe.transpose(M[0:NS, 1, 2 * P:3 * P], d_es[:, 2 * P:2 * P + NS], ident[:, :]).then_inc(s.st_ps, 1)
                        fill(1)
                        pe.wait_ge(s.st_red, g + 1)
                        base = 2 * PAGE + NS
                        for hd in range(HEADS):
                            pe.matmul(M[:, 0, base + 16 * hd:base + 16 * (hd + 1)], dv[0:NS, PT, hd, :], d_wTn[:, :, hd, :],
                                      start=(hd == 0), stop=False, skip_group_check=True)
                        for j in range(4):
                            for pg in range(PAGES):
                                n = PAGES * (4 * g + j) + pg
                                pe.wait_ge(s.vpage[n % 4], 16 * (n // 4 + 1))
                                if pg:
                                    fill(1)
                                for hd in range(HEADS):
                                    c0 = base + 16 * hd + DEC_SEQ * j
                                    mm = pe.matmul(M[:, 0, c0:c0 + DEC_SEQ], d_V[:, n % 4, hd * DV:(hd + 1) * DV],
                                                   d_wTs[:, pg, j, hd, :], start=False, stop=(j == 3 and pg == 1),
                                                   skip_group_check=True)
                                mm.then_inc(s.v_used, 1)
                        pe.matmul(M[0:1, 1, 500:502], ones[:, 0:1], ones[:, 0:2], start=True, stop=True).then_inc(s.sp_ps, 1)
                    fill(2 * 48 - fill.n)
                    branch_pe(pe, 2, fill)

                def gate_sigmoid(act, b, m):
                    act.wait_ge(s.u_lin, KD * b + m + 1)
                    act.activation(u_g[:, m % 2, :], u_g[:, m % 2, :], ACT.Sigmoid).then_inc(s.u_sig, 1)

                def merge_output(dve, step, b, at):
                    q, kind = at // 4, at % 4
                    n, out, m = CHUNK[f"merge{b}"] + 3 * q, OUT[f"merge{b}"] + at, 2 * q + kind % 2
                    done, u = KD * b + m, u_g[:, m % 2, :]
                    if kind < 2:
                        if at == 0 and b == 0:
                            dve.wait_ge(s.tok_copied, TOK["dv"] + 5)
                        dve.wait_ge(s.chunk_done, n + kind + 1)
                        if done >= 2:
                            dve.wait_ge(s.u_mul, done - 1)
                        dve.tensor_tensor(halves(u), out2(out % 2), halves(rB[:, :]), ALU.mult).then_inc(s.u_lin, 1)
                        dve.wait_ge(s.u_lin, done + 1)
                        dve.sem_inc(s.out_taken, 1)
                        return
                    dve.wait_ge(s.u_sig, done + 1)
                    if kind == 2:
                        dve.wait_ge(s.first_done, done // 2 + 1)
                    else:
                        dve.wait_ge(s.chunk_done, n + 3)
                    if b == 0:
                        step(dve.tensor_tensor(halves(MG[:, m, :]), out2(out % 2), halves(u), ALU.mult))
                        dve.sem_inc(s.out_taken, 1)
                        dve.sem_inc(s.u_mul, 1)
                    else:
                        step(dve.tensor_tensor(halves(u), out2(out % 2), halves(u), ALU.mult))
                        dve.sem_inc(s.out_taken, 1)
                        dve.tensor_tensor(MG[:, m, :], MG[:, m, :], u, ALU.add).then_inc(s.mg_ready, 1)
                        dve.wait_ge(s.mg_ready, KD * (b - 1) + m + 1)
                        dve.sem_inc(s.u_mul, 1)

                def merge_piece(pe, b, at):
                    c, part = at // 4, at % 4
                    q, kind = c // 3, c % 3
                    n, out = CHUNK[f"merge{b}"] + c, OUT[f"merge{b}"] + 4 * q
                    if part == 0:
                        pe.wait_ge(s.wl_split, n + 1)
                    if at == 8:
                        pe.wait_ge(s.bn_l, b + 1)
                    if kind < 2:
                        out += kind
                        blocks = [(2 * part, 2 * part), (2 * part + 1, 2 * part + 1)]
                        begin, end, hi, lo = part == 0, part == 3, xH, xL
                    else:
                        o, part = part // 2, part % 2
                        out += 2 + o
                        blocks = [(2 * k + o, k) for k in (2 * part, 2 * part + 1)]
                        begin, end, hi, lo = part == 0, part == 1, oH[b], oL[b]
                    if begin:
                        pe.wait_ge(s.out_taken, out - 1)
                    mm = blocks_product(pe, n, out % 2, hi, lo, blocks, begin, end)
                    if end:
                        mm.then_inc(s.first_done if kind == 2 and o == 0 else s.chunk_done, 1)

                def merged_act(act):
                    act.wait_ge(s.chunk_done, CHUNK["merge2"])
                    for m in range(KD):
                        act.wait_ge(s.mg_ready, KD + m + 1)
                        act.activation(mH[:, m, :], MG[:, m, :], ACT.Copy).then_inc(s.mh_ready, 1)
                    act.wait_ge(s.ml_split, KD)
                    act.dma_start(h[:, :, :], spill).then_inc(s.h_back, 16)

                def merged_dve(dve):
                    for m in range(KD):
                        dve.wait_ge(s.mh_ready, m + 1)
                        dve.tensor_tensor(mL[:, m, :], MG[:, m, :], mH[:, m, :].bitcast(F32), ALU.subtract).then_inc(s.ml_split, 1)

                def add_to_h(dve, n, name, sem, gain, sq, per=1):
                    if n == 1:
                        dve.wait_ge(s.h_back, 16)
                    for m in range(KD):
                        dve.wait_ge(s.chunk_done, CHUNK[name] + per * (m + 1))
                        dve.tensor_tensor(halves(h[:, m, :]), out2((OUT[name] + m) % 2), halves(h[:, m, :]), ALU.add).then_inc(sem, 1)
                        dve.wait_ge(sem, m + 1)
                        dve.sem_inc(s.out_taken, 1)
                        if m:
                            x_low(dve, n, m - 1, gain)
                        if m > 1:
                            add_square(dve, n, m - 1, sq)
                    x_low(dve, n, KD - 1, gain)
                    add_square(dve, n, KD - 1, sq)

                def embed_pe(pe):
                    pe.wait_ge(s.ptok_in, 32)
                    pe.wait_ge(s.bn_ln, 12)
                    for m in range(KP):
                        for i, n in enumerate(TILES):
                            mm = pe.transpose(M[:, 2 * m + i // PT, (i % PT) * P:(i % PT) * P + n],
                                              p_tok[0:n, i, m * P:(m + 1) * P], ident[0:n, 0:n])
                    mm.then_inc(s.p_ps, 1)

                def embed_act(act):
                    act.wait_ge(s.p_copied, 1)
                    act.wait_ge(s.kstore, 16 * 5)
                    act.activation(pH[:, :, :], p_raw[:, :, :], ACT.Copy).then_inc(s.ph_ready, 1)

                def embed_dve(dve, step):
                    dve.wait_ge(s.p_ps, 1)
                    for m in range(KP):
                        step(dve.tensor_copy(p_raw[:, m, 0:SEQ], M[:, 2 * m, :]))
                        step(dve.tensor_copy(p_raw[:, m, SEQ:T], M[:, 2 * m + 1, 0:NS]))
                    dve.sem_inc(s.p_copied, 1)
                    dve.wait_ge(s.ph_ready, 1)
                    dve.tensor_tensor(pL[:, :, :], p_raw[:, :, :], pH[:, :, :].bitcast(F32), ALU.subtract).then_inc(s.pl_ready, 1)

                def ffn_act(act):
                    base = CHUNK["ffn"]

                    def high(j, i):
                        n = base + j
                        act.wait_ge(s.w_in[n % RAW], w_count(n, i, 4))
                        act.wait_ge(s.chunk_done, n + 4 * i - (SPLIT - 1))
                        act.activation(wH[n % SPLIT][:, :, :], raw[n % RAW][:, :, :], ACT.Copy).then_inc(s.wh_split, 1)

                    def silu(u, at):
                        act.wait_ge(s.f_lin, at + 1)
                        act.activation(f_g[:, u, :], f_g[:, u, :], ACT.Silu).then_inc(s.f_silu, 1)

                    def hidden(u, at):
                        act.wait_ge(s.f_hid, at + 1)
                        blk = hidH[:, at:at + 1, :] if isinstance(at, int) else hidH[:, bass.ds(at, 1), :]
                        act.activation(blk.rearrange("p o n -> p (o n)"), f_u[:, u, :], ACT.Copy).then_inc(s.fh_ready, 1)

                    silu(0, 0)
                    high(3, 0)
                    hidden(0, 0)
                    with act.Fori(1, KF // 2) as i:
                        high(0, i)
                        silu(1, 2 * i - 1)
                        high(1, i)
                        hidden(1, 2 * i - 1)
                        high(2, i)
                        silu(0, 2 * i)
                        high(3, i)
                        hidden(0, 2 * i)
                    high_chunk(act, CHUNK["down"], DOWN_K[0][1])
                    silu(1, KF - 1)
                    high_chunk(act, CHUNK["down"] + 1, DOWN_K[1][1])
                    hidden(1, KF - 1)

                def ffn_dve(dve):
                    base, out = CHUNK["ffn"], OUT["ffn"]

                    def unit(u, at):
                        dve.wait_ge(s.chunk_done, base + 2 * at + 1)
                        dve.tensor_tensor(halves(f_g[:, u, :]), out2(out % 2), halves(rB[:, :]), ALU.mult).then_inc(s.f_lin, 1)
                        dve.wait_ge(s.f_lin, at + 1)
                        dve.sem_inc(s.out_taken, 1)
                        dve.wait_ge(s.chunk_done, base + 2 * at + 2)
                        dve.tensor_tensor(halves(f_u[:, u, :]), out2((out + 1) % 2), halves(rB[:, :]), ALU.mult
                                          ).then_inc(s.out_taken, 1)
                        dve.wait_ge(s.out_taken, out + 2 * at + 2)
                        dve.wait_ge(s.f_silu, at + 1)
                        dve.tensor_tensor(f_u[:, u, :], f_u[:, u, :], f_g[:, u, :], ALU.mult).then_inc(s.f_hid, 1)

                    def low(u, at):
                        dve.wait_ge(s.fh_ready, at + 1)
                        one = isinstance(at, int)
                        lo, hi = (x[:, at:at + 1, :] if one else x[:, bass.ds(at, 1), :] for x in (hidL, hidH))
                        dve.tensor_tensor(lo.rearrange("p o n -> p (o n)"), f_u[:, u, :],
                                          hi.rearrange("p o n -> p (o n)").bitcast(F32), ALU.subtract).then_inc(s.fl_ready, 1)
                        dve.wait_ge(s.fl_ready, at + 1)

                    unit(0, 0)
                    unit(1, 1)
                    low(0, 0)
                    with dve.Fori(1, KF // 2) as i:
                        unit(0, 2 * i)
                        low(1, 2 * i - 1)
                        unit(1, 2 * i + 1)
                        low(0, 2 * i)
                    low(1, KF - 1)

                def ple_act(act):
                    base = CHUNK["ple"]
                    for at in range(2, 2 + KD + 2):
                        if 4 <= at < 2 + KD:
                            high_chunk(act, base + at)
                        m = at - 4
                        if m >= 0:
                            act.wait_ge(s.e_lin, m + 1)
                            act.activation(e_g[:, m % 2, :], e_g[:, m % 2, :], ACT.Sigmoid).then_inc(s.e_sig, 1)

                def proj_dve(dve):
                    for m in range(KD):
                        dve.wait_ge(s.proj_done, m + 1)
                        dve.tensor_copy(halves(e_p[:, m, :]), out2((OUT["ple"] + m) % 2)).then_inc(s.proj_taken, 1)
                        dve.wait_ge(s.proj_taken, m + 1)
                        dve.sem_inc(s.out_taken, 1)

                def ple_dve(dve, step):
                    out = OUT["ple"]
                    for m in range(KD + 1):
                        if m < KD:
                            dve.wait_ge(s.chunk_done, CHUNK["ple"] + 2 + m + 1)
                            if m >= 2:
                                dve.wait_ge(s.e_mul, m - 1)
                            dve.tensor_tensor(halves(e_g[:, m % 2, :]), out2((out + m) % 2), halves(rB[:, :]), ALU.mult).then_inc(s.e_lin, 1)
                            dve.wait_ge(s.e_lin, m + 1)
                            dve.sem_inc(s.out_taken, 1)
                        if m:
                            u = m - 1
                            dve.wait_ge(s.e_sig, u + 1)
                            dve.tensor_tensor(e_p[:, u, :], e_p[:, u, :], e_g[:, u % 2, :], ALU.mult).then_inc(s.e_mul, 1)
                            dve.wait_ge(s.e_mul, u + 1)
                            dve.tensor_tensor(h[:, u, :], h[:, u, :], e_p[:, u, :], ALU.add).then_inc(s.h_ple, 1)

                def proj_pe(pe):
                    for q in range(2):
                        n = CHUNK["ple"] + q
                        pe.wait_ge(s.wl_split, n + 1)
                        for o_at in range(4):
                            out = OUT["ple"] + 4 * q + o_at
                            pe.wait_ge(s.out_taken, out - 1)
                            mm = blocks_product(pe, n, out % 2, pH, pL, [(4 * k + o_at, k) for k in range(KP)], True, True)
                            mm.then_inc(s.proj_done, 1)
                        pe.wait_ge(s.proj_done, 4 * (q + 1))
                        pe.sem_inc(s.chunk_done, 1)

                def down_pe(pe):
                    def output(m, i, per):
                        for j, (k0, kb) in enumerate(DOWN_K):
                            n = CHUNK["down"] + 4 * m + j
                            pe.wait_ge(s.wl_split, n + 1 + 4 * per * i)
                            if per == 0 and m == 0:
                                pe.wait_ge(s.fl_ready, k0 + kb)
                            if j == 0:
                                pe.wait_ge(s.out_taken, OUT["down"] + m - 1 + per * i)
                            mm = blocks_product(pe, n, (OUT["down"] + m) % 2, hidH, hidL, [(k, k0 + k) for k in range(kb)],
                                                j == 0, j == 3)
                            mm.then_inc(s.chunk_done, 1)

                    output(0, 0, 0)
                    output(1, 0, 0)
                    with pe.Fori(1, KD // 2) as i:
                        output(0, i, 2)
                        output(1, i, 2)

                @block.scalar
                def _(act):
                    step = Steps(act, s.act_step)
                    act.wait_ge(s.gain_in, 16 * 3)
                    high_chunk(act, 0)
                    high_chunk(act, 1)
                    for k in range(KD):
                        x_high(act, 0, k, sq0, gains[:, 0, :])
                    norm_factor(act, step, 0)
                    high_loop(act, "gla", 12)
                    high_chunk(act, CHUNK["small"])
                    act.wait_ge(s.par_in, 16 * 10)
                    gla_act(act, step)
                    mlstm_act(act, step)
                    gates = Between(lambda n: gate_sigmoid(act, n // KD, n % KD), 3 * KD)
                    attention_act(act, step, gates)
                    gates(2)
                    embed_act(act)
                    gates.rest()
                    act.wait_ge(s.wl_split, CHUNK["out"])
                    for j in range(SPLIT):
                        high_chunk(act, CHUNK["out"] + j)
                    merged_act(act)
                    for m in range(KD):
                        if m < KD - SPLIT:
                            high_chunk(act, CHUNK["out"] + SPLIT + m)
                        else:
                            high_chunk(act, CHUNK["ffn"] + m - (KD - SPLIT))
                        x_high(act, 1, m, sq0, gains[:, 1, :], s.h_mix)
                    high_chunk(act, CHUNK["ffn"] + 2)
                    norm_factor(act, step, 1)
                    ffn_act(act)
                    for n in range(SPLIT, 4 * KD + SPLIT):
                        if n < 4 * KD:
                            high_chunk(act, CHUNK["down"] + n, DOWN_K[n % 4][1])
                        else:
                            high_chunk(act, CHUNK["ple"] + n - 4 * KD)
                        if n % 4 == 1 and n > SPLIT:
                            x_high(act, 2, n // 4 - 1, sq2, gains[:, 2, :], s.h_ffn)
                    for n in range(2, 4):
                        high_chunk(act, CHUNK["ple"] + n)
                    norm_factor(act, step, 2)
                    ple_act(act)

                @block.tensor
                def _(pe):
                    panel_chunk(pe, 0, 0, xH, xL, before=x_there(pe, 0))
                    stats(pe, 0, sq0)
                    panel_chunk(pe, 1, 1, xH, xL)
                    panel_loop(pe, "gla", 12, xH, xL, 2)
                    pe.wait_ge(s.par_in, 16 * 10)
                    panel_chunk(pe, CHUNK["small"], OUT["small"], xH, xL)
                    gla_pe(pe, Between(lambda n: panel_piece(pe, "ml", n), 48))
                    mlstm_pe(pe, Between(lambda n: panel_piece(pe, "df", n), 48))
                    fill = Between(lambda n: merge_piece(pe, n // 48, n % 48), 3 * 48)
                    attention_pe(pe, fill)
                    fill(4)
                    embed_pe(pe)
                    fill.rest()
                    panel_chunk(pe, CHUNK["out"], OUT["out"], mH, mL, before=lambda k: pe.wait_ge(s.ml_split, k + 1))
                    for m in range(1, KD):
                        panel_chunk(pe, CHUNK["out"] + m, OUT["out"] + m, mH, mL)
                    panel_chunk(pe, CHUNK["ffn"], OUT["ffn"], xH, xL, before=x_there(pe, 1))
                    stats(pe, 1, sq0)
                    panel_chunk(pe, CHUNK["ffn"] + 1, OUT["ffn"] + 1, xH, xL)
                    panel_loop(pe, "ffn", 2 * KF, xH, xL, 2)
                    down_pe(pe)
                    pe.wait_ge(s.pl_ready, 1)
                    proj_pe(pe)
                    stats(pe, 2, sq2)
                    for m in range(KD):
                        panel_chunk(pe, CHUNK["ple"] + 2 + m, OUT["ple"] + KD + m, xH, xL, before=x_there(pe, 2) if m == 0 else None)

                @block.vector
                def _(dve):
                    step = Steps(dve, s.dve_step)
                    dve.wait_ge(s.gain_in, 16 * 3)
                    for k in range(KD):
                        x_low(dve, 0, k, gains[:, 0, :])
                    dve.wait_ge(s.par_in, 16 * 10)
                    dve.wait_ge(s.r_ready, 1)
                    gla_dve(dve, step)
                    mlstm_dve(dve, step)
                    outputs = Between(lambda n: merge_output(dve, step, n // 16, n % 16), 48)
                    attention_dve(dve, step, outputs)
                    embed_dve(dve, step)
                    outputs.rest()
                    merged_dve(dve)
                    add_to_h(dve, 1, "out", s.h_mix, gains[:, 1, :], sq0)
                    dve.wait_ge(s.r_ready, 2)
                    ffn_dve(dve)
                    add_to_h(dve, 2, "down", s.h_ffn, gains[:, 2, :], sq2, 4)
                    proj_dve(dve)
                    dve.wait_ge(s.r_ready, 3)
                    ple_dve(dve, step)

            clear_all()

        with nc.Block() as block:

            @block.scalar
            def _(act):
                step = Steps(act, s.act_step)
                for k in range(KD):
                    if k >= 3:
                        act.wait_ge(s.sq_used, k - 2)
                    act.activation(sq0[:, k % 2 if k else 2, :], h[:, k, :], ACT.Square).then_inc(s.sq_ready, 1)
                norm_factor(act, step, 0)

            @block.vector
            def _(dve):
                for k in range(1, KD):
                    add_square(dve, 0, k, sq0)
                dve.wait_ge(s.r_ready, 1)
                for k in range(KD):
                    dve.scalar_tensor_tensor(out=y_f[:, k, :], in0=h[:, k, :], scalar=gfin[:, k:k + 1], in1=rB[:, :],
                                             op0=ALU.mult, op1=ALU.mult).then_inc(s.y_ready, 1)
                for i, n in enumerate(TILES):
                    for half in range(2):
                        dve.wait_ge(s.y_ps, 2 * i + half + 1)
                        dve.tensor_copy(io_tok[0:n, i, half * 512:(half + 1) * 512], M[0:n, 2 * (i % 2) + half, :]).then_inc(s.io_copied, 1)

            @block.tensor
            def _(pe):
                stats(pe, 0, sq0)
                pe.wait_ge(s.y_ready, KD)
                for i, n in enumerate(TILES):
                    for half in range(2):
                        if i >= 2:
                            pe.wait_ge(s.io_copied, 2 * (i - 2) + half + 1)
                        for k in range(4):
                            mm = pe.transpose(M[0:n, 2 * (i % 2) + half, k * P:(k + 1) * P], y_f[:, 4 * half + k, i * P:i * P + n],
                                              ident[:, :])
                        mm.then_inc(s.y_ps, 1)

            @block.sync
            def _(sp):
                for i, n in enumerate(TILES):
                    sp.wait_ge(s.io_copied, 2 * (i + 1))
                    dst = o["y_prompt"][0, i * P:(i + 1) * P, :] if n == P else o["y_sample"].rearrange("b t d -> (b t) d")
                    sp.dma_start(dst, io_tok[0:n, i, :]).then_inc(s.io_out, 16)
                sp.wait_ge(s.io_out, 16 * 5)


_INS = ["x_prompt", "x_sample", "cache_k", "cache_v", "state_gla", "state_mlstm_c", "state_mlstm_n", "state_mlstm_m",
        "page_table", "p_prompt", "p_sample", "g_mix", "w_in", "w_gla_gk", "b_gla_gk", "g_gla_norm", "b_mlstm_if",
        "g_mlstm_norm", "diff_lambda", "g_diff_norm", "w_branch", "w_gate", "w_out", "g_ffn", "w_ffn_gate", "w_ffn_up",
        "w_ffn_down", "g_ple", "w_ple_gate", "w_ple_proj", "g_final"]
_OUTS = [("y_prompt", (1, SEQ, D)), ("y_sample", (DEC_BATCH, DEC_SEQ, D)),
         ("k_prompt", (DEPTH, 1, SEQ, 2 * HEADS, DK)), ("v_prompt", (DEPTH, 1, SEQ, HEADS, DV)),
         ("gla_prompt", (DEPTH, 1, HEADS, DK, DV)), ("c_prompt", (DEPTH, 1, HEADS, DK, DV)),
         ("n_prompt", (DEPTH, 1, HEADS, DK)), ("m_prompt", (DEPTH, 1, HEADS)),
         ("k_sample", (DEPTH, DEC_BATCH, DEC_SEQ, 2 * HEADS, DK)), ("v_sample", (DEPTH, DEC_BATCH, DEC_SEQ, HEADS, DV)),
         ("gla_sample", (DEPTH, DEC_BATCH, HEADS, DK, DV)), ("c_sample", (DEPTH, DEC_BATCH, HEADS, DK, DV)),
         ("n_sample", (DEPTH, DEC_BATCH, HEADS, DK)), ("m_sample", (DEPTH, DEC_BATCH, HEADS))]


def constants():
    import math
    import numpy as np
    f = np.float32
    i = np.arange(P)
    k = {"ident": np.eye(P), "ones": np.ones((P, P)), "epsc": np.full((P, 1), EPS)}
    k["big"] = np.where(i[:, None] > i[None, :], BIG, 0.0)
    k["neg"] = np.where(i[None, :] > i[:, None], -BIG, 0.0)
    k["gmask"] = (i[:, None] // CH == i[None, :] // CH) & (i[:, None] <= i[None, :])
    n = np.arange(NS)
    seen = (n[:, None] // DEC_SEQ == n[None, :] // DEC_SEQ) & (n[:, None] <= n[None, :])
    k["smask"] = seen
    k["sbig"] = np.where(seen, 0.0, BIG)
    row_seq, row_t = i // NS, i % DEC_SEQ
    k["sneg"] = np.stack([np.where(seen[:, (4 * g + row_seq) * DEC_SEQ + row_t].T, 0.0, -BIG) for g in range(2)], 1)
    k["sel"] = np.repeat(np.eye(HEADS)[:, :, None], P, 2)
    k["selp"] = np.stack([(np.arange(HEADS)[:, None] == 2 * p + i[None, :] // DK) for p in range(2)], 1)
    k["seqm"] = (n[:, None] // DEC_SEQ == np.arange(DEC_BATCH)[None, :])
    k["sign"] = np.stack([(i // DEC_SEQ) % 2 == 0, (i // DEC_SEQ) % 2 == 1], 1)
    half = DK // 8
    rot = np.zeros((P, P))
    for h0 in (0, DK):
        for j in range(half):
            rot[h0 + half + j, h0 + j] = -1.0
            rot[h0 + j, h0 + half + j] = 1.0
    k["rot"] = rot
    pos = np.concatenate([np.arange(SEQ), PAGE * PAGES + n % DEC_SEQ]).astype(f)
    inv = f(500000.0) ** (-np.arange(half, dtype=f) * f(2.0) / f(2 * half))
    ang = (pos[:, None] * inv[None, :]).astype(f)
    cos, sin = np.ones((P, T), f), np.zeros((P, T), f)
    for h0 in (0, DK):
        for q in range(2):
            cos[h0 + half * q:h0 + half * (q + 1)] = np.cos(ang).T
            sin[h0 + half * q:h0 + half * (q + 1)] = np.sin(ang).T
    k["cos"], k["sin"] = cos, sin
    t = np.arange(SEQ)
    k["greset"] = np.repeat(np.concatenate([t % CH != 0, n % DEC_SEQ != 0])[None], P, 0)
    k["rreset"] = np.repeat(np.concatenate([t % P != 0, n % DEC_SEQ != 0])[None], HEADS, 0)
    init = [0.8 - 0.6 * math.exp(-0.3 * layer) for layer in range(DEPTH)]
    k["lamc"] = np.repeat(np.array([[x, 1.0 - x] for x in init])[:, None, :], P, 1)
    return {name: np.ascontiguousarray(v, dtype=f) for name, v in k.items()}


def kernel(**inputs):
    import numpy as _np
    import concourse.bacc as _bacc
    from concourse import mybir as _mybir
    from concourse.bass_utils import run_bass_kernel_spmd as _run

    nc = _bacc.Bacc("TRN2", target_bir_lowering=False, num_devices=1)
    arrays, args, consts, outs = {}, {}, {}, {}
    for name in _INS:
        x = _np.ascontiguousarray(inputs[name])
        arrays[f"in_{name}"] = x
        args[name] = nc.dram_tensor(f"in_{name}", x.shape, _mybir.dt.from_np(x.dtype), kind="ExternalInput").ap()
    for name, x in constants().items():
        arrays[f"const_{name}"] = x
        consts[name] = nc.dram_tensor(f"const_{name}", x.shape, _mybir.dt.from_np(x.dtype), kind="ExternalInput").ap()
    for name, shape in _OUTS:
        outs[name] = nc.dram_tensor(f"out_{name}", shape, F32, kind="ExternalOutput").ap()
    outs["spill"] = nc.dram_tensor("spill", (P, KD, T), F32).ap()
    program(nc, args, consts, outs)
    r = _run(nc, [arrays], core_ids=[0])
    return tuple(r.results[0][f"out_{name}"] for name, _ in _OUTS)
```
